# Optimizing a Trainium2 kernel written in Bass

```python
import math
import jax, jax.numpy as jnp
from jax import lax
import numpy as np

D_MODEL = 1024
BATCH = 1
SEQ = 512
DEPTH = 2

GLA_HEADS = 4
GLA_DK = 64
GLA_DV = 128
GLA_LOWRANK = 16
GLA_TAU = 16.0
GLA_CHUNK = 64
DIFF_HEADS = 4
DIFF_DQK = 64
DIFF_DV = 128
Q_BLOCK = 128
NUM_BUCKETS = 32
MAX_DISTANCE = 128
S5_GROUPS = 32
S5_GROUP_CH = 16
S5_STATE = 64
S5_WIDTH = S5_GROUPS * S5_GROUP_CH
S5_DT_MIN = 1e-3
S5_DT_MAX = 1e-1
D_FF = 2816
N_BRANCH = 3
ADA_CHUNKS = 9
EPS = 1e-6

GLA_QK_W = GLA_HEADS * GLA_DK
GLA_V_W = GLA_HEADS * GLA_DV
DIFF_QK_W = DIFF_HEADS * 2 * DIFF_DQK
DIFF_V_W = DIFF_HEADS * DIFF_DV
BRANCH_W = 512
SPLIT_WIDTHS = (GLA_QK_W, GLA_QK_W, GLA_V_W, GLA_V_W, GLA_LOWRANK,
                DIFF_QK_W, DIFF_QK_W, DIFF_V_W, S5_WIDTH, N_BRANCH * D_MODEL)
IN_W = 256 + 256 + 512 + 512 + 16 + 512 + 512 + 512 + 512 + 3 * 1024

kernel_name = 'hybrid_gla_diffattn_s5_macaron_block'

def rmsnorm(x, g):
    xf = x.astype(jnp.float32)
    y = xf * lax.rsqrt(jnp.mean(xf * xf, axis=-1, keepdims=True) + EPS)
    return (y * g.astype(jnp.float32)).astype(x.dtype)

def modulate(x, g, shift, scale):
    return rmsnorm(x, g) * (1.0 + scale[:, None, :]) + shift[:, None, :]

def swiglu(u, w_up, w_down):
    gu = u @ w_up
    gate, up = gu[..., :D_FF], gu[..., D_FF:]
    return (jax.nn.silu(gate) * up) @ w_down

def gla_mixer(q, k, v, r, a_low, w_alpha, b_alpha, norm_g):
    bsz, L, _ = q.shape
    n_chunks = L // GLA_CHUNK
    f32 = jnp.float32

    def heads(t, d):
        return t.astype(f32).reshape(bsz, n_chunks, GLA_CHUNK, GLA_HEADS, d).transpose(0, 3, 1, 2, 4)

    log_a = jax.nn.log_sigmoid((a_low @ w_alpha + b_alpha).astype(f32)) / GLA_TAU
    qh = heads(q, GLA_DK) * (GLA_DK ** -0.5)
    kh = heads(k, GLA_DK)
    vh = heads(v, GLA_DV)
    b = jnp.cumsum(heads(log_a, GLA_DK), axis=3)
    b_last = b[:, :, :, -1:, :]
    q_dec = qh * jnp.exp(b)
    k_dec = kh * jnp.exp(-b)
    causal = jnp.tril(jnp.ones((GLA_CHUNK, GLA_CHUNK), dtype=bool))
    att = jnp.where(causal, jnp.einsum('bhncd,bhnsd->bhncs', q_dec, k_dec), 0.0)
    o_intra = jnp.einsum('bhncs,bhnse->bhnce', att, vh)
    d_state = jnp.einsum('bhncd,bhnce->bhnde', kh * jnp.exp(b_last - b), vh)
    chunk_decay = jnp.exp(b_last[:, :, :, 0, :])

    def step(S, inp):
        dec, ds = inp
        return dec[..., None] * S + ds, S

    s0 = jnp.zeros((bsz, GLA_HEADS, GLA_DK, GLA_DV), f32)
    _, s_prev = lax.scan(step, s0, (jnp.moveaxis(chunk_decay, 2, 0), jnp.moveaxis(d_state, 2, 0)))
    s_prev = jnp.moveaxis(s_prev, 0, 2)
    o = o_intra + jnp.einsum('bhncd,bhnde->bhnce', q_dec, s_prev)
    o = o * lax.rsqrt(jnp.mean(o * o, axis=-1, keepdims=True) + EPS)
    o = o.transpose(0, 2, 3, 1, 4).reshape(bsz, L, GLA_V_W) * norm_g.astype(f32)
    return (o * jax.nn.silu(r.astype(f32))).astype(q.dtype)

def t5_bucket(dist):
    max_exact = NUM_BUCKETS // 2
    d = jnp.maximum(dist, 1).astype(jnp.float32)
    large = max_exact + (jnp.log(d / max_exact) / math.log(MAX_DISTANCE / max_exact)
                         * (NUM_BUCKETS - max_exact)).astype(jnp.int32)
    large = jnp.minimum(large, NUM_BUCKETS - 1)
    return jnp.where(dist < max_exact, dist, large)

def diff_attention(q, k, v, lam_vecs, lam_init, norm_g, rel_bias):
    bsz, L, _ = q.shape
    f32 = jnp.float32
    n_maps = 2 * DIFF_HEADS
    qm = q.astype(f32).reshape(bsz, L, n_maps, DIFF_DQK).transpose(0, 2, 1, 3) * (DIFF_DQK ** -0.5)
    km = k.astype(f32).reshape(bsz, L, n_maps, DIFF_DQK).transpose(0, 2, 1, 3)
    vh = v.reshape(bsz, L, DIFF_HEADS, DIFF_DV).transpose(0, 2, 1, 3)
    lv = lam_vecs.astype(f32)
    lam = jnp.exp(jnp.sum(lv[0] * lv[1])) - jnp.exp(jnp.sum(lv[2] * lv[3])) + lam_init
    outs = []
    for blk in range(L // Q_BLOCK):
        s, e = blk * Q_BLOCK, (blk + 1) * Q_BLOCK
        logits = jnp.einsum('bmqd,bmkd->bmqk', qm[:, :, s:e], km[:, :, :e])
        dist = jnp.arange(s, e)[:, None] - jnp.arange(e)[None, :]
        bias = rel_bias.astype(f32)[t5_bucket(jnp.maximum(dist, 0))].transpose(2, 0, 1)
        logits = jnp.where(dist >= 0, logits + bias, -jnp.inf)
        p = jax.nn.softmax(logits, axis=-1).reshape(bsz, DIFF_HEADS, 2, Q_BLOCK, e)
        a = p[:, :, 0] - lam * p[:, :, 1]
        outs.append(jnp.einsum('bhqk,bhkd->bhqd', a, vh[:, :, :e].astype(f32)))
    o = jnp.concatenate(outs, axis=2)
    o = o * lax.rsqrt(jnp.mean(o * o, axis=-1, keepdims=True) + EPS)
    o = o.transpose(0, 2, 1, 3).reshape(bsz, L, DIFF_V_W) * norm_g.astype(f32) * (1.0 - lam_init)
    return o.astype(q.dtype)

def s5_mixer(u, lam_re, lam_im, log_step, b_re, b_im, c_re, c_im, d_skip, w_glu, b_glu):
    bsz, L, _ = u.shape
    f32 = jnp.float32
    uf = u.astype(f32).reshape(bsz, L, S5_GROUPS, S5_GROUP_CH)
    lr, li = lam_re.astype(f32), lam_im.astype(f32)
    dt = jnp.exp(log_step.astype(f32))[:, None]
    mag = jnp.exp(lr * dt)
    abar_re, abar_im = mag * jnp.cos(li * dt), mag * jnp.sin(li * dt)
    nr, ni = abar_re - 1.0, abar_im
    den = lr * lr + li * li
    f_re = (nr * lr + ni * li) / den
    f_im = (ni * lr - nr * li) / den
    br, bi = b_re.astype(f32), b_im.astype(f32)
    bbar_re = f_re[..., None] * br - f_im[..., None] * bi
    bbar_im = f_re[..., None] * bi + f_im[..., None] * br
    bu_re = jnp.einsum('blgh,gph->blgp', uf, bbar_re)
    bu_im = jnp.einsum('blgh,gph->blgp', uf, bbar_im)
    a_re = jnp.broadcast_to(abar_re, bu_re.shape)
    a_im = jnp.broadcast_to(abar_im, bu_im.shape)

    def combine(e1, e2):
        a1r, a1i, b1r, b1i = e1
        a2r, a2i, b2r, b2i = e2
        return (a2r * a1r - a2i * a1i,
                a2r * a1i + a2i * a1r,
                a2r * b1r - a2i * b1i + b2r,
                a2r * b1i + a2i * b1r + b2i)

    _, _, xr, xi = lax.associative_scan(combine, (a_re, a_im, bu_re, bu_im), axis=1)
    y = (jnp.einsum('gnp,blgp->blgn', c_re.astype(f32), xr)
         - jnp.einsum('gnp,blgp->blgn', c_im.astype(f32), xi))
    y = y + d_skip.astype(f32) * uf
    y = jax.nn.gelu(y.reshape(bsz, L, S5_WIDTH))
    z = y @ w_glu.astype(f32) + b_glu.astype(f32)
    return (z[..., :S5_WIDTH] * jax.nn.sigmoid(z[..., S5_WIDTH:])).astype(u.dtype)

def hybrid_mixer(u, layer_idx, w_in, gla_w_alpha, gla_b_alpha, gla_norm, diff_lambda, diff_norm,
                 s5_lam_re, s5_lam_im, s5_log_step, s5_b_re, s5_b_im, s5_c_re, s5_c_im, s5_d,
                 s5_w_glu, s5_b_glu, w_branch, w_out, rel_bias):
    bsz, L, _ = u.shape
    proj = u @ w_in
    offsets = [int(o) for o in np.cumsum(SPLIT_WIDTHS)[:-1]]
    (g_q, g_k, g_v, g_r, g_a, d_q, d_k, d_v, s_u, gate_logits) = jnp.split(proj, offsets, axis=-1)
    y_gla = gla_mixer(g_q, g_k, g_v, g_r, g_a, gla_w_alpha, gla_b_alpha, gla_norm)
    lam_init = 0.8 - 0.6 * math.exp(-0.3 * layer_idx)
    y_diff = diff_attention(d_q, d_k, d_v, diff_lambda, lam_init, diff_norm, rel_bias)
    y_s5 = s5_mixer(s_u, s5_lam_re, s5_lam_im, s5_log_step, s5_b_re, s5_b_im, s5_c_re, s5_c_im,
                    s5_d, s5_w_glu, s5_b_glu)
    gates = jax.nn.sigmoid(gate_logits.astype(jnp.float32)).reshape(bsz, L, N_BRANCH, D_MODEL).astype(u.dtype)
    merged = (gates[:, :, 0] * (y_gla @ w_branch[0])
              + gates[:, :, 1] * (y_diff @ w_branch[1])
              + gates[:, :, 2] * (y_s5 @ w_branch[2]))
    return merged @ w_out

def setup_inputs(seed: int = 0) -> dict:
    key = jax.random.key(seed)
    ks = jax.random.split(key, 32)
    f32 = jnp.float32
    nrm = lambda k, shape, s: jax.random.normal(k, shape, f32) * s
    n_idx = jnp.arange(S5_STATE, dtype=f32)
    return {
        'x': nrm(ks[0], (BATCH, SEQ, D_MODEL), 1.0),
        'c': nrm(ks[1], (BATCH, D_MODEL), 1.0),
        'rel_bias': nrm(ks[2], (NUM_BUCKETS, 2 * DIFF_HEADS), 0.5),
        'w_ada': nrm(ks[3], (DEPTH, D_MODEL, ADA_CHUNKS * D_MODEL), D_MODEL ** -0.5),
        'b_ada': nrm(ks[4], (DEPTH, ADA_CHUNKS * D_MODEL), 0.02),
        'norm_pre': 1.0 + nrm(ks[5], (DEPTH, 3, D_MODEL), 0.05),
        'norm_post': 1.0 + nrm(ks[6], (DEPTH, 3, D_MODEL), 0.05),
        'ffn1_w_up': nrm(ks[7], (DEPTH, D_MODEL, 2 * D_FF), D_MODEL ** -0.5),
        'ffn1_w_down': nrm(ks[8], (DEPTH, D_FF, D_MODEL), D_FF ** -0.5),
        'ffn2_w_up': nrm(ks[9], (DEPTH, D_MODEL, 2 * D_FF), D_MODEL ** -0.5),
        'ffn2_w_down': nrm(ks[10], (DEPTH, D_FF, D_MODEL), D_FF ** -0.5),
        'w_in': nrm(ks[11], (DEPTH, D_MODEL, IN_W), D_MODEL ** -0.5),
        'gla_w_alpha': nrm(ks[12], (DEPTH, GLA_LOWRANK, GLA_QK_W), GLA_LOWRANK ** -0.5),
        'gla_b_alpha': nrm(ks[13], (DEPTH, GLA_QK_W), 0.1),
        'gla_norm': 1.0 + nrm(ks[14], (DEPTH, GLA_V_W), 0.05),
        'diff_lambda': nrm(ks[15], (DEPTH, 4, DIFF_DQK), 0.1),
        'diff_norm': 1.0 + nrm(ks[16], (DEPTH, DIFF_V_W), 0.05),
        's5_lam_re': -0.5 + nrm(ks[17], (DEPTH, S5_GROUPS, S5_STATE), 0.01),
        's5_lam_im': math.pi * n_idx + nrm(ks[18], (DEPTH, S5_GROUPS, S5_STATE), 0.01),
        's5_log_step': jax.random.uniform(ks[19], (DEPTH, S5_GROUPS), f32,
                                          math.log(S5_DT_MIN), math.log(S5_DT_MAX)),
        's5_b_re': nrm(ks[20], (DEPTH, S5_GROUPS, S5_STATE, S5_GROUP_CH), (2 * S5_GROUP_CH) ** -0.5),
        's5_b_im': nrm(ks[21], (DEPTH, S5_GROUPS, S5_STATE, S5_GROUP_CH), (2 * S5_GROUP_CH) ** -0.5),
        's5_c_re': nrm(ks[22], (DEPTH, S5_GROUPS, S5_GROUP_CH, S5_STATE), (2 * S5_STATE) ** -0.5),
        's5_c_im': nrm(ks[23], (DEPTH, S5_GROUPS, S5_GROUP_CH, S5_STATE), (2 * S5_STATE) ** -0.5),
        's5_d': nrm(ks[24], (DEPTH, S5_GROUPS, S5_GROUP_CH), 1.0),
        's5_w_glu': nrm(ks[25], (DEPTH, S5_WIDTH, 2 * S5_WIDTH), S5_WIDTH ** -0.5),
        's5_b_glu': nrm(ks[26], (DEPTH, 2 * S5_WIDTH), 0.02),
        'w_branch': nrm(ks[27], (DEPTH, N_BRANCH, BRANCH_W, D_MODEL), BRANCH_W ** -0.5),
        'w_out': nrm(ks[28], (DEPTH, D_MODEL, D_MODEL), D_MODEL ** -0.5),
    }

def reference(x, c, rel_bias, w_ada, b_ada, norm_pre, norm_post, ffn1_w_up, ffn1_w_down,
              ffn2_w_up, ffn2_w_down, w_in, gla_w_alpha, gla_b_alpha, gla_norm, diff_lambda,
              diff_norm, s5_lam_re, s5_lam_im, s5_log_step, s5_b_re, s5_b_im, s5_c_re, s5_c_im,
              s5_d, s5_w_glu, s5_b_glu, w_branch, w_out):
    h = x
    cond = jax.nn.silu(c)
    bsz = c.shape[0]
    for l in range(DEPTH):
        ada = (cond @ w_ada[l] + b_ada[l]).reshape(bsz, ADA_CHUNKS, D_MODEL)
        u = modulate(h, norm_pre[l, 0], ada[:, 0], ada[:, 1])
        y = swiglu(u, ffn1_w_up[l], ffn1_w_down[l])
        h = h + 0.5 * ada[:, 2][:, None, :] * rmsnorm(y, norm_post[l, 0])
        u = modulate(h, norm_pre[l, 1], ada[:, 3], ada[:, 4])
        y = hybrid_mixer(u, l, w_in[l], gla_w_alpha[l], gla_b_alpha[l], gla_norm[l], diff_lambda[l],
                         diff_norm[l], s5_lam_re[l], s5_lam_im[l], s5_log_step[l], s5_b_re[l],
                         s5_b_im[l], s5_c_re[l], s5_c_im[l], s5_d[l], s5_w_glu[l], s5_b_glu[l],
                         w_branch[l], w_out[l], rel_bias)
        h = h + ada[:, 5][:, None, :] * rmsnorm(y, norm_post[l, 1])
        u = modulate(h, norm_pre[l, 2], ada[:, 6], ada[:, 7])
        y = swiglu(u, ffn2_w_up[l], ffn2_w_down[l])
        h = h + 0.5 * ada[:, 8][:, None, :] * rmsnorm(y, norm_post[l, 2])
    return h


_drawn_inputs = setup_inputs


def setup_inputs(seed=0):
    import zlib

    import numpy as np

    out = dict(_drawn_inputs(seed))
    spreads = {}
    factors = {'diff_lambda': 7.167,
     's5_lam_re': 64.0,
     's5_log_step': 16.393,
     's5_b_re': 19.409,
     's5_b_im': 21.677,
     's5_c_re': 19.756,
     's5_c_im': 18.587,
     's5_b_glu': 7.098,
     's5_lam_im': 5.071}
    for name, (base, spread) in spreads.items():
        noise = np.random.default_rng([zlib.crc32(name.encode()), seed]).standard_normal(out[name].shape)
        drawn = base * np.exp(spread * noise) if base else spread * noise
        out[name] = __import__('jax').numpy.asarray(drawn.astype(out[name].dtype))
    for name, factor in factors.items():
        out[name] = (out[name] * factor).astype(out[name].dtype)
    return out
```

```python
import math
from contextlib import ExitStack

import numpy as np
import concourse.bass as bass
from concourse import mybir

F32 = mybir.dt.float32
F32R = mybir.dt.float32r
BF16 = mybir.dt.bfloat16
I32 = mybir.dt.int32
ALU = mybir.AluOpType
ACT = mybir.ActivationFunctionType
AX_X = mybir.AxisListType.X

P = 128
D_MODEL, SEQ, DEPTH, D_FF = 1024, 512, 2, 2816
KT = D_MODEL // P
FT = D_FF // P
TB = SEQ // P
EPS = 1e-6
CHUNK_ELEMS = 2048
GLA_HEADS, GLA_DK, GLA_CHUNK, LOWRANK, GLA_TAU = 4, 64, 64, 16, 16.0
N_GCH = SEQ // GLA_CHUNK
DIFF_HEADS, N_MAPS = 4, 8
NUM_BUCKETS, MAX_DISTANCE = 32, 128
S5_PAIRS, S5_CH = 16, 16
LINE = SEQ + P
MAGIC = 1.5 * 2.0 ** 23
BIG = 3.0e38
MASKED = -1.0e30
TWO_PI = 2.0 * math.pi
TWO_PI_A, TWO_PI_B = 6.28125, 0.0019340515136718750
TWO_PI_C = TWO_PI - TWO_PI_A - TWO_PI_B
LN2_A = 0.693359375
LN2_B = math.log(2.0) - LN2_A

OFF_GQ, OFF_GK, OFF_GV, OFF_GR, OFF_A = 0, 256, 512, 1024, 1536
OFF_DQ, OFF_DK, OFF_DV, OFF_SU, OFF_GATE = 1552, 2064, 2576, 3088, 3600

MIXER = [("su0", 2, "act"), ("su1", 1, "act"), ("su2", 1, "act"),
         ("gq", 2, "act"), ("gk", 2, "act"), ("ga", 1, "act"), ("gv0", 2, "act"), ("gv1", 2, "act"),
         ("gr0", 2, "act"), ("gr1", 2, "act")] + [(f"gs{i}", 2, "act") for i in range(4)] + \
        [("glu1", 4, "act"), ("glu0", 4, "vec"), ("bs0", 4, "vec"), ("bs1", 4, "vec")] + \
        [(f"d{x}{i}", 2, "act") for x in "qkv" for i in range(2)] + \
        [("gg0", 2, "act"), ("gg1", 2, "act"), ("bg0", 4, "vec"), ("gg2", 2, "act"), ("gg3", 2, "act"), ("bg1", 4, "vec")] + \
        [("gd0", 2, "act"), ("gd1", 2, "act"), ("bd0", 4, "vec"), ("gd2", 2, "act"), ("gd3", 2, "act"), ("bd1", 4, "vec")] + \
        [(f"wo{i}", 2, "sub") for i in range(4)]
FFN_CHUNKS = 2 * FT // 2 + FT // 2
C_MIX, C_FFN2 = FFN_CHUNKS, FFN_CHUNKS + len(MIXER)
CHUNKS = 2 * FFN_CHUNKS + len(MIXER)
assert CHUNKS % 2 == 0 and C_MIX % 2 == 1
SLOT_USES = CHUNKS // 2
FFN_TILES = FT + KT - 1


class Tile:
    pass


def mixer_tiles():
    tiles, evac = {}, {"act": 0, "vec": 0, "sub": 0}
    t, ready = 0, FFN_TILES
    order = []
    for i, (name, n, engine) in enumerate(MIXER):
        for k in range(n):
            x = Tile()
            x.chunk, x.bank, x.engine = C_MIX + i, t % 4, engine
            x.last = k == n - 1
            if not x.last:
                ready += 1
            x.ready = ready
            evac[engine] += 1
            x.emptied = evac[engine]
            x.before = order[t - 4] if t >= 4 else None
            order.append(x)
            tiles[name, k] = x
            t += 1
    return tiles, evac, ready


TILES, EMPTIED, READY_BEFORE_FFN2 = mixer_tiles()
CHUNK_OF = {name: C_MIX + i for i, (name, _, _) in enumerate(MIXER)}
READY_PER_LAYER = READY_BEFORE_FFN2 + FFN_TILES
VECTOR_STEPS, SCALAR_STEPS = 369, 36

V_BADA, V_PRE, V_POST, V_GNORM, V_DNORM, V_SD, V_BGLU, V_BALPHA, V_LRE, V_LIM, V_LSTEP, V_END = \
    0, 72, 96, 120, 124, 128, 132, 140, 142, 158, 174, 190


class Signal:

    def __init__(self, ctx, nc, name, per_layer, head_start=0):
        self.sem = ctx.enter_context(nc.semaphore(name))
        self.per_layer, self.head_start = per_layer, head_start

    def of(self, layer, k):
        return layer * self.per_layer + k + self.head_start


class Steps:

    def __init__(self, engine, counter, layer):
        self.engine, self.counter, self.layer, self.n = engine, counter, layer, 0

    def did(self, instruction):
        instruction.then_inc(self.counter.sem, 1)
        self.n += 1

    def wait(self, back=0):
        if self.n - back > 0:
            self.engine.wait_ge(self.counter.sem, self.counter.of(self.layer, self.n - back))


def build(nc, x, c, rel_bias, w_ada, b_ada, norm_pre, norm_post, ffn1_w_up, ffn1_w_down, ffn2_w_up, ffn2_w_down,
          w_in, gla_w_alpha, gla_b_alpha, gla_norm, diff_lambda, diff_norm, s5_lam_re, s5_lam_im, s5_log_step,
          s5_b_re, s5_b_im, s5_c_re, s5_c_im, s5_d, s5_w_glu, s5_b_glu, w_branch, w_out, bucket_onehot, out):
    ctx = ExitStack()
    with ctx:
        BASE = 16512
        X0 = 104

        def at(name, kib, shape, dt=F32):
            return nc.alloc_sbuf_tensor_at(name, shape, dt, offset=BASE + int(round(kib * 1024)))

        def shared(name, kib, shape, dt=F32):
            return at(name, X0 + kib, shape, dt)

        h = at("h", 0, [P, KT, SEQ])
        u_hi = at("u_hi", 16, [P, KT, SEQ], F32R)
        u_lo = at("u_lo", 32, [P, KT, SEQ], F32R)
        y_sub = at("y_sub", 16, [P, KT, SEQ])
        raw = [at(f"raw{s}", 48 + 8 * s, [P, CHUNK_ELEMS]) for s in range(2)]
        w_hi = [at(f"w_hi{s}", 64 + 8 * s, [P, CHUNK_ELEMS], F32R) for s in range(2)]
        w_lo = [at(f"w_lo{s}", 80 + 8 * s, [P, CHUNK_ELEMS], F32R) for s in range(2)]
        ident = at("ident", 96, [P, P])
        ones = at("ones", 96.5, [P, P])
        time_row = at("time_row", 97, [P, SEQ])
        chunk_mask = at("chunk_mask", 99, [P, SEQ], BF16)
        clamp_hi = at("clamp_hi", 100, [P, P])
        clamp_lo = at("clamp_lo", 100.5, [P, P])
        vec = at("vec", 101, [P, V_END])
        ada = at("ada", 101.75, [P, 72])
        pre_gain = at("pre_gain", 102.0625, [P, 24])
        post_gain = at("post_gain", 102.1875, [P, 24])
        s5v = at("s5v", 102.3125, [P, 4, S5_PAIRS])
        small = at("small", 102.5625, [P, 48])
        cond = at("cond", 102.75, [P, KT])
        sq_root = at("sq_root", 102.8125, [P, 16])
        rstd_tok = at("rstd_tok", 102.875, [P, 16])
        ms_heads = at("ms_heads", 102.9375, [P, 16])
        gd_gain = at("gd_gain", 103, [P, 4])
        smax = at("smax", 103.0625, [P, 2, 8])
        lam_tab = at("lam_tab", 103.25, [P, 2 * DEPTH])
        inv_d = at("inv_d", 103.3125, [P, 2])
        cst = at("cst", 103.375, [P, 2])
        EPS_COL, HALF_PI = cst[:, 0:1], cst[:, 1:2]
        neg_lam = small[:, 46:47]
        phase, mag, f_re, f_im = (s5v[:, i, :] for i in range(4))

        g_hi = shared("g_hi", 0, [P, FT, SEQ], F32R)
        g_lo = shared("g_lo", 44, [P, FT, SEQ], F32R)
        silu_buf = shared("silu_buf", 88, [P, 2, SEQ])
        diag = shared("diag", 88, [P, TB, P])
        mod_buf = shared("mod_buf", 92, [P, 2, SEQ])
        sq_buf = shared("sq_buf", 96, [P, 2, SEQ])
        sq_sum = shared("sq_sum", 100, [P, SEQ])
        ada_w = [shared(f"ada_w{s}", 8 * s, [P, KT, 256]) for s in range(4)]
        ada_acc = [shared(f"ada_acc{s}", 32 + s, [P, 256]) for s in range(2)]
        rows_a = shared("rows_a", 36, [72, P])
        rows_b = shared("rows_b", 37, [V_LSTEP - 72, P])
        lam_rows = shared("lam_rows", 38, [P, 4, 64])
        lam_prod = shared("lam_prod", 39, [P, 64])
        log_steps = shared("log_steps", 39.5, [P, 2 * S5_PAIRS])
        x_tok = shared("x_tok", 0, [P, TB, D_MODEL])
        c_row = shared("c_row", 16, [KT, P])
        onehot = shared("onehot", 17, [NUM_BUCKETS + 1, LINE])
        rel33 = shared("rel33", 20, [NUM_BUCKETS + 1, N_MAPS])
        bias_line = shared("bias_line", 21, [N_MAPS, LINE])
        pscr = shared("pscr", 40, [P, 12, S5_PAIRS])
        pint = shared("pint", 41, [P, S5_PAIRS], I32)
        su = shared("su", 0, [P, 4, SEQ])
        s_state = shared("s_state", 0, [P, 2, N_GCH, P])
        gq = shared("gq", 8, [P, 2, SEQ])
        gk = shared("gk", 12, [P, 2, SEQ])
        gv = shared("gv", 16, [P, TB, SEQ])
        gr = shared("gr", 24, [P, 4, SEQ])
        merged = shared("merged", 32, [P, KT, SEQ])
        s5_bt = shared("s5_bt", 48, [P, 2, 4, P])
        s5_ct = shared("s5_ct", 52, [P, 2, 4, P])
        s5_bx = shared("s5_bx", 58, [P, 2, 4, 4, 2, S5_CH])
        s5_cd = shared("s5_cd", 62, [P, 2, 4, 2, 64])
        s5_b = shared("s5_b", 66, [P, 2, S5_PAIRS, S5_CH])
        s5_t = shared("s5_t", 68, [P, 2, S5_PAIRS, S5_CH])
        s5_mask = shared("s5_mask", 70, [P, 4, 2, S5_CH])
        rot = shared("rot", 58, [P, 2, 4, SEQ])
        tab_c = shared("tab_c", 74, [P, 3, SEQ])
        tab_s = shared("tab_s", 80, [P, 3, SEQ])
        turns = shared("turns", 86, [P, 2, SEQ])
        rounded = shared("rounded", 90, [P, SEQ])
        a_low = shared("a_low", 92, [LOWRANK, SEQ])
        w_alpha = shared("w_alpha", 56, [LOWRANK, 256])
        yg_hi = shared("yg_hi", 58, [P, 4, SEQ], F32R)
        yg_lo = shared("yg_lo", 66, [P, 4, SEQ], F32R)
        z_gate = shared("z_gate", 0, [P, 4, SEQ])
        ys_hi = shared("ys_hi", 74, [P, 4, SEQ], F32R)
        ys_lo = shared("ys_lo", 82, [P, 4, SEQ], F32R)
        la = shared("la", 48, [P, 2, SEQ])
        lb = shared("lb", 52, [P, 2, SEQ])
        eb = shared("eb", 56, [P, 2, SEQ])
        kk_tok = shared("kk_tok", 60, [P, TB, 2 * P])
        att = shared("att", 64, [P, 2, TB, P])
        o_head = [shared(f"o_head{i}", k, [P, SEQ]) for i, k in enumerate((68, 70, 90, 72))]
        o_sq = shared("o_sq", 92, [P, SEQ])
        head_diag = [shared("gla_diag", 52, [P, SEQ]), shared("diff_diag", 90, [P, SEQ])]
        dq = shared("dq", 74, [P, 4, SEQ])
        dk = shared("dk", 82, [P, 4, SEQ])
        dv = shared("dv", 94, [P, TB, SEQ])
        yga_hi = shared("yga_hi", 48, [P, 4, SEQ], F32R)
        yga_lo = shared("yga_lo", 56, [P, 4, SEQ], F32R)
        sig = shared("sig", 0, [P, 4, SEQ])
        bias_tab = shared("bias_tab", 8, [P, N_MAPS, SEQ])
        a_t = shared("a_t", 24, [P, TB, SEQ])
        prob = [shared("prob0", 64, [P, 2, SEQ]), shared("prob1", 68, [P, 2, SEQ])]
        yd_hi = shared("yd_hi", 48, [P, 4, SEQ], F32R)
        yd_lo = shared("yd_lo", 56, [P, 4, SEQ], F32R)
        mg_hi = shared("mg_hi", 8, [P, KT, SEQ], F32R)
        mg_lo = shared("mg_lo", 74, [P, KT, SEQ], F32R)

        bank = [ctx.enter_context(nc.psum_tensor(f"bank{i}", [P, SEQ], F32)) for i in range(8)]
        bias_dram = nc.dram_tensor("bias_line_dram", (N_MAPS, LINE), F32, kind="Internal").ap()
        bias_copies = nc.dram_tensor("bias_copies_dram", (N_MAPS, P, LINE), F32, kind="Internal").ap()

        def signal(name, per_layer, head_start=0):
            return Signal(ctx, nc, name, per_layer, head_start)

        def sem(name):
            return ctx.enter_context(nc.semaphore(name))

        raw_loaded = [signal(f"raw_loaded{s}", 16 * SLOT_USES) for s in range(2)]
        hi_split = [signal(f"hi_split{s}", SLOT_USES, 1) for s in range(2)]
        lo_split = [signal(f"lo_split{s}", SLOT_USES, 1) for s in range(2)]
        chunk_done = [signal(f"chunk_done{s}", SLOT_USES, 1) for s in range(2)]
        tile_ready = signal("tile_ready", READY_PER_LAYER)
        emptied = {"act": signal("emptied_by_act", EMPTIED["act"]), "vec": signal("emptied_by_vec", EMPTIED["vec"])}
        silu_done = signal("silu_done", 2 * FT, 2)
        prod_done = signal("prod_done", 2 * FT, 2)
        g_hi_ready = signal("g_hi_ready", 2 * FT)
        g_lo_ready = signal("g_lo_ready", 2 * FT, 2)
        h_ready = signal("h_ready", 3 * KT, KT)
        sq_ready = signal("sq_ready", 6 * KT)
        sq_summed = signal("sq_summed", 6 * KT, 2)
        y_copied = signal("y_copied", 3 * KT)
        ms_ready = signal("ms_ready", 6)
        root_ready = signal("root_ready", 6)
        diag_ready = signal("diag_ready", 6)
        rstd_ready = signal("rstd_ready", 6)
        modulated = signal("modulated", 3 * KT)
        u_hi_ready = signal("u_hi_ready", 3 * KT)
        u_ready = signal("u_ready", 3 * KT)
        vector_steps = signal("vector_steps", VECTOR_STEPS)
        scalar_steps = signal("scalar_steps", SCALAR_STEPS)
        x_loaded, c_loaded, line_loaded = sem("x_loaded"), sem("c_loaded"), sem("line_loaded")
        const_ready, x_turned, c_turned = sem("const_ready"), sem("x_turned"), sem("c_turned")
        cond_ready, line_made, line_copied, line_stored = sem("cond_ready"), sem("line_made"), sem("line_copied"), sem("line_stored")
        out_turned, out_half, out_copied, out_stored = sem("out_turned"), sem("out_half"), sem("out_copied"), sem("out_stored")
        pool_start = sem("pool_start")
        ada_loaded = [signal(f"ada_loaded{s}", 16 * 9) for s in range(4)]
        ada_step = signal("ada_step", 36 * KT, 4 * KT)
        ada_column = signal("ada_column", 36, 2)
        ROW_DMAS = 10
        rows_loaded = signal("rows_loaded", 16 * ROW_DMAS)
        rows_turned = signal("rows_turned", 1)
        vec_ready = signal("vec_ready", 1)
        theta_ready = signal("theta_ready", 1)
        sines_ready = signal("sines_ready", 2)
        lam_sums = signal("lam_sums", 2)
        lam_exps = signal("lam_exps", 1)
        gains_ready = signal("gains_ready", 1)
        s5w_loaded = signal("s5w_loaded", 16 * 8)
        s5_bx_zero = signal("s5_bx_zero", 1)
        s5_mask_ready = signal("s5_mask_ready", 3)
        s5_bx_ready = signal("s5_bx_ready", 1)
        s5_turned = signal("s5_turned", 2)
        s5_mats_ready = signal("s5_mats_ready", 1)
        turns_ready = signal("turns_ready", S5_PAIRS)
        tables_ready = signal("tables_ready", S5_PAIRS)
        bu_ready = signal("bu_ready", S5_PAIRS)
        front_done = signal("front_done", S5_PAIRS)
        z_in_ready = signal("z_in_ready", 2 * S5_PAIRS)
        back_done = signal("back_done", S5_PAIRS)
        state_ready = signal("state_ready", 2 * S5_PAIRS)
        alpha_loaded = signal("alpha_loaded", 16)
        s5_y_ready = signal("s5_y_ready", S5_PAIRS)
        s5_y_summed = signal("s5_y_summed", 4)
        gelu_done = signal("gelu_done", 4)
        split_hi = signal("split_hi", 4 + 4 + 4 + 4 + 8)
        split_lo = signal("split_lo", 4 + 4 + 4 + 4 + 8)
        YG, YS, YGA, YD, MG = 0, 4, 8, 12, 16
        merged_ready = signal("merged_ready", 16)
        alpha_ready = signal("alpha_ready", 2)
        alpha_read = signal("alpha_read", 2)
        alpha_exps = signal("alpha_exps", 2)
        decay_sum = signal("decay_sum", 2)
        decay_last = signal("decay_last", 2)
        gla_exps = signal("gla_exps", 6)
        gla_keys = signal("gla_keys", 6)
        kk_turned = signal("kk_turned", 1)
        kk_copied = signal("kk_copied", 2)
        ds_ready = signal("ds_ready", 2)
        s_ready = signal("s_ready", 2)
        att_ready = signal("att_ready", 4)
        att_clamped = signal("att_clamped", 4)
        o_ready = signal("o_ready", 8)
        o_copied = signal("o_copied", 8)
        o_squared = signal("o_squared", 8)
        o_ms = signal("o_ms", 8)
        o_ms_kept = signal("o_ms_kept", 8)
        o_roots = signal("o_roots", 2)
        o_diag = signal("o_diag", 8)
        o_rstd = signal("o_rstd", 8)
        o_normed = signal("o_normed", 8)
        yga_done = signal("yga_done", 4)
        bias_loaded = signal("bias_loaded", 16)
        scores_ready = signal("scores_ready", 32)
        scores_seen, states_begun, room_seen = signal("scores_seen", 16), signal("states_begun", 2), signal("room_seen", 2)
        max_ready = signal("max_ready", 16)
        prob_ready = signal("prob_ready", 16)
        mix_ready = signal("mix_ready", 16)
        at_ready = signal("at_ready", 16)
        at_copied = signal("at_copied", 16)

        def cols(j, n=1):
            return bass.ds(j, n)

        def flat(ap):
            return ap.rearrange("p a n -> p (a n)")

        def slot_value(sig, L, chunk, extra=0):
            return sig.of(L, chunk // 2 + 1 + extra)

        def chunk_widths(name):
            return P if name in ("su1", "su2", "ga") else 256

        block = ctx.enter_context(nc.Block())

        @block.sync
        def _(sp):
            def load(L, s, n, dst, src):
                sp.wait_ge(hi_split[s].sem, hi_split[s].of(L, n - 1))
                sp.wait_ge(lo_split[s].sem, lo_split[s].of(L, n - 1))
                sp.dma_start(dst, src).then_inc(raw_loaded[s].sem, 16)

            def load_ffn(L, f, c0, w_up, w_down):
                with sp.Fori(0, FT // 2) as j:
                    for half in range(2):
                        s = (c0 + half) % 2
                        n = (c0 + half) // 2 + j + 1
                        src = w_up[L, :, bass.ds(j * 256 + half * D_FF, 256)].rearrange("(k p) n -> p k n", p=P)
                        load(L, s, n, raw[s][:, :].rearrange("p (k n) -> p k n", k=KT), src)
                c1 = c0 + FT
                s = c1 % 2
                load(L, s, c1 // 2 + 1, raw[s][:, :].rearrange("p (k n) -> p k n", k=2),
                     w_down[L, 0:256, :].rearrange("(k p) n -> p k n", p=P))
                with sp.Fori(0, FT // 4) as j:
                    for half in range(2):
                        s = (c1 + 1 + half) % 2
                        n = (c1 + 1 + half) // 2 + j + 1
                        src = w_down[L, bass.ds(j * 512 + half * 256 + 256, 256), :].rearrange("(k p) n -> p k n", p=P)
                        load(L, s, n, raw[s][:, :].rearrange("p (k n) -> p k n", k=2), src)

            def load_chunk(L, name):
                ch = CHUNK_OF[name]
                s = ch % 2
                i = int(name[-1]) if name[-1].isdigit() else 0
                start = {"su": OFF_SU, "gq": OFF_GQ, "gk": OFF_GK, "ga": OFF_A, "gv": OFF_GV, "gr": OFF_GR,
                         "dq": OFF_DQ, "dk": OFF_DK, "dv": OFF_DV, "gg": OFF_GATE, "gd": OFF_GATE + D_MODEL,
                         "gs": OFF_GATE + 2 * D_MODEL}.get(name[:2])
                if start is not None:
                    w = chunk_widths(name)
                    start += {"su1": 256, "su2": 384}.get(name, 256 * i)
                    load(L, s, ch // 2 + 1, raw[s][:, 0:KT * w].rearrange("p (k n) -> p k n", k=KT),
                         w_in[L, :, start:start + w].rearrange("(k p) n -> p k n", p=P))
                elif name[:2] == "wo":
                    load(L, s, ch // 2 + 1, raw[s][:, :].rearrange("p (k n) -> p k n", k=KT),
                         w_out[L, :, 256 * i:256 * i + 256].rearrange("(k p) n -> p k n", p=P))
                else:
                    src = s5_w_glu[L] if name[:3] == "glu" else w_branch[L, {"bg": 0, "bd": 1, "bs": 2}[name[:2]]]
                    load(L, s, ch // 2 + 1, raw[s][:, :].rearrange("p (k n) -> p k n", k=4),
                         src[:, 512 * i:512 * i + 512].rearrange("(k p) n -> p k n", p=P))

            sp.dma_start(c_row[:, :], c.rearrange("a (k p) -> (a k) p", p=P)).then_inc(c_loaded, 16)
            sp.dma_start(x_tok[:, :, :], x.rearrange("a (b p) d -> p (a b) d", p=P)).then_inc(x_loaded, 16)
            sp.dma_start(onehot[:, :], bucket_onehot).then_inc(line_loaded, 16)
            sp.dma_start(rel33[0:NUM_BUCKETS, :], rel_bias).then_inc(line_loaded, 16)
            sp.wait_ge(line_copied, 2)
            sp.dma_start(bias_dram, bias_line[:, :]).then_inc(line_stored, 16)
            sp.wait_ge(line_stored, 16)
            sp.dma_start(bias_copies, bias_dram.unsqueeze(1).to_broadcast([N_MAPS, P, LINE])).then_inc(line_stored, 16)

            with sp.Fori(0, DEPTH) as L:
                sp.wait_ge(h_ready.sem, h_ready.of(L, 0))
                sp.wait_ge(cond_ready, 1)

                def row(dst, src):
                    sp.dma_start(dst, src).then_inc(rows_loaded.sem, 16)

                def rb(a, b):
                    return rows_b[a - 72:b - 72, :]

                row(rows_a[:, :], b_ada[L].rearrange("(k p) -> k p", p=P))
                row(rb(V_PRE, V_POST), norm_pre[L].rearrange("a (k p) -> (a k) p", p=P))
                row(rb(V_POST, V_GNORM), norm_post[L].rearrange("a (k p) -> (a k) p", p=P))
                row(rb(V_GNORM, V_DNORM), gla_norm[L].rearrange("(k p) -> k p", p=P))
                row(rb(V_DNORM, V_SD), diff_norm[L].rearrange("(k p) -> k p", p=P))
                row(rb(V_SD, V_BGLU), s5_d[L].rearrange("(k g) n -> k (g n)", k=4))
                row(rb(V_BGLU, V_BALPHA), s5_b_glu[L].rearrange("(k p) -> k p", p=P))
                row(rb(V_BALPHA, V_LRE), gla_b_alpha[L].rearrange("(k p) -> k p", p=P))
                row(rb(V_LRE, V_LIM), s5_lam_re[L].rearrange("(j g) p -> j (g p)", g=2))
                row(rb(V_LIM, V_LSTEP), s5_lam_im[L].rearrange("(j g) p -> j (g p)", g=2))
                sp.dma_start(log_steps[:, :], s5_log_step[L].unsqueeze(0).to_broadcast([P, 2 * S5_PAIRS])).then_inc(s5w_loaded.sem, 16)
                sp.dma_start(lam_rows[:, :, :], diff_lambda[L].unsqueeze(0).to_broadcast([P, 4, 64])).then_inc(s5w_loaded.sem, 16)
                with sp.Fori(0, 9) as i:
                    for s in range(4):
                        sp.wait_ge(ada_step.sem, ada_step.of(L, (i * 4 + s - 3) * KT))
                        sp.dma_start(ada_w[s][:, :, :], w_ada[L, :, bass.ds(i * 1024 + s * 256, 256)]
                                     .rearrange("(k p) n -> p k n", p=P)).then_inc(ada_loaded[s].sem, 16)
                load_ffn(L, 0, 0, ffn1_w_up, ffn1_w_down)
                s = (C_MIX - 1) % 2
                sp.wait_ge(chunk_done[s].sem, slot_value(chunk_done[s], L, C_MIX - 1))
                for i, (b, cc) in enumerate(((s5_b_re, s5_c_re), (s5_b_im, s5_c_im))):
                    sp.dma_start(s5_b[:, i, :, :], b[L].rearrange("(j g) p h -> (g p) j h", g=2)).then_inc(s5w_loaded.sem, 16)
                    for d in range(2):
                        sp.dma_start(s5_cd[:, i, :, d, :], cc[L].rearrange("(q g) n p -> (g n) q p", q=4))\
                          .then_inc(s5w_loaded.sem, 16)
                for name, _, _ in MIXER[:14]:
                    load_chunk(L, name)
                for name, _, _ in MIXER[14:18]:
                    load_chunk(L, name)
                sp.dma_start(w_alpha[:, :], gla_w_alpha[L]).then_inc(alpha_loaded.sem, 16)
                for name, _, _ in MIXER[18:26]:
                    load_chunk(L, name)
                sp.wait_ge(yga_done.sem, yga_done.of(L, 4))
                sp.wait_ge(line_stored, 32)
                lines = bass.AP(tensor=bias_copies.tensor, offset=P - 1, ap=[[LINE - 1, P], [P * LINE, N_MAPS], [1, SEQ]])
                sp.dma_start(bias_tab[:, :, :], lines).then_inc(bias_loaded.sem, 16)
                for name, _, _ in MIXER[26:]:
                    load_chunk(L, name)
                load_ffn(L, 1, C_FFN2, ffn2_w_up, ffn2_w_down)

            for b in range(TB):
                sp.wait_ge(out_copied, b + 1)
                sp.dma_start(out[0, b * P:(b + 1) * P, :], x_tok[:, b, :]).then_inc(out_stored, 16)
            sp.wait_ge(out_stored, 16 * TB)

        @block.tensor
        def _(pe):
            for s in range(2):
                pe.sem_inc(chunk_done[s].sem, 1)
            pe.sem_inc(ada_column.sem, 2)

            def matmul3(dst, hi, lo, rhi, rlo, first, last):
                pe.matmul(dst, hi, rhi, start=first, stop=False)
                pe.matmul(dst, hi, rlo, start=False, stop=False)
                return pe.matmul(dst, lo, rhi, start=False, stop=last)

            def mean_square(L, r):
                pe.wait_ge(sq_summed.sem, sq_summed.of(L, KT * (r + 1)))
                for b in range(TB):
                    m = pe.matmul(bank[0][:, b:b + 1], sq_sum[:, b * P:(b + 1) * P], inv_d[:, 0:1], start=True, stop=True)
                m.then_inc(ms_ready.sem, 1)
                pe.wait_ge(diag_ready.sem, diag_ready.of(L, r + 1))
                pe.matmul(bank[1][:, :], ones[:, :], flat(diag[:, :, :]), start=True, stop=True).then_inc(rstd_ready.sem, 1)

            def ffn(L, f, c0):
                ui = 2 * f
                i0 = f * FT
                with pe.Fori(0, FT // 2) as j:
                    for half in range(2):
                        s = (c0 + half) % 2
                        wh = w_hi[s][:, :].rearrange("p (k n) -> p k n", k=KT)
                        wl = w_lo[s][:, :].rearrange("p (k n) -> p k n", k=KT)
                        pe.wait_ge(lo_split[s].sem, lo_split[s].of(L, (c0 + half) // 2 + j + 1))
                        for mt in range(2):
                            freed = (silu_done, prod_done)[half]
                            pe.wait_ge(freed.sem, freed.of(L, i0 + 2 * j + mt - 1))
                            for k in range(KT):
                                if half == 0 and mt == 0:
                                    pe.wait_ge(u_ready.sem, u_ready.of(L, ui * KT + k + 1))
                                m = matmul3(bank[2 * half + mt][:, :], wh[:, k, mt * P:(mt + 1) * P], wl[:, k, mt * P:(mt + 1) * P],
                                            u_hi[:, k, :], u_lo[:, k, :], k == 0, k == KT - 1)
                            m.then_inc(chunk_done[s].sem if mt else tile_ready.sem, 1)
                c1 = c0 + FT

                def down(s, n, kt, first, last):
                    wh = w_hi[s][:, :].rearrange("p (k n) -> p k n", k=2)
                    wl = w_lo[s][:, :].rearrange("p (k n) -> p k n", k=2)
                    pe.wait_ge(lo_split[s].sem, lo_split[s].of(L, n))
                    pe.wait_ge(g_lo_ready.sem, g_lo_ready.of(L, i0 + kt + 2))
                    order = [(k, m) for m in range(KT) for k in range(2)] if last else \
                        [(k, m) for k in range(2) for m in ((4, 5, 6, 7, 0, 1, 2, 3) if first else range(KT))]
                    for k, m in order:
                        if first and k == 0 and m == 0:
                            pe.wait_ge(silu_done.sem, silu_done.of(L, i0 + FT))
                            pe.wait_ge(prod_done.sem, prod_done.of(L, i0 + FT))
                        if isinstance(kt, int):
                            rh, rl = g_hi[:, kt + k, :], g_lo[:, kt + k, :]
                        else:
                            rh, rl = flat(g_hi[:, cols(kt + k), :]), flat(g_lo[:, cols(kt + k), :])
                        i = matmul3(bank[m][:, :], wh[:, k, m * P:(m + 1) * P], wl[:, k, m * P:(m + 1) * P], rh, rl,
                                    first and k == 0, last and k == 1)
                        if last and k == 1 and m < KT - 1:
                            i.then_inc(tile_ready.sem, 1)
                    i.then_inc(chunk_done[s].sem, 1)

                down(c1 % 2, c1 // 2 + 1, 0, True, False)
                with pe.Fori(0, FT // 4 - 1) as j:
                    for half in range(2):
                        cc = c1 + 1 + half
                        down(cc % 2, cc // 2 + j + 1, j * 4 + 2 + 2 * half, False, False)
                for d in (FT // 2 - 2, FT // 2 - 1):
                    down((c1 + d) % 2, (c1 + d) // 2 + 1, 2 * d, False, d == FT // 2 - 1)

            def bank_free(L, t):
                last = t.before
                if last is not None and last.engine == "sub":
                    pe.wait_ge(sq_ready.sem, sq_ready.of(L, 3 * KT + last.emptied))
                elif last is not None:
                    pe.wait_ge(emptied[last.engine].sem, emptied[last.engine].of(L, last.emptied))

            def chunk_tile(L, name, k, src=None):
                ch = CHUNK_OF[name]
                s = ch % 2
                if k == 0:
                    pe.wait_ge(lo_split[s].sem, slot_value(lo_split[s], L, ch))
                t = TILES[name, k]
                bank_free(L, t)
                hi, lo, n, ready = src or (u_hi, u_lo, KT, None)
                w = 512 if n == 4 else chunk_widths(name)
                wh = w_hi[s][:, 0:n * w].rearrange("p (k n) -> p k n", k=n)
                wl = w_lo[s][:, 0:n * w].rearrange("p (k n) -> p k n", k=n)
                for kt in range(n):
                    if k == 0 and ready is not None:
                        pe.wait_ge(split_lo.sem, split_lo.of(L, ready + kt + 1))
                    elif k == 0 and name == "su0":
                        pe.wait_ge(u_ready.sem, u_ready.of(L, KT + kt + 1))
                    m = matmul3(bank[t.bank][:, :], wh[:, kt, k * P:(k + 1) * P], wl[:, kt, k * P:(k + 1) * P],
                                hi[:, kt, :], lo[:, kt, :], kt == 0, kt == n - 1)
                m.then_inc(chunk_done[s].sem if t.last else tile_ready.sem, 1)

            def value_tile(L, name, k):
                ch = CHUNK_OF[name]
                s = ch % 2
                if k == 0:
                    pe.wait_ge(lo_split[s].sem, slot_value(lo_split[s], L, ch))
                t = TILES[name, k]
                bank_free(L, t)
                wh = w_hi[s][:, :].rearrange("p (k n) -> p k n", k=KT)
                wl = w_lo[s][:, :].rearrange("p (k n) -> p k n", k=KT)
                for half in range(2):
                    b = 2 * k + half
                    dst = bank[t.bank][:, half * 256:(half + 1) * 256]
                    tok = slice(b * P, (b + 1) * P)
                    for kt in range(KT):
                        pe.matmul(dst, u_hi[:, kt, tok], wh[:, kt, :], start=kt == 0, stop=False)
                        pe.matmul(dst, u_lo[:, kt, tok], wh[:, kt, :], start=False, stop=False)
                        m = pe.matmul(dst, u_hi[:, kt, tok], wl[:, kt, :], start=False, stop=kt == KT - 1)
                m.then_inc(chunk_done[s].sem if t.last else tile_ready.sem, 1)

            def s5_matrices(L):
                pe.wait_ge(s5_bx_ready.sem, s5_bx_ready.of(L, 1))
                for i in range(2):
                    for q in range(4):
                        m = pe.transpose(bank[4 + i][:, q * P:(q + 1) * P],
                                         s5_bx[:, i, q].rearrange("p a g h -> p (a g h)"), ident[:, :])
                m.then_inc(s5_turned.sem, 1)
                pe.wait_ge(s5w_loaded.sem, s5w_loaded.of(L, 16 * 8))
                for i in range(2):
                    for q in range(4):
                        m = pe.transpose(bank[6 + i][:, q * P:(q + 1) * P],
                                         s5_cd[:, i, q].rearrange("p a n -> p (a n)"), ident[:, :])
                m.then_inc(s5_turned.sem, 1)

            def s5_in(L, j):
                q, i = divmod(j, 4)
                if j == 0:
                    pe.wait_ge(s5_mats_ready.sem, s5_mats_ready.of(L, 1))
                else:
                    pe.wait_ge(front_done.sem, front_done.of(L, j))
                t = TILES[("su0", q) if q < 2 else (f"su{q - 1}", 0)]
                pe.wait_ge(emptied["act"].sem, emptied["act"].of(L, t.emptied))
                rows = slice(32 * i, 32 * i + 32)
                for part in range(2):
                    m = pe.matmul(bank[4 + part][:, :], s5_bt[rows, part, q, :], su[rows, q, :], start=True, stop=True)
                m.then_inc(bu_ready.sem, 1)

            def s5_out(L, j):
                q, i = divmod(j, 4)
                if i == 0 and q >= 2:
                    pe.wait_ge(s5_y_summed.sem, s5_y_summed.of(L, q - 1))
                pe.wait_ge(state_ready.sem, state_ready.of(L, 2 * j + 2))
                for part in range(2):
                    m = pe.matmul(bank[6 + q % 2][32 * i:32 * i + 32, :], s5_ct[:, part, q, 32 * i:32 * i + 32],
                                  rot[:, j % 2, part, :], start=part == 0, stop=part == 1)
                m.then_inc(s5_y_ready.sem, 1)

            def gla_alpha(L):
                pe.wait_ge(alpha_loaded.sem, alpha_loaded.of(L, 16))
                pe.wait_ge(emptied["act"].sem, emptied["act"].of(L, TILES["ga", 0].emptied))
                for t in range(2):
                    pe.matmul(bank[4 + t][:, :], w_alpha[:, t * P:(t + 1) * P], a_low[:, :], start=True, stop=True)\
                      .then_inc(alpha_ready.sem, 1)

            def gla_turn_keys(L):
                pe.wait_ge(gla_keys.sem, gla_keys.of(L, 6))
                for b in range(TB):
                    for t in range(2):
                        m = pe.transpose(bank[4 + b // 2][:, (b % 2) * 256 + t * P:(b % 2) * 256 + (t + 1) * P],
                                         gk[:, t, b * P:(b + 1) * P], ident[:, :])
                m.then_inc(kk_turned.sem, 1)

            def gla_states(L, t):
                if t == 0:
                    pe.wait_ge(kk_copied.sem, kk_copied.of(L, 2))
                else:
                    pe.wait_ge(s_ready.sem, s_ready.of(L, 1))
                pe.sem_inc(states_begun.sem, 1)
                for n in range(N_GCH - 1):
                    b, rows = n // 2, slice(64 * (n % 2), 64 * (n % 2) + 64)
                    for par in range(2):
                        hd = 2 * t + par
                        m = pe.matmul(bank[6 + n % 2][64 * par:64 * par + 64, (n // 2) * P:(n // 2 + 1) * P],
                                      kk_tok[rows, b, t * P + 64 * par:t * P + 64 * par + 64],
                                      gv[rows, b, hd * P:(hd + 1) * P], start=True, stop=True)
                m.then_inc(ds_ready.sem, 1)

            def gla_scores(L, hd):
                t, par = divmod(hd, 2)
                rows = slice(64 * par, 64 * par + 64)
                if hd == 0:
                    pe.wait_ge(kk_copied.sem, kk_copied.of(L, 2))
                else:
                    pe.wait_ge(att_clamped.sem, att_clamped.of(L, hd))
                for b in range(TB):
                    blk = slice(b * P, (b + 1) * P)
                    m = pe.matmul(bank[4][:, blk], la[rows, t, blk], gq[rows, t, blk], start=True, stop=True)
                m.then_inc(att_ready.sem, 1)

            def head_ms(L, hh, bk):
                pe.wait_ge(o_squared.sem, o_squared.of(L, hh + 1))
                pe.wait_ge(o_copied.sem, o_copied.of(L, hh + 1))
                for b in range(TB):
                    m = pe.matmul(bank[bk][:, b:b + 1], o_sq[:, b * P:(b + 1) * P], inv_d[:, 1:2], start=True, stop=True)
                m.then_inc(o_ms.sem, 1)

            def gla_out(L, hd):
                t, par = divmod(hd, 2)
                rows = slice(64 * par, 64 * par + 64)
                bk = 6 + hd % 2
                pe.wait_ge(att_clamped.sem, att_clamped.of(L, hd + 1))
                pe.wait_ge(s_ready.sem, s_ready.of(L, 2))
                if hd >= 2:
                    pe.wait_ge(o_ms_kept.sem, o_ms_kept.of(L, hd - 1))
                for b in range(TB):
                    pe.matmul(bank[bk][:, b * P:(b + 1) * P], gv[:, b, hd * P:(hd + 1) * P], att[:, hd % 2, b, :],
                              start=True, stop=False)
                    for n in (2 * b, 2 * b + 1):
                        if n:
                            tok = slice(n * GLA_CHUNK, (n + 1) * GLA_CHUNK)
                            m = pe.matmul(bank[bk][:, tok], s_state[rows, t, n, :], gq[rows, t, tok], start=False, stop=n % 2 == 1)
                m.then_inc(o_ready.sem, 1)

            def head_rstd(L, hh, bk):
                pe.wait_ge(o_diag.sem, o_diag.of(L, hh + 1))
                pe.matmul(bank[bk][:, :], ones[:, :], head_diag[hh // 4][:, :], start=True, stop=True).then_inc(o_rstd.sem, 1)

            def diff_scores(L, hd, qb):
                i = hd * TB + qb
                n = (qb + 1) * P
                if i == 0:
                    pe.wait_ge(o_normed.sem, o_normed.of(L, 4))
                else:
                    pe.wait_ge(max_ready.sem, max_ready.of(L, i))
                for par in range(2):
                    rows = slice(64 * par, 64 * par + 64)
                    pe.matmul(bank[4 + par][:, 0:n], dq[rows, hd, qb * P:(qb + 1) * P], dk[rows, hd, 0:n],
                              start=True, stop=True).then_inc(scores_ready.sem, 1)

            def diff_turn(L, hd, qb):
                i = hd * TB + qb
                pe.wait_ge(mix_ready.sem, mix_ready.of(L, i + 1))
                if i:
                    pe.wait_ge(at_copied.sem, at_copied.of(L, i))
                for j in range(qb + 1):
                    m = pe.transpose(bank[6][:, j * P:(j + 1) * P], prob[i % 2][:, 0, j * P:(j + 1) * P], ident[:, :])
                m.then_inc(at_ready.sem, 1)

            def diff_out(L, hd):
                pe.wait_ge(at_copied.sem, at_copied.of(L, (hd + 1) * TB))
                pe.wait_ge(o_ms_kept.sem, o_ms_kept.of(L, 4 + hd))
                for j in range(TB):
                    m = pe.matmul(bank[7][:, j * P:SEQ], dv[:, j, hd * P:(hd + 1) * P], a_t[:, j, j * P:SEQ],
                                  start=j == 0, stop=j == TB - 1)
                m.then_inc(o_ready.sem, 1)

            def mixer(L):
                s5_matrices(L)
                for name, n, _ in MIXER[:3]:
                    for k in range(n):
                        chunk_tile(L, name, k)
                s5_in(L, 0)
                done = 0
                gaps = 0
                for name, n, _ in MIXER[3:14]:
                    for k in range(n):
                        (value_tile if name[:2] == "gv" else chunk_tile)(L, name, k)
                        gaps += 1
                        while done < min(S5_PAIRS, (gaps * S5_PAIRS) // 20):
                            if done + 1 < S5_PAIRS:
                                s5_in(L, done + 1)
                            if done:
                                s5_out(L, done - 1)
                            done += 1
                s5_out(L, S5_PAIRS - 1)
                for name in ("glu1", "glu0"):
                    for k in range(4):
                        chunk_tile(L, name, k, (yg_hi, yg_lo, 4, YG))
                for name in ("bs0", "bs1"):
                    for k in range(4):
                        chunk_tile(L, name, k, (ys_hi, ys_lo, 4, YS))
                gla_alpha(L)
                for k in range(2):
                    chunk_tile(L, "dq0", k)
                for k in range(2):
                    chunk_tile(L, "dq1", k)
                gla_turn_keys(L)
                for k in range(2):
                    chunk_tile(L, "dk0", k)
                gla_states(L, 0)
                gla_scores(L, 0)
                for k in range(2):
                    chunk_tile(L, "dk1", k)
                gla_states(L, 1)
                gla_scores(L, 1)
                value_tile(L, "dv0", 0)
                for hd in range(GLA_HEADS):
                    gla_out(L, hd)
                    if hd + 2 < GLA_HEADS:
                        gla_scores(L, hd + 2)
                    if hd < 3:
                        value_tile(L, *(("dv0", 1), ("dv1", 0), ("dv1", 1))[hd])
                    head_ms(L, hd, 6 + hd % 2)
                for hd in range(GLA_HEADS):
                    head_rstd(L, hd, 4 + hd % 2)
                between = [("gg0", 0), ("gg0", 1), ("gg1", 0), ("gg1", 1)] + [("bg0", k) for k in range(4)] + \
                    [("gg2", 0), ("gg2", 1), ("gg3", 0), ("gg3", 1)] + [("bg1", k) for k in range(4)]
                diff_scores(L, 0, 0)
                for i in range(DIFF_HEADS * TB):
                    hd, qb = divmod(i, TB)
                    name, k = between[i]
                    chunk_tile(L, name, k, (yga_hi, yga_lo, 4, YGA) if name[0] == "b" else None)
                    if i + 1 < DIFF_HEADS * TB:
                        diff_scores(L, *divmod(i + 1, TB))
                    diff_turn(L, hd, qb)
                    if qb == TB - 1:
                        diff_out(L, hd)
                        head_ms(L, 4 + hd, 7)
                for hd in range(DIFF_HEADS):
                    head_rstd(L, 4 + hd, 4 + hd % 2)
                for name, n, _ in MIXER[30:36]:
                    for k in range(n):
                        chunk_tile(L, name, k, (yd_hi, yd_lo, 4, YD) if name[0] == "b" else None)
                for name, n, _ in MIXER[36:]:
                    for k in range(n):
                        chunk_tile(L, name, k, (mg_hi, mg_lo, 8, MG))

            pe.wait_ge(const_ready, 4)
            pe.wait_ge(c_loaded, 16)
            pe.transpose(bank[7][:, 0:KT], c_row[:, :], ident[0:KT, 0:KT]).then_inc(c_turned, 1)
            pe.wait_ge(x_loaded, 16)
            for m in range(6):
                for b in range(TB):
                    i = pe.transpose(bank[m][:, b * P:(b + 1) * P], x_tok[:, b, m * P:(m + 1) * P], ident[:, :])
                i.then_inc(x_turned, 1)
            pe.wait_ge(line_loaded, 32)
            for m in range(6, 8):
                pe.wait_ge(h_ready.sem, m - 5)
                for b in range(TB):
                    i = pe.transpose(bank[m - 6][:, b * P:(b + 1) * P], x_tok[:, b, m * P:(m + 1) * P], ident[:, :])
                i.then_inc(x_turned, 1)
            pe.matmul(bank[6][0:N_MAPS, :], rel33[:, :], onehot[:, 0:SEQ], start=True, stop=True).then_inc(line_made, 1)
            pe.wait_ge(cond_ready, 1)
            pe.matmul(bank[7][0:N_MAPS, 0:P], rel33[:, :], onehot[:, SEQ:LINE], start=True, stop=True).then_inc(line_made, 1)
            pe.wait_ge(line_copied, 2)

            with pe.Fori(0, DEPTH) as L:
                pe.wait_ge(h_ready.sem, h_ready.of(L, 0))
                pe.wait_ge(rows_loaded.sem, rows_loaded.of(L, 16 * ROW_DMAS))
                pe.transpose(bank[6][:, 0:72], rows_a[:, :], ident[0:72, 0:72])
                pe.transpose(bank[6][:, 72:V_LSTEP], rows_b[:, :], ident[0:V_LSTEP - 72, 0:V_LSTEP - 72]).then_inc(rows_turned.sem, 1)
                with pe.Fori(0, 9) as i:
                    for s in range(4):
                        a = i * 4 + s
                        pe.wait_ge(ada_step.sem, ada_step.of(L, (a + 1) * KT))
                        for t in range(2):
                            m = pe.matmul(bank[7][:, bass.ds(a * 2 + t, 1)], ada_acc[s % 2][:, t * P:(t + 1) * P],
                                          ones[:, 0:1], start=True, stop=True)
                        m.then_inc(ada_column.sem, 1)
                mean_square(L, 0)
                ffn(L, 0, 0)
                mean_square(L, 1)
                mean_square(L, 2)
                mixer(L)
                mean_square(L, 3)
                mean_square(L, 4)
                ffn(L, 1, C_FFN2)
                mean_square(L, 5)

            pe.wait_ge(h_ready.sem, h_ready.of(DEPTH, 0))
            for b in range(TB):
                for m in range(KT):
                    i = pe.transpose(bank[2 * b + m // 4][:, (m % 4) * P:(m % 4 + 1) * P], h[:, m, b * P:(b + 1) * P], ident[:, :])
                    if m % 4 == 3:
                        i.then_inc(out_turned, 1)

        @block.scalar
        def _(act):
            for s in range(2):
                act.sem_inc(hi_split[s].sem, 1)
            act.sem_inc(silu_done.sem, 2)

            def split(L, s, n, elems=CHUNK_ELEMS):
                act.wait_ge(raw_loaded[s].sem, raw_loaded[s].of(L, 16 * n))
                act.wait_ge(chunk_done[s].sem, chunk_done[s].of(L, n - 1))
                act.activation(w_hi[s][:, 0:elems], raw[s][:, 0:elems], ACT.Copy).then_inc(hi_split[s].sem, 1)

            def split_chunk(L, name):
                ch = CHUNK_OF[name]
                split(L, ch % 2, ch // 2 + 1, KT * P if chunk_widths(name) == P else CHUNK_ELEMS)

            def root(L, r):
                act.wait_ge(ms_ready.sem, ms_ready.of(L, r + 1))
                act.activation(sq_root[:, 0:TB], bank[0][:, 0:TB], ACT.Sqrt, bias=EPS_COL).then_inc(root_ready.sem, 1)

            def h_squares(L, ui):
                r = 2 * ui
                for m in range(KT):
                    act.wait_ge(h_ready.sem, h_ready.of(L, (ui - 1) * KT + m + 1))
                    act.wait_ge(sq_summed.sem, sq_summed.of(L, KT * r + m - 1))
                    act.activation(sq_buf[:, m % 2, :], h[:, m, :], ACT.Square).then_inc(sq_ready.sem, 1)
                root(L, r)

            def modulate(L, ui):
                for m in range(KT):
                    act.wait_ge(modulated.sem, modulated.of(L, ui * KT + m + 1))
                    act.activation(u_hi[:, m, :], mod_buf[:, m % 2, :], ACT.Identity,
                                   bias=ada[:, 24 * ui + m:24 * ui + m + 1]).then_inc(u_hi_ready.sem, 1)

            def y_tile(L, ui, m, bk, wait):
                r = 2 * ui + 1
                wait()
                act.activation(y_sub[:, m, :], bank[bk][:, :], ACT.Copy).then_inc(y_copied.sem, 1)
                act.wait_ge(sq_summed.sem, sq_summed.of(L, KT * r + m - 1))
                act.activation(sq_buf[:, m % 2, :], bank[bk][:, :], ACT.Square).then_inc(sq_ready.sem, 1)

            def ffn(L, f, c0):
                i0 = f * FT
                split(L, c0 % 2, c0 // 2 + 1)
                with act.Fori(0, FT // 2) as j:
                    split(L, (c0 + 1) % 2, (c0 + 1) // 2 + j + 1)
                    split(L, c0 % 2, (c0 + 2) // 2 + j + 1)
                    for mt in range(2):
                        i = i0 + 2 * j + mt
                        if mt:
                            s = c0 % 2
                            act.wait_ge(chunk_done[s].sem, chunk_done[s].of(L, c0 // 2 + j + 1))
                        else:
                            act.wait_ge(tile_ready.sem, tile_ready.of(L, f * READY_BEFORE_FFN2 + 2 * j + 1))
                        act.wait_ge(g_lo_ready.sem, g_lo_ready.of(L, i - 1))
                        act.activation(silu_buf[:, mt, :], bank[mt][:, :], ACT.Silu).then_inc(silu_done.sem, 1)
                    for mt in range(2):
                        i = i0 + 2 * j + mt
                        act.wait_ge(prod_done.sem, prod_done.of(L, i + 1))
                        act.activation(flat(g_hi[:, cols(j * 2 + mt), :]), silu_buf[:, mt, :], ACT.Copy).then_inc(g_hi_ready.sem, 1)
                c1 = c0 + FT
                with act.Fori(0, FT // 4) as j:
                    for half in range(2):
                        cc = c1 + 1 + half
                        split(L, cc % 2, cc // 2 + j + 1)
                s = (c1 + FT // 2 - 1) % 2
                for m in range(KT):
                    def wait():
                        if m < KT - 1:
                            act.wait_ge(tile_ready.sem, tile_ready.of(L, f * READY_BEFORE_FFN2 + FT + m + 1))
                        else:
                            act.wait_ge(chunk_done[s].sem, slot_value(chunk_done[s], L, c1 + FT // 2 - 1))
                    y_tile(L, 2 * f, m, m, wait)
                root(L, 4 * f + 1)

            def tile_wait(L, name, k):
                t = TILES[name, k]
                if t.last:
                    s = t.chunk % 2
                    act.wait_ge(chunk_done[s].sem, slot_value(chunk_done[s], L, t.chunk))
                else:
                    act.wait_ge(tile_ready.sem, tile_ready.of(L, t.ready))
                return bank[t.bank]

            def empty(L, name, k):
                b = tile_wait(L, name, k)
                i = int(name[-1]) if name[-1].isdigit() else 0
                kind = name[:2]
                if kind == "su":
                    q = k if i == 0 else i + 1
                    ins = act.activation(su[:, q, :], b[:, :], ACT.Copy)
                elif kind in ("gq", "gk"):
                    ins = act.activation((gq if kind == "gq" else gk)[:, k, :], b[:, :], ACT.Copy)
                elif kind == "ga":
                    ins = act.activation(a_low[:, :], b[0:LOWRANK, :], ACT.Copy)
                elif kind in ("gv", "dv"):
                    dst = (gv if kind == "gv" else dv)[:, 2 * k:2 * k + 2, i * 256:(i + 1) * 256]
                    ins = act.activation(dst, b[:, :].rearrange("p (a n) -> p a n", a=2), ACT.Copy)
                elif kind == "gr":
                    ins = act.activation(gr[:, 2 * i + k, :], b[:, :], ACT.Silu)
                elif kind == "gs":
                    ins = act.activation(merged[:, 2 * i + k, :], b[:, :], ACT.Sigmoid)
                elif kind == "gl":
                    ins = act.activation(z_gate[:, k, :], b[:, :], ACT.Sigmoid, bias=vec[:, V_BGLU + 4 + k:V_BGLU + 5 + k])
                elif kind == "dq":
                    ins = act.activation(dq[:, 2 * i + k, :], b[:, :], ACT.Copy, scale=0.125)
                elif kind == "dk":
                    ins = act.activation(dk[:, 2 * i + k, :], b[:, :], ACT.Copy)
                else:
                    t4 = (2 * i + k) % 4
                    n = {"gg": 0, "gd": 8}[kind] + (2 * i + k)
                    if n >= 4:
                        act.wait_ge(merged_ready.sem, merged_ready.of(L, n - 3))
                    ins = act.activation(sig[:, t4, :], b[:, :], ACT.Sigmoid)
                ins.then_inc(emptied["act"].sem, 1)

            def make_tables(L, j):
                act.wait_ge(turns_ready.sem, turns_ready.of(L, j + 1))
                if j >= 3:
                    act.wait_ge(back_done.sem, back_done.of(L, j - 2))
                act.activation(tab_s[:, j % 3, :], turns[:, j % 2, :], ACT.Sin, scale=6.283185)
                st.did(act.activation(turns[:, j % 2, :], turns[:, j % 2, :], ACT.Abs))
                st.wait()
                act.activation(tab_c[:, j % 3, :], turns[:, j % 2, :], ACT.Sin, scale=-6.283185, bias=HALF_PI)\
                   .then_inc(tables_ready.sem, 1)

            def split_tile(L, base, k, dst, src):
                act.activation(dst[:, k, :], src, ACT.Copy).then_inc(split_hi.sem, 1)

            def head_squares(L, hh, bk):
                act.wait_ge(o_ready.sem, o_ready.of(L, hh + 1))
                dst = o_head[hh][:, :] if hh < 4 else dq[:, hh - 4, :]
                act.activation(dst, bank[bk][:, :], ACT.Copy).then_inc(o_copied.sem, 1)
                if hh:
                    act.wait_ge(o_ms.sem, o_ms.of(L, hh))
                act.activation(o_sq[:, :], bank[bk][:, :], ACT.Square).then_inc(o_squared.sem, 1)

            def head_roots(L, g):
                act.wait_ge(o_ms_kept.sem, o_ms_kept.of(L, 4 * g + 4))
                act.activation(sq_root[:, 0:16], ms_heads[:, :], ACT.Sqrt, bias=EPS_COL).then_inc(o_roots.sem, 1)

            def diff_exp(L, i):
                hd, qb = divmod(i, TB)
                n = (qb + 1) * P
                act.wait_ge(max_ready.sem, max_ready.of(L, i + 1))
                sm = smax[:, i % 2, :]
                for par in range(2):
                    ins = act.activation(prob[i % 2][:, par, 0:n], prob[i % 2][:, par, 0:n], ACT.Exp, bias=sm[:, 2 + par:3 + par],
                                         accum_out=sm[:, 4 + par:5 + par])
                    st.did(ins) if par == 0 else ins.then_inc(prob_ready.sem, 1)
                st.wait()

            def diff_copy(L, i):
                hd, qb = divmod(i, TB)
                act.wait_ge(at_ready.sem, at_ready.of(L, i + 1))
                if qb == 0 and hd:
                    act.wait_ge(o_ready.sem, o_ready.of(L, 4 + hd))
                act.activation(a_t[:, 0:qb + 1, qb * P:(qb + 1) * P],
                               bank[6][:, 0:(qb + 1) * P].rearrange("p (a n) -> p a n", n=P), ACT.Copy).then_inc(at_copied.sem, 1)

            act.wait_ge(c_turned, 1)
            act.activation(cond[:, :], bank[7][:, 0:KT], ACT.Silu).then_inc(cond_ready, 1)
            act.wait_ge(line_made, 2)
            act.activation(bias_line[:, 0:SEQ], bank[6][0:N_MAPS, :], ACT.Copy).then_inc(line_copied, 1)
            act.activation(bias_line[:, SEQ:LINE], bank[7][0:N_MAPS, 0:P], ACT.Copy).then_inc(line_copied, 1)

            with act.Fori(0, DEPTH) as L:
                st = Steps(act, scalar_steps, L)
                act.wait_ge(theta_ready.sem, theta_ready.of(L, 1))
                act.activation(pscr[:, 8, :], pscr[:, 3, :], ACT.Sin).then_inc(sines_ready.sem, 1)
                act.activation(pscr[:, 9, :], pscr[:, 3, :], ACT.Sin, scale=0.5).then_inc(sines_ready.sem, 1)
                act.wait_ge(lam_sums.sem, lam_sums.of(L, 2))
                act.activation(small[:, 42:44], small[:, 40:42], ACT.Exp).then_inc(lam_exps.sem, 1)
                h_squares(L, 0)
                modulate(L, 0)
                ffn(L, 0, 0)
                h_squares(L, 1)
                modulate(L, 1)
                split_chunk(L, "su0")
                for i in range(3):
                    split_chunk(L, MIXER[i + 1][0])
                    for k in range(MIXER[i][1]):
                        empty(L, MIXER[i][0], k)
                make_tables(L, 0)
                make_tables(L, 1)
                done = 0
                gaps = 0
                for i in range(3, 14):
                    name, n, _ = MIXER[i]
                    split_chunk(L, MIXER[i + 1][0])
                    for k in range(n):
                        empty(L, name, k)
                        gaps += 1
                        while done < min(S5_PAIRS, (gaps * S5_PAIRS) // 20):
                            if done + 2 < S5_PAIRS:
                                make_tables(L, done + 2)
                            done += 1
                split_chunk(L, "glu0")
                for q in range(4):
                    act.wait_ge(s5_y_summed.sem, s5_y_summed.of(L, q + 1))
                    act.activation(su[:, q, :], su[:, q, :], ACT.Gelu_apprx_tanh).then_inc(gelu_done.sem, 1)
                for q in range(4):
                    act.wait_ge(gelu_done.sem, gelu_done.of(L, q + 1))
                    split_tile(L, YG, q, yg_hi, su[:, q, :])
                for k in range(4):
                    act.wait_ge(split_lo.sem, split_lo.of(L, YG + k + 1))
                    empty(L, "glu1", k)
                split_chunk(L, "bs0")
                for q in range(4):
                    act.wait_ge(emptied["vec"].sem, emptied["vec"].of(L, TILES["glu0", q].emptied))
                    split_tile(L, YS, q, ys_hi, z_gate[:, q, :])
                split_chunk(L, "bs1")
                for t in range(2):
                    act.wait_ge(alpha_read.sem, alpha_read.of(L, t + 1))
                    st.did(act.activation(la[:, t, :], bank[4 + t][:, :], ACT.Abs, bias=vec[:, V_BALPHA + t:V_BALPHA + t + 1]))
                    st.wait()
                for t in range(2):
                    st.did(act.activation(la[:, t, :], la[:, t, :], ACT.Exp, scale=-1.0))
                    st.wait()
                    act.activation(la[:, t, :], la[:, t, :], ACT.Ln, bias=1.0).then_inc(alpha_exps.sem, 1)
                split_chunk(L, "dq0")
                split_chunk(L, "dq1")
                for t in range(2):
                    act.wait_ge(decay_sum.sem, decay_sum.of(L, t + 1))
                    act.activation(eb[:, t, :], lb[:, t, :], ACT.Exp, scale=1.0 / GLA_TAU).then_inc(gla_exps.sem, 1)
                    act.activation(la[:, t, :], lb[:, t, :], ACT.Exp, scale=-1.0 / GLA_TAU).then_inc(gla_exps.sem, 1)
                for t in range(2):
                    act.wait_ge(decay_last.sem, decay_last.of(L, t + 1))
                    act.activation(lb[:, t, :], lb[:, t, :], ACT.Exp, scale=1.0 / GLA_TAU).then_inc(gla_exps.sem, 1)
                for k in range(2):
                    empty(L, "dq0", k)
                split_chunk(L, "dk0")
                for k in range(2):
                    empty(L, "dq1", k)
                act.wait_ge(kk_turned.sem, kk_turned.of(L, 1))
                for i in range(2):
                    act.activation(kk_tok[:, 2 * i:2 * i + 2, :], bank[4 + i][:, :].rearrange("p (a n) -> p a n", a=2),
                                   ACT.Copy).then_inc(kk_copied.sem, 1)
                split_chunk(L, "dk1")
                for k in range(2):
                    empty(L, "dk0", k)
                split_chunk(L, "dv0")
                for k in range(2):
                    empty(L, "dk1", k)
                split_chunk(L, "dv1")
                empty(L, "dv0", 0)
                for hd in range(GLA_HEADS):
                    head_squares(L, hd, 6 + hd % 2)
                    if hd < 3:
                        empty(L, *(("dv0", 1), ("dv1", 0), ("dv1", 1))[hd])
                    if hd == 1:
                        split_chunk(L, "gg0")
                head_roots(L, 0)
                split_chunk(L, "gg1")
                act.wait_ge(yga_done.sem, yga_done.of(L, 4))
                for k in range(4):
                    split_tile(L, YGA, k, yga_hi, gr[:, k, :])
                between = [("gg0", 0), ("gg0", 1), ("gg1", 0), ("gg1", 1), None, None, None, None,
                           ("gg2", 0), ("gg2", 1), ("gg3", 0), ("gg3", 1), None, None, None, None]
                splits = {2: "bg0", 4: "gg2", 8: "gg3", 10: "bg1", 12: "gd0"}
                diff_exp(L, 0)
                for i in range(DIFF_HEADS * TB):
                    hd, qb = divmod(i, TB)
                    if i in splits:
                        split_chunk(L, splits[i])
                    if between[i]:
                        empty(L, *between[i])
                    if i + 1 < DIFF_HEADS * TB:
                        diff_exp(L, i + 1)
                    diff_copy(L, i)
                    if qb == TB - 1:
                        head_squares(L, 4 + hd, 7)
                head_roots(L, 1)
                split_chunk(L, "gd1")
                for k in range(2):
                    empty(L, "gd0", k)
                split_chunk(L, "bd0")
                for k in range(2):
                    empty(L, "gd1", k)
                for k in range(4):
                    act.wait_ge(o_normed.sem, o_normed.of(L, 4 + k + 1))
                    if k == 0:
                        t = TILES["bg1", 3]
                        act.wait_ge(chunk_done[t.chunk % 2].sem, slot_value(chunk_done[t.chunk % 2], L, t.chunk))
                    split_tile(L, YD, k, yd_hi, dq[:, k, :])
                split_chunk(L, "gd2")
                split_chunk(L, "gd3")
                for k in range(2):
                    empty(L, "gd2", k)
                split_chunk(L, "bd1")
                for k in range(2):
                    empty(L, "gd3", k)
                split_chunk(L, "wo0")
                for m in range(KT):
                    act.wait_ge(merged_ready.sem, merged_ready.of(L, 8 + m + 1))
                    if m == 0:
                        act.wait_ge(split_lo.sem, split_lo.of(L, YD + 4))
                    split_tile(L, MG, m, mg_hi, merged[:, m, :])
                split_chunk(L, "wo1")
                for i in range(4):
                    if i >= 1 and i + 1 < 4:
                        split_chunk(L, f"wo{i + 1}")
                    for k in range(2):
                        t = TILES[f"wo{i}", k]
                        y_tile(L, 1, 2 * i + k, t.bank, lambda: tile_wait(L, f"wo{i}", k))
                root(L, 3)
                h_squares(L, 2)
                modulate(L, 2)
                ffn(L, 1, C_FFN2)
                assert st.n == SCALAR_STEPS, st.n

            for b in range(TB):
                act.wait_ge(out_turned, 2 * b + 1)
                act.activation(x_tok[:, b, 0:SEQ], bank[2 * b][:, :], ACT.Copy).then_inc(out_half, 1)

        @block.vector
        def _(v):
            for s in range(2):
                v.sem_inc(lo_split[s].sem, 1)
            v.sem_inc(prod_done.sem, 2)
            v.sem_inc(g_lo_ready.sem, 2)
            v.sem_inc(ada_step.sem, 4 * KT)

            def stt(o, a, s, b, op0, op1):
                return v.scalar_tensor_tensor(out=o, in0=a, scalar=s, in1=b, op0=op0, op1=op1)

            MUL, ADD, SUB = ALU.mult, ALU.add, ALU.subtract

            def split(L, s, n):
                v.wait_ge(hi_split[s].sem, hi_split[s].of(L, n))
                v.tensor_tensor(w_lo[s][:, :], raw[s][:, :], w_hi[s][:, :].bitcast(F32), SUB).then_inc(lo_split[s].sem, 1)

            def rstd(L, r):
                v.wait_ge(root_ready.sem, root_ready.of(L, r + 1))
                st.did(v.reciprocal(rstd_tok[:, 0:TB], sq_root[:, 0:TB]))
                st.wait()
                v.tensor_tensor(diag[:, :, :], ident[:, :].unsqueeze(1).to_broadcast([P, TB, P]),
                                rstd_tok[:, 0:TB].unsqueeze(2).to_broadcast([P, TB, P]), MUL).then_inc(diag_ready.sem, 1)
                v.wait_ge(rstd_ready.sem, rstd_ready.of(L, r + 1))

            def modulate(L, ui):
                rstd(L, 2 * ui)
                for m in range(KT + 1):
                    if m < KT:
                        if m >= 2:
                            v.wait_ge(u_ready.sem, u_ready.of(L, ui * KT + m - 1))
                        stt(mod_buf[:, m % 2, :], h[:, m, :], pre_gain[:, KT * ui + m:KT * ui + m + 1], bank[1][:, :],
                            MUL, MUL).then_inc(modulated.sem, 1)
                    if m:
                        i = m - 1
                        v.wait_ge(u_hi_ready.sem, u_hi_ready.of(L, ui * KT + i + 1))
                        stt(u_lo[:, i, :], mod_buf[:, i % 2, :], ada[:, 24 * ui + i:24 * ui + i + 1],
                            u_hi[:, i, :].bitcast(F32), ADD, SUB).then_inc(u_ready.sem, 1)

            def post(L, ui):
                rstd(L, 2 * ui + 1)
                for m in range(KT + 1):
                    if m < KT:
                        v.wait_ge(y_copied.sem, y_copied.of(L, ui * KT + m + 1))
                        st.did(stt(y_sub[:, m, :], y_sub[:, m, :], post_gain[:, KT * ui + m:KT * ui + m + 1], bank[1][:, :], MUL, MUL))
                    if m:
                        st.wait(back=1 if m < KT else 0)
                        v.tensor_tensor(h[:, m - 1, :], h[:, m - 1, :], y_sub[:, m - 1, :], ADD).then_inc(h_ready.sem, 1)

            def ffn(L, f, c0):
                i0 = f * FT
                split(L, c0 % 2, c0 // 2 + 1)
                with v.Fori(0, FT // 2) as j:
                    split(L, (c0 + 1) % 2, (c0 + 1) // 2 + j + 1)
                    split(L, c0 % 2, (c0 + 2) // 2 + j + 1)
                    for mt in range(2):
                        i = i0 + 2 * j + mt
                        v.wait_ge(silu_done.sem, silu_done.of(L, i + 1))
                        if mt:
                            s = (c0 + 1) % 2
                            v.wait_ge(chunk_done[s].sem, chunk_done[s].of(L, (c0 + 1) // 2 + j + 1))
                        else:
                            v.wait_ge(tile_ready.sem, tile_ready.of(L, f * READY_BEFORE_FFN2 + 2 * j + 2))
                        v.tensor_tensor(silu_buf[:, mt, :], silu_buf[:, mt, :], bank[2 + mt][:, :], MUL).then_inc(prod_done.sem, 1)
                    for mt in range(2):
                        i = i0 + 2 * j + mt
                        v.wait_ge(g_hi_ready.sem, g_hi_ready.of(L, i + 1))
                        v.tensor_tensor(flat(g_lo[:, cols(j * 2 + mt), :]), silu_buf[:, mt, :],
                                        flat(g_hi[:, cols(j * 2 + mt), :]).bitcast(F32), SUB).then_inc(g_lo_ready.sem, 1)
                c1 = c0 + FT
                with v.Fori(0, FT // 4) as j:
                    for half in range(2):
                        cc = c1 + 1 + half
                        split(L, cc % 2, cc // 2 + j + 1)

            def tile_wait(L, name, k):
                t = TILES[name, k]
                if t.last:
                    s = t.chunk % 2
                    v.wait_ge(chunk_done[s].sem, slot_value(chunk_done[s], L, t.chunk))
                else:
                    v.wait_ge(tile_ready.sem, tile_ready.of(L, t.ready))
                return bank[t.bank]

            def layer_vectors(L):
                v.wait_ge(rows_turned.sem, rows_turned.of(L, 1))
                v.tensor_copy(vec[:, 0:V_LSTEP], bank[6][:, 0:V_LSTEP]).then_inc(vec_ready.sem, 1)
                v.wait_ge(s5w_loaded.sem, s5w_loaded.of(L, 32))
                for g in range(2):
                    rows = slice(64 * g, 64 * g + 64)
                    st.did(v.tensor_copy(vec[rows, V_LSTEP:V_END], log_steps[rows, :].rearrange("p (j g) -> p j g", g=2)[:, :, g]))
                st.wait()
                v.wait_ge(vec_ready.sem, vec_ready.of(L, 1))
                lre, lim, lst = vec[:, V_LRE:V_LIM], vec[:, V_LIM:V_LSTEP], vec[:, V_LSTEP:V_END]
                R = [pscr[:, i, :] for i in range(12)]

                def do(ins):
                    st.did(ins)
                    st.wait()

                def ts(o, a, s1, s2, op0, op1):
                    do(v.tensor_scalar(o, a, s1, s2, op0, op1))

                def stv(o, a, s, b, op0, op1):
                    do(stt(o, a, s, b, op0, op1))

                def tt(o, a, b, op):
                    do(v.tensor_tensor(o, a, b, op))

                ts(R[0], lst, 1.0 / math.log(2.0), MAGIC, MUL, ADD)
                ts(R[0], R[0], -MAGIC, None, ADD, ALU.bypass)
                stv(R[1], R[0], -LN2_A, lst, MUL, ADD)
                stv(R[1], R[0], -LN2_B, R[1], MUL, ADD)
                ts(R[2], R[1], 1.0 / 5040, None, MUL, ALU.bypass)
                for d in (720, 120, 24, 6, 2, 1):
                    stv(R[2], R[2], 1.0 / d, R[1], ADD, MUL)
                ts(R[2], R[2], 1.0, None, ADD, ALU.bypass)
                ts(R[0], R[0], 127.0, 1.0, ADD, ALU.max)
                do(v.tensor_scalar(pint[:, :], R[0], 254.0, 8388608.0, ALU.min, MUL))
                tt(R[2], R[2], pint[:, :].bitcast(F32), MUL)
                tt(R[3], lim, R[2], MUL)
                ts(R[0], R[3], 1.0 / TWO_PI, MAGIC, MUL, ADD)
                ts(R[0], R[0], -MAGIC, None, ADD, ALU.bypass)
                for part in (TWO_PI_A, TWO_PI_B, TWO_PI_C):
                    stv(R[3], R[0], -part, R[3], MUL, ADD)
                v.tensor_scalar(R[3], R[3], 3.1415925, -3.1415925, ALU.min, ALU.max).then_inc(theta_ready.sem, 1)
                v.wait_ge(theta_ready.sem, theta_ready.of(L, 1))
                ts(phase, R[3], 1.0 / TWO_PI, None, MUL, ALU.bypass)
                tt(R[4], lre, R[2], MUL)
                ts(R[4], R[4], 1.0 / 1024, -1.0, MUL, ALU.max)
                ts(R[5], R[4], 1.0 / 24, None, MUL, ALU.bypass)
                for d in (6, 2, 1):
                    stv(R[5], R[5], 1.0 / d, R[4], ADD, MUL)
                for _ in range(10):
                    stv(R[5], R[5], 2.0, R[5], ADD, MUL)
                ts(mag, R[5], 1.0, None, ADD, ALU.bypass)
                v.wait_ge(sines_ready.sem, sines_ready.of(L, 2))
                stv(R[6], R[9], -2.0, R[9], MUL, MUL)
                stv(R[7], R[6], 1.0, R[5], ADD, MUL)
                tt(R[7], R[7], R[6], ADD)
                tt(R[8], mag, R[8], MUL)
                tt(R[10], lre, lre, MUL)
                tt(R[11], lim, lim, MUL)
                tt(R[10], R[10], R[11], ADD)
                do(v.reciprocal(R[10], R[10]))
                tt(f_re, R[7], lre, MUL)
                tt(R[11], R[8], lim, MUL)
                tt(f_re, f_re, R[11], ADD)
                tt(f_re, f_re, R[10], MUL)
                tt(f_im, R[8], lre, MUL)
                tt(R[11], R[7], lim, MUL)
                tt(f_im, f_im, R[11], SUB)
                tt(f_im, f_im, R[10], MUL)
                for i in range(2):
                    if i:
                        v.wait_ge(lam_sums.sem, lam_sums.of(L, 1))
                    v.tensor_tensor_reduce(lam_prod[:, :], lam_rows[:, 2 * i, :], lam_rows[:, 2 * i + 1, :], 1.0, 0.0, MUL, ADD,
                                           small[:, 40 + i:41 + i]).then_inc(lam_sums.sem, 1)
                v.wait_ge(lam_exps.sem, lam_exps.of(L, 1))
                stv(small[:, 44:45], small[:, 42:43], -1.0, small[:, 43:44], MUL, ADD)
                tt(neg_lam, small[:, 44:45], lam_tab[:, cols(L)], SUB)
                st.did(v.tensor_scalar(gd_gain[:, :], vec[:, V_DNORM:V_SD], lam_tab[:, cols(L + DEPTH)], None, MUL, ALU.bypass))

            def layer_ada(L):
                with v.Fori(0, 9) as i:
                    for s in range(4):
                        a = i * 4 + s
                        v.wait_ge(ada_loaded[s].sem, ada_loaded[s].of(L, i * 16 + 16))
                        v.wait_ge(ada_column.sem, ada_column.of(L, a - 1))
                        acc = ada_acc[s % 2][:, :]
                        for k in range(KT):
                            w = ada_w[s][:, k, :]
                            if k == 0:
                                ins = v.tensor_scalar(acc, w, cond[:, 0:1], None, MUL, ALU.bypass)
                            else:
                                v.wait_ge(ada_step.sem, ada_step.of(L, a * KT + k))
                                ins = stt(acc, w, cond[:, k:k + 1], acc, MUL, ADD)
                            ins.then_inc(ada_step.sem, 1)
                v.wait_ge(ada_column.sem, ada_column.of(L, 36))
                st.did(v.tensor_tensor(ada[:, :], bank[7][:, 0:72], vec[:, 0:72], ADD))
                st.wait()
                for ui in range(3):
                    k8 = slice(KT * ui, KT * ui + KT)
                    st.did(stt(pre_gain[:, k8], ada[:, 24 * ui + 8:24 * ui + 16], 1.0, vec[:, V_PRE + KT * ui:V_PRE + KT * ui + KT], ADD, MUL))
                    st.did(stt(post_gain[:, k8], ada[:, 24 * ui + 16:24 * ui + 24], 1.0 if ui == 1 else 0.5,
                               vec[:, V_POST + KT * ui:V_POST + KT * ui + KT], MUL, MUL))
                st.wait()

            def s5_matrices(L):
                b, t = s5_b, s5_t

                def bc(f):
                    return f.unsqueeze(2).to_broadcast([P, S5_PAIRS, S5_CH])

                v.wait_ge(s5w_loaded.sem, s5w_loaded.of(L, 16 * 8))
                st.did(v.tensor_tensor(t[:, 0], b[:, 1], bc(f_im), MUL))
                st.did(v.tensor_tensor(t[:, 1], b[:, 0], bc(f_im), MUL))
                st.wait()
                st.did(v.tensor_tensor(b[:, 0], b[:, 0], bc(f_re), MUL))
                st.did(v.tensor_tensor(b[:, 1], b[:, 1], bc(f_re), MUL))
                st.wait()
                v.wait_ge(s5_bx_zero.sem, s5_bx_zero.of(L, 1))
                for g in range(2):
                    rows = slice(64 * g, 64 * g + 64)
                    for part in range(2):
                        dst = s5_bx[rows, part, :, :, g, :].rearrange("p q i h -> p (q i) h")
                        ins = v.tensor_tensor(dst, b[rows, part], t[rows, part], ADD if part else SUB)
                        if g == 0 or part == 0:
                            st.did(ins)
                st.wait()
                ins.then_inc(s5_bx_ready.sem, 1)
                v.wait_ge(s5_turned.sem, s5_turned.of(L, 1))
                for part in range(2):
                    st.did(v.tensor_copy(flat(s5_bt[:, part]), bank[4 + part][:, :]))
                v.wait_ge(s5_turned.sem, s5_turned.of(L, 2))
                v.wait_ge(s5_mask_ready.sem, s5_mask_ready.of(L, 3))
                mask = s5_mask[:, :, :, :].rearrange("p a g n -> p (a g n)").unsqueeze(1).to_broadcast([P, 4, P])
                for part in range(2):
                    ins = stt(s5_ct[:, part], bank[6 + part][:, :].rearrange("p (q n) -> p q n", q=4), -1.0 if part else 1.0,
                              mask, MUL, MUL)
                    if part == 0:
                        st.did(ins)
                st.wait()
                ins.then_inc(s5_mats_ready.sem, 1)

            def s5_turns(L, j):
                ph = phase[:, j:j + 1]
                if j >= 1:
                    v.wait_ge(turns_ready.sem, turns_ready.of(L, j))
                st.did(v.tensor_scalar(rounded[:, :], time_row[:, :], ph, MAGIC, MUL, ADD))
                st.wait()
                st.did(v.tensor_scalar(rounded[:, :], rounded[:, :], -MAGIC, None, ADD, ALU.bypass))
                st.wait()
                if j >= 2:
                    v.wait_ge(tables_ready.sem, tables_ready.of(L, j - 1))
                stt(turns[:, j % 2, :], time_row[:, :], ph, rounded[:, :], MUL, SUB).then_inc(turns_ready.sem, 1)

            def s5_front(L, j):
                r = [rot[:, j % 2, i, :] for i in range(4)]
                cs, sn = tab_c[:, j % 3, :], tab_s[:, j % 3, :]
                v.wait_ge(bu_ready.sem, bu_ready.of(L, j + 1))
                v.wait_ge(tables_ready.sem, tables_ready.of(L, j + 1))
                if j >= 2:
                    v.wait_ge(s5_y_ready.sem, s5_y_ready.of(L, j - 1))
                st.did(v.tensor_tensor(r[0], bank[4][:, :], cs, MUL))
                st.did(v.tensor_tensor(r[1], bank[5][:, :], sn, MUL))
                st.did(v.tensor_tensor(r[2], bank[5][:, :], cs, MUL))
                st.wait()
                v.tensor_tensor(r[3], bank[4][:, :], sn, MUL).then_inc(front_done.sem, 1)

            def s5_back(L, j):
                r = [rot[:, j % 2, i, :] for i in range(4)]
                cs, sn = tab_c[:, j % 3, :], tab_s[:, j % 3, :]
                m = mag[:, j:j + 1].to_broadcast([P, SEQ])
                v.wait_ge(z_in_ready.sem, z_in_ready.of(L, 2 * j + 2))
                st.did(v.tensor_tensor_scan(r[1], m, r[0], 0.0, MUL, ADD))
                st.did(v.tensor_tensor_scan(r[3], m, r[2], 0.0, MUL, ADD))
                st.wait()
                st.did(v.tensor_tensor(r[0], r[1], cs, MUL))
                st.did(v.tensor_tensor(r[2], r[3], sn, MUL))
                st.wait()
                st.did(v.tensor_tensor(r[1], r[1], sn, MUL))
                st.wait()
                v.tensor_tensor(r[3], r[3], cs, MUL).then_inc(back_done.sem, 1)

            def s5_y(L, q):
                v.wait_ge(s5_y_ready.sem, s5_y_ready.of(L, 4 * q + 4))
                stt(su[:, q, :], su[:, q, :], vec[:, V_SD + q:V_SD + q + 1], bank[6 + q % 2][:, :], MUL, ADD)\
                    .then_inc(s5_y_summed.sem, 1)

            def split_tile(L, base, k, lo, hi, src):
                v.wait_ge(split_hi.sem, split_hi.of(L, base + k + 1))
                v.tensor_tensor(lo[:, k, :], src, hi[:, k, :].bitcast(F32), SUB).then_inc(split_lo.sem, 1)

            def head_keep(L, hh, bk):
                v.wait_ge(o_ms.sem, o_ms.of(L, hh + 1))
                v.tensor_copy(ms_heads[:, (hh % 4) * 4:(hh % 4) * 4 + 4], bank[bk][:, 0:TB]).then_inc(o_ms_kept.sem, 1)

            def heads_norm(L, g):
                v.wait_ge(o_roots.sem, o_roots.of(L, g + 1))
                st.did(v.reciprocal(rstd_tok[:, :], sq_root[:, :]))
                st.wait()
                for hd in range(4):
                    hh = 4 * g + hd
                    if hd:
                        v.wait_ge(o_rstd.sem, o_rstd.of(L, hh))
                    v.tensor_tensor(head_diag[g][:, :].rearrange("p (a n) -> p a n", a=TB),
                                    ident[:, :].unsqueeze(1).to_broadcast([P, TB, P]),
                                    rstd_tok[:, 4 * hd:4 * hd + 4].unsqueeze(2).to_broadcast([P, TB, P]), MUL)\
                     .then_inc(o_diag.sem, 1)
                    v.wait_ge(o_rstd.sem, o_rstd.of(L, hh + 1))
                    bk = bank[4 + hd % 2]
                    if g == 0:
                        stt(o_head[hd][:, :], o_head[hd][:, :], vec[:, V_GNORM + hd:V_GNORM + hd + 1], bk[:, :], MUL, MUL)\
                            .then_inc(o_normed.sem, 1)
                        v.wait_ge(o_normed.sem, o_normed.of(L, hh + 1))
                        v.tensor_tensor(gr[:, hd, :], gr[:, hd, :], o_head[hd][:, :], MUL).then_inc(yga_done.sem, 1)
                    else:
                        stt(dq[:, hd, :], dq[:, hd, :], gd_gain[:, hd:hd + 1], bk[:, :], MUL, MUL).then_inc(o_normed.sem, 1)

            def branch_tile(L, name, k, n):
                b = tile_wait(L, name, k)
                m = n % 8
                gate = TILES[f"g{name[1]}{m // 2}", m % 2]
                v.wait_ge(emptied["act"].sem, emptied["act"].of(L, gate.emptied))
                v.tensor_tensor(sig[:, n % 4, :], sig[:, n % 4, :], b[:, :], MUL).then_inc(emptied["vec"].sem, 1)
                v.wait_ge(emptied["vec"].sem, emptied["vec"].of(L, TILES[name, k].emptied))
                if n >= 8:
                    v.wait_ge(merged_ready.sem, merged_ready.of(L, n - 7))
                v.tensor_tensor(merged[:, m, :], merged[:, m, :], sig[:, n % 4, :], ADD).then_inc(merged_ready.sem, 1)

            def diff_max(L, i):
                hd, qb = divmod(i, TB)
                n = (qb + 1) * P
                sm = smax[:, i % 2, :]
                if i >= 2:
                    v.wait_ge(at_ready.sem, at_ready.of(L, i - 1))
                v.wait_ge(scores_ready.sem, scores_ready.of(L, 2 * i + 2))
                v.sem_inc(scores_seen.sem, 1)
                for par in range(2):
                    st.did(v.tensor_tensor_reduce(prob[i % 2][:, par, 0:n], bank[4 + par][:, 0:n],
                                                  bias_tab[:, 2 * hd + par, SEQ - n:SEQ], 1.0, -3.4e38, ADD, ALU.max,
                                                  sm[:, par:par + 1]))
                st.wait()
                v.tensor_scalar(sm[:, 2:4], sm[:, 0:2], -1.0, None, MUL, ALU.bypass).then_inc(max_ready.sem, 1)

            def diff_mix(L, i):
                hd, qb = divmod(i, TB)
                n = (qb + 1) * P
                sm = smax[:, i % 2, :]
                pr = prob[i % 2]
                v.wait_ge(prob_ready.sem, prob_ready.of(L, i + 1))
                st.did(v.reciprocal(sm[:, 6:8], sm[:, 4:6]))
                st.wait()
                st.did(v.tensor_tensor(sm[:, 7:8], sm[:, 7:8], neg_lam, MUL))
                st.did(v.tensor_scalar(pr[:, 0, 0:n], pr[:, 0, 0:n], sm[:, 6:7], None, MUL, ALU.bypass))
                st.wait()
                stt(pr[:, 0, 0:n], pr[:, 1, 0:n], sm[:, 7:8], pr[:, 0, 0:n], MUL, ADD).then_inc(mix_ready.sem, 1)

            v.memset(rel33[NUM_BUCKETS:NUM_BUCKETS + 1, :], MASKED).then_inc(const_ready, 1)
            for m in range(KT):
                v.wait_ge(x_turned, m + 1)
                v.tensor_copy(h[:, m, :], bank[m if m < 6 else m - 6][:, :]).then_inc(h_ready.sem, 1)

            v.wait_ge(const_ready, 4)
            with v.Fori(0, DEPTH) as L:
                st = Steps(v, vector_steps, L)
                v.wait_ge(line_copied, 2)
                layer_vectors(L)
                layer_ada(L)
                modulate(L, 0)
                ffn(L, 0, 0)
                post(L, 0)
                modulate(L, 1)
                s5_matrices(L)
                s5_turns(L, 0)
                s5_turns(L, 1)
                s5_front(L, 0)
                for j in range(S5_PAIRS):
                    if j + 2 < S5_PAIRS:
                        s5_turns(L, j + 2)
                    if j + 1 < S5_PAIRS:
                        s5_front(L, j + 1)
                    s5_back(L, j)
                    if j >= 4 and j % 4 == 1:
                        s5_y(L, j // 4 - 1)
                s5_y(L, 3)
                for q in range(4):
                    v.wait_ge(gelu_done.sem, gelu_done.of(L, q + 1))
                    split_tile(L, YG, q, yg_lo, yg_hi, su[:, q, :])
                for k in range(4):
                    b = tile_wait(L, "glu0", k)
                    v.wait_ge(emptied["act"].sem, emptied["act"].of(L, TILES["glu1", k].emptied))
                    stt(z_gate[:, k, :], b[:, :], vec[:, V_BGLU + k:V_BGLU + k + 1], z_gate[:, k, :], ADD, MUL)\
                        .then_inc(emptied["vec"].sem, 1)
                v.wait_ge(emptied["vec"].sem, emptied["vec"].of(L, 4))
                for k in range(4):
                    split_tile(L, YS, k, ys_lo, ys_hi, z_gate[:, k, :])
                for k in range(8):
                    b = tile_wait(L, f"bs{k // 4}", k % 4)
                    v.wait_ge(emptied["act"].sem, emptied["act"].of(L, TILES[f"gs{k // 2}", k % 2].emptied))
                    v.tensor_tensor(merged[:, k, :], merged[:, k, :], b[:, :], MUL).then_inc(emptied["vec"].sem, 1)
                for t in range(2):
                    v.wait_ge(alpha_ready.sem, alpha_ready.of(L, t + 1))
                    v.tensor_scalar(lb[:, t, :], bank[4 + t][:, :], vec[:, V_BALPHA + t:V_BALPHA + t + 1], 0.0, ADD, ALU.min)\
                     .then_inc(alpha_read.sem, 1)
                for t in range(2):
                    v.wait_ge(alpha_exps.sem, alpha_exps.of(L, t + 1))
                    v.wait_ge(alpha_read.sem, alpha_read.of(L, t + 1))
                    st.did(v.tensor_tensor(la[:, t, :], lb[:, t, :], la[:, t, :], SUB))
                    st.wait()
                    v.tensor_tensor_scan(lb[:, t, :], chunk_mask[:, :], la[:, t, :], 0.0, MUL, ADD).then_inc(decay_sum.sem, 1)
                for t in range(2):
                    b3 = lb[:, t, :].rearrange("p (n i) -> p n i", i=GLA_CHUNK)
                    v.wait_ge(gla_exps.sem, gla_exps.of(L, 2 * t + 2))
                    st.did(v.tensor_copy(small[:, 8 * t:8 * t + 8], b3[:, :, GLA_CHUNK - 1]))
                    st.wait()
                    v.tensor_tensor(b3, small[:, 8 * t:8 * t + 8].unsqueeze(2).to_broadcast([P, N_GCH, GLA_CHUNK]), b3, SUB)\
                     .then_inc(decay_last.sem, 1)
                for t in range(2):
                    v.wait_ge(gla_exps.sem, gla_exps.of(L, 2 * t + 2))
                    stt(gq[:, t, :], gq[:, t, :], GLA_DK ** -0.5, eb[:, t, :], MUL, MUL).then_inc(gla_keys.sem, 1)
                    v.tensor_tensor(la[:, t, :], la[:, t, :], gk[:, t, :], MUL).then_inc(gla_keys.sem, 1)
                for t in range(2):
                    v.wait_ge(gla_exps.sem, gla_exps.of(L, 4 + t + 1))
                    v.wait_ge(gla_keys.sem, gla_keys.of(L, 2 * t + 2))
                    v.tensor_tensor(gk[:, t, :], gk[:, t, :], lb[:, t, :], MUL).then_inc(gla_keys.sem, 1)

                def clamp(hd):
                    v.wait_ge(att_ready.sem, att_ready.of(L, hd + 1))
                    a = att[:, hd % 2, :, :]
                    if hd >= 2:
                        v.wait_ge(o_ready.sem, o_ready.of(L, hd - 1))
                    st.did(v.tensor_tensor(a, bank[4][:, :].rearrange("p (b n) -> p b n", b=TB),
                                           clamp_hi[:, :].unsqueeze(1).to_broadcast([P, TB, P]), ALU.min))
                    st.wait()
                    v.tensor_tensor(a, a, clamp_lo[:, :].unsqueeze(1).to_broadcast([P, TB, P]), ALU.max)\
                     .then_inc(att_clamped.sem, 1)

                for t in range(2):
                    v.wait_ge(ds_ready.sem, ds_ready.of(L, t + 1))
                    for n in range(N_GCH - 1):
                        d = bank[6 + n % 2][:, (n // 2) * P:(n // 2 + 1) * P]
                        if n == 0:
                            ins = v.tensor_copy(s_state[:, t, 1, :], d)
                        else:
                            e = n * GLA_CHUNK + GLA_CHUNK - 1
                            ins = stt(s_state[:, t, n + 1, :], s_state[:, t, n, :], eb[:, t, e:e + 1], d, MUL, ADD)
                        if n < N_GCH - 2:
                            st.did(ins)
                            st.wait()
                    ins.then_inc(s_ready.sem, 1)
                    clamp(t)
                for hd in range(GLA_HEADS):
                    if hd + 2 < GLA_HEADS:
                        clamp(hd + 2)
                    head_keep(L, hd, 6 + hd % 2)
                heads_norm(L, 0)
                for k in range(4):
                    split_tile(L, YGA, k, yga_lo, yga_hi, gr[:, k, :])
                v.wait_ge(bias_loaded.sem, bias_loaded.of(L, 16))
                diff_max(L, 0)
                for i in range(DIFF_HEADS * TB):
                    hd, qb = divmod(i, TB)
                    if 8 <= i < 12:
                        branch_tile(L, "bg0", i - 8, i - 8)
                    if i + 1 < DIFF_HEADS * TB:
                        diff_max(L, i + 1)
                    diff_mix(L, i)
                    if qb == TB - 1:
                        head_keep(L, 4 + hd, 7)
                heads_norm(L, 1)
                for k in range(4):
                    branch_tile(L, "bg1", k, 4 + k)
                for k in range(4):
                    split_tile(L, YD, k, yd_lo, yd_hi, dq[:, k, :])
                for k in range(8):
                    branch_tile(L, f"bd{k // 4}", k % 4, 8 + k)
                for m in range(KT):
                    split_tile(L, MG, m, mg_lo, mg_hi, merged[:, m, :])
                post(L, 1)
                modulate(L, 2)
                ffn(L, 1, C_FFN2)
                post(L, 2)
                assert st.n == VECTOR_STEPS, st.n

            for b in range(TB):
                v.wait_ge(out_turned, 2 * b + 2)
                v.wait_ge(out_half, b + 1)
                v.tensor_copy(x_tok[:, b, SEQ:D_MODEL], bank[2 * b + 1][:, :]).then_inc(out_copied, 1)

        @block.gpsimd
        def _(pool):
            pool.sem_inc(sq_summed.sem, 2)
            pool.memset(ident[:, :], 0.0).then_inc(pool_start, 1)
            pool.memset(ones[:, :], 1.0).then_inc(pool_start, 1)
            pool.memset(chunk_mask[:, :], 1.0).then_inc(pool_start, 1)
            pool.memset(clamp_hi[:, :], BIG).then_inc(pool_start, 1)
            pool.memset(clamp_lo[:, :], -BIG).then_inc(pool_start, 1)
            pool.memset(inv_d[:, 0:1], 1.0 / D_MODEL).then_inc(pool_start, 1)
            pool.memset(inv_d[:, 1:2], 1.0 / P).then_inc(pool_start, 1)
            pool.memset(cst[:, 0:1], EPS).then_inc(pool_start, 1)
            pool.memset(cst[:, 1:2], math.pi / 2).then_inc(pool_start, 1)
            for l in range(DEPTH):
                lam_init = 0.8 - 0.6 * math.exp(-0.3 * l)
                pool.memset(lam_tab[:, l:l + 1], lam_init).then_inc(pool_start, 1)
                pool.memset(lam_tab[:, DEPTH + l:DEPTH + l + 1], 1.0 - lam_init).then_inc(pool_start, 1)
            pool.iota(time_row[:, :], [[1, SEQ]], base=0, channel_multiplier=0, allow_small_or_imprecise_dtypes=True)\
                .then_inc(pool_start, 1)
            pool.wait_ge(pool_start, 10 + 2 * DEPTH)
            pool.affine_select(out=ident[:, :], in_=ident[:, :], compare_op=ALU.not_equal, fill=1.0, base=0,
                               pattern=[[-1, P]], channel_multiplier=1).then_inc(const_ready, 1)
            pool.affine_select(out=chunk_mask[:, :], in_=chunk_mask[:, :], compare_op=ALU.not_equal, fill=0.0, base=0,
                               pattern=[[0, N_GCH], [1, GLA_CHUNK]], channel_multiplier=0).then_inc(const_ready, 1)
            for m in (clamp_hi, clamp_lo):
                pool.affine_select(out=m[:, :], in_=m[:, :], compare_op=ALU.is_ge, fill=0.0, base=0,
                                   pattern=[[1, P]], channel_multiplier=-1).then_inc(pool_start, 1)
            pool.wait_ge(pool_start, 12 + 2 * DEPTH)
            for m in (clamp_hi, clamp_lo):
                pool.memset(m[0:64, 64:128], 0.0).then_inc(pool_start, 1)
            pool.wait_ge(pool_start, 14 + 2 * DEPTH)
            pool.sem_inc(const_ready, 1)

            def squares(L, r, tiles=range(1, KT)):
                for m in tiles:
                    pool.wait_ge(sq_ready.sem, sq_ready.of(L, KT * r + m + 1))
                    if m == 1:
                        pool.tensor_tensor(sq_sum[:, :], sq_buf[:, 0, :], sq_buf[:, 1, :], ALU.add).then_inc(sq_summed.sem, 2)
                    else:
                        pool.wait_ge(sq_summed.sem, sq_summed.of(L, KT * r + m))
                        pool.tensor_tensor(sq_sum[:, :], sq_sum[:, :], sq_buf[:, m % 2, :], ALU.add).then_inc(sq_summed.sem, 1)

            def split(L, name):
                ch = CHUNK_OF[name]
                s = ch % 2
                n = KT * P if chunk_widths(name) == P else CHUNK_ELEMS
                pool.wait_ge(hi_split[s].sem, slot_value(hi_split[s], L, ch))
                pool.tensor_tensor(w_lo[s][:, 0:n], raw[s][:, 0:n], w_hi[s][:, 0:n].bitcast(F32), ALU.subtract)\
                    .then_inc(lo_split[s].sem, 1)

            with pool.Fori(0, DEPTH) as L:
                squares(L, 0)
                squares(L, 1)
                squares(L, 2)
                s = (C_MIX - 1) % 2
                pool.wait_ge(chunk_done[s].sem, slot_value(chunk_done[s], L, C_MIX - 1))
                pool.sem_inc(room_seen.sem, 1)
                pool.memset(s5_bx[:, :, :, :, :, :].rearrange("p a q i g h -> p (a q i g h)"), 0.0).then_inc(s5_bx_zero.sem, 1)
                pool.memset(s5_mask[:, :, :, :], 0.0).then_inc(s5_mask_ready.sem, 1)
                pool.wait_ge(s5_mask_ready.sem, s5_mask_ready.of(L, 1))
                pool.sem_inc(room_seen.sem, 1)
                for g in range(2):
                    pool.memset(s5_mask[64 * g:64 * g + 64, :, g, :], 1.0).then_inc(s5_mask_ready.sem, 1)
                pool.wait_ge(s5_mask_ready.sem, s5_mask_ready.of(L, 3))
                for name, _, _ in MIXER[:3]:
                    split(L, name)
                split(L, "gq")
                ahead, first = [], 0
                for name, n, _ in MIXER[3:14]:
                    ahead.append((first, name))
                    first += n
                ahead = ahead[1:]
                for j in range(S5_PAIRS):
                    r = [rot[:, j % 2, i, :] for i in range(4)]
                    while ahead and ahead[0][0] <= -(-5 * (j + 1) // 4) + 1:
                        split(L, ahead.pop(0)[1])
                    pool.wait_ge(front_done.sem, front_done.of(L, j + 1))
                    pool.tensor_tensor(r[0], r[0], r[1], ALU.add).then_inc(z_in_ready.sem, 1)
                    pool.tensor_tensor(r[2], r[2], r[3], ALU.subtract).then_inc(z_in_ready.sem, 1)
                    pool.wait_ge(back_done.sem, back_done.of(L, j + 1))
                    pool.tensor_tensor(r[0], r[0], r[2], ALU.subtract).then_inc(state_ready.sem, 1)
                    pool.tensor_tensor(r[1], r[1], r[3], ALU.add).then_inc(state_ready.sem, 1)
                assert not ahead
                for name, _, _ in MIXER[14:-1]:
                    split(L, name)
                squares(L, 3, (1,))
                split(L, MIXER[-1][0])
                squares(L, 3, range(2, KT))
                squares(L, 4)
                squares(L, 5)


_NAMES = ["x", "c", "rel_bias", "w_ada", "b_ada", "norm_pre", "norm_post", "ffn1_w_up", "ffn1_w_down", "ffn2_w_up",
          "ffn2_w_down", "w_in", "gla_w_alpha", "gla_b_alpha", "gla_norm", "diff_lambda", "diff_norm", "s5_lam_re",
          "s5_lam_im", "s5_log_step", "s5_b_re", "s5_b_im", "s5_c_re", "s5_c_im", "s5_d", "s5_w_glu", "s5_b_glu",
          "w_branch", "w_out"]


def bucket_onehot():
    hot = np.zeros((NUM_BUCKETS + 1, LINE), np.float32)
    exact = NUM_BUCKETS // 2
    for y in range(LINE):
        d = SEQ - 1 - y
        if d < 0:
            hot[NUM_BUCKETS, y] = 1.0
        elif d < exact:
            hot[d, y] = 1.0
        else:
            scaled = np.log(np.float32(d) / np.float32(exact)) / np.float32(math.log(MAX_DISTANCE / exact))
            hot[min(exact + int(np.float32(scaled * np.float32(NUM_BUCKETS - exact))), NUM_BUCKETS - 1), y] = 1.0
    return hot


def kernel(**inputs):
    import concourse.bacc as bacc
    from concourse.bass_utils import run_bass_kernel_spmd

    nc = bacc.Bacc("TRN2", target_bir_lowering=False, num_devices=1)
    nc.disable_value_cache = True
    arrays = {"in_" + name: np.ascontiguousarray(inputs[name]) for name in _NAMES}
    arrays["in_bucket_onehot"] = bucket_onehot()
    args = [nc.dram_tensor(name, a.shape, mybir.dt.from_np(a.dtype), kind="ExternalInput").ap() for name, a in arrays.items()]
    args.append(nc.dram_tensor("out", (1, SEQ, D_MODEL), F32, kind="ExternalOutput").ap())
    build(nc, *args)
    return run_bass_kernel_spmd(nc, [arrays], core_ids=[0]).results[0]["out"]
```

```python
import math
from contextlib import ExitStack

import numpy as np
import concourse.bass as bass
from concourse import mybir

F32 = mybir.dt.float32
F32R = mybir.dt.float32r
BF16 = mybir.dt.bfloat16
I32 = mybir.dt.int32
ALU = mybir.AluOpType
ACT = mybir.ActivationFunctionType
AX_X = mybir.AxisListType.X

P = 128
D_MODEL, SEQ, DEPTH, D_FF = 1024, 512, 2, 2816
KT = D_MODEL // P
FT = D_FF // P
TB = SEQ // P
EPS = 1e-6
CHUNK_ELEMS = 2048
GLA_HEADS, GLA_DK, GLA_CHUNK, LOWRANK, GLA_TAU = 4, 64, 64, 16, 16.0
N_GCH = SEQ // GLA_CHUNK
DIFF_HEADS, N_MAPS = 4, 8
NUM_BUCKETS, MAX_DISTANCE = 32, 128
S5_PAIRS, S5_CH = 16, 16
LINE = SEQ + P
MAGIC = 1.5 * 2.0 ** 23
BIG = 3.0e38
MASKED = -1.0e30
TWO_PI = 2.0 * math.pi
TWO_PI_A, TWO_PI_B = 6.28125, 0.0019340515136718750
TWO_PI_C = TWO_PI - TWO_PI_A - TWO_PI_B
LN2_A = 0.693359375
LN2_B = math.log(2.0) - LN2_A

OFF_GQ, OFF_GK, OFF_GV, OFF_GR, OFF_A = 0, 256, 512, 1024, 1536
OFF_DQ, OFF_DK, OFF_DV, OFF_SU, OFF_GATE = 1552, 2064, 2576, 3088, 3600

MIXER = [("su0", 2, "act"), ("su1", 1, "act"), ("su2", 1, "act"),
         ("gq", 2, "act"), ("gk", 2, "act"), ("ga", 1, "act"), ("gv0", 2, "act"), ("gv1", 2, "act"),
         ("gr0", 2, "act"), ("gr1", 2, "act")] + [(f"gs{i}", 2, "act") for i in range(4)] + \
        [("glu1", 4, "act"), ("glu0", 4, "vec"), ("bs0", 4, "vec"), ("bs1", 4, "vec")] + \
        [(f"d{x}{i}", 2, "act") for x in "qkv" for i in range(2)] + \
        [("gg0", 2, "act"), ("gg1", 2, "act"), ("bg0", 4, "vec"), ("gg2", 2, "act"), ("gg3", 2, "act"), ("bg1", 4, "vec")] + \
        [(f"gd{i}", 2, "act") for i in range(4)] + [("bd0", 4, "vec"), ("bd1", 4, "vec")] + \
        [(f"wo{i}", 2, "sub") for i in range(4)]
FFN_CHUNKS = 2 * FT // 2 + FT // 2
C_MIX, C_FFN2 = FFN_CHUNKS, FFN_CHUNKS + len(MIXER)
CHUNKS = 2 * FFN_CHUNKS + len(MIXER)
assert CHUNKS % 2 == 0 and C_MIX % 2 == 1
SLOT_USES = CHUNKS // 2
ADA_ROUNDS = (2 * 3 * D_MODEL // 768, 3 * D_MODEL // 768)
FFN_TILES = FT + KT - 1


class Tile:
    pass


def mixer_tiles():
    tiles, evac = {}, {"act": 0, "vec": 0, "sub": 0}
    t, ready = 0, FFN_TILES
    order = []
    for i, (name, n, engine) in enumerate(MIXER):
        for k in range(n):
            x = Tile()
            x.chunk, x.bank, x.engine = C_MIX + i, t % 4, engine
            x.last = k == n - 1
            if not x.last:
                ready += 1
            x.ready = ready
            evac[engine] += 1
            x.emptied = evac[engine]
            x.before = order[t - 4] if t >= 4 else None
            order.append(x)
            tiles[name, k] = x
            t += 1
    return tiles, evac, ready


TILES, EMPTIED, READY_BEFORE_FFN2 = mixer_tiles()
S5_SIDE = [name for name, _, _ in MIXER[3:14]]
S5_SIDE_TILES = sum(n for _, n, _ in MIXER[3:14])
S5_FIRST = [sum(n for _, n, _ in MIXER[3:3 + i]) for i in range(len(S5_SIDE))]
S5_PACE = S5_SIDE_TILES - 2
S5_SPLIT_AT = [max(0, min(S5_PAIRS - 1, first * S5_PAIRS // S5_PACE - 2)) for first in S5_FIRST]
DIFF_BLOCKS = DIFF_HEADS * TB
BESIDE = [t for t in TILES if t[0] in ("gg1", "bg0", "gg2", "gg3", "bg1", "gd0")]
BESIDE_DIFF = [[t for n, t in enumerate(BESIDE) if n * DIFF_BLOCKS // len(BESIDE) == i] for i in range(DIFF_BLOCKS)]
CHUNK_OF = {name: C_MIX + i for i, (name, _, _) in enumerate(MIXER)}
READY_PER_LAYER = READY_BEFORE_FFN2 + FFN_TILES
VECTOR_STEPS, SCALAR_STEPS = 238, 35

V_BADA, V_PRE, V_POST, V_GNORM, V_DNORM, V_SD, V_BGLU, V_BALPHA, V_LRE, V_LIM, V_LSTEP, \
    V_PHASE, V_MAG, V_FRE, V_FIM, V_NEGLAM, V_END = \
    0, 72, 96, 120, 124, 128, 132, 140, 142, 158, 174, 190, 206, 222, 238, 254, 255
V_LOADED = V_LSTEP
ADA_WIDTH = 256
ADA_THIRD = 3 * D_MODEL // ADA_WIDTH
assert DEPTH == 2


class Signal:

    def __init__(self, ctx, nc, name, per_layer, head_start=0):
        self.sem = ctx.enter_context(nc.semaphore(name))
        self.per_layer, self.head_start = per_layer, head_start

    def of(self, layer, k):
        return layer * self.per_layer + k + self.head_start


class Steps:

    def __init__(self, engine, counter, layer):
        self.engine, self.counter, self.layer, self.n = engine, counter, layer, 0

    def did(self, instruction):
        instruction.then_inc(self.counter.sem, 1)
        self.n += 1

    def wait(self, back=0):
        if self.n - back > 0:
            self.engine.wait_ge(self.counter.sem, self.counter.of(self.layer, self.n - back))


def build(nc, x, c, rel_bias, w_ada, b_ada, norm_pre, norm_post, ffn1_w_up, ffn1_w_down, ffn2_w_up, ffn2_w_down,
          w_in, gla_w_alpha, gla_b_alpha, gla_norm, diff_lambda, diff_norm, s5_lam_re, s5_lam_im, s5_log_step,
          s5_b_re, s5_b_im, s5_c_re, s5_c_im, s5_d, s5_w_glu, s5_b_glu, w_branch, w_out, bucket_onehot, out):
    ctx = ExitStack()
    with ctx:
        BASE = 16512
        X0 = 105

        def at(name, kib, shape, dt=F32):
            return nc.alloc_sbuf_tensor_at(name, shape, dt, offset=BASE + int(round(kib * 1024)))

        def shared(name, kib, shape, dt=F32):
            return at(name, X0 + kib, shape, dt)

        h = at("h", 0, [P, KT, SEQ])
        u_hi = at("u_hi", 16, [P, KT, SEQ], F32R)
        u_lo = at("u_lo", 32, [P, KT, SEQ], F32R)
        y_sub = at("y_sub", 16, [P, KT, SEQ])
        raw = [at(f"raw{s}", 48 + 8 * s, [P, CHUNK_ELEMS]) for s in range(2)]
        w_hi = [at(f"w_hi{s}", 64 + 8 * s, [P, CHUNK_ELEMS], F32R) for s in range(2)]
        w_lo = [at(f"w_lo{s}", 80 + 8 * s, [P, CHUNK_ELEMS], F32R) for s in range(2)]
        ident = at("ident", 96, [P, P])
        ones = at("ones", 96.5, [P, P])
        time_row = at("time_row", 97, [P, SEQ])
        chunk_mask = at("chunk_mask", 99, [P, SEQ], BF16)
        clamp_hi = at("clamp_hi", 100, [P, P])
        clamp_lo = at("clamp_lo", 100.5, [P, P])
        vec_all = at("vec_all", 101, [P, DEPTH, V_END])
        vec = at("vec", 103, [P, V_END])
        ada = at("ada", 104, [P, 72])
        pre_gain = at("pre_gain", 104.28125, [P, 24])
        post_gain = at("post_gain", 104.375, [P, 24])
        small = at("small", 104.46875, [P, 48])
        cond = at("cond", 104.65625, [P, KT])
        sq_root = at("sq_root", 104.6875, [P, 16])
        rstd_tok = at("rstd_tok", 104.75, [P, 16])
        ms_heads = at("ms_heads", 104.8125, [P, 16])
        smax = at("smax", 104.875, [P, 2, 8])
        inv_d = at("inv_d", 104.9375, [P, 2])
        cst = at("cst", 104.96875, [P, 2])
        EPS_COL, HALF_PI = cst[:, 0:1], cst[:, 1:2]
        neg_lam = vec[:, V_NEGLAM:V_END]
        phase, mag, f_re, f_im = (vec[:, i:i + S5_PAIRS] for i in (V_PHASE, V_MAG, V_FRE, V_FIM))

        g_hi = shared("g_hi", 0, [P, FT, SEQ], F32R)
        g_lo = shared("g_lo", 44, [P, FT, SEQ], F32R)
        silu_buf = shared("silu_buf", 88, [P, 2, SEQ])
        mod_buf = shared("mod_buf", 92, [P, 2, SEQ])
        sq_buf = shared("sq_buf", 94, [P, 3, SEQ])
        sq_sum = shared("sq_sum", 100, [P, SEQ])
        ada_w = [shared(f"ada_w{s}", k, [P, KT, ADA_WIDTH]) for s, k in enumerate((32, 76, 92))]
        first_ada_w = [shared(f"first_ada_w{s}", k, [P, KT, ADA_WIDTH]) for s, k in enumerate((32, 50, 58, 66, 74, 82))]
        ada_acc = [shared(f"ada_acc{s}", 40 + s, [P, ADA_WIDTH]) for s in range(3)]
        rows_a = [shared(f"rows_a{l}", 24 + l, [72, P]) for l in range(DEPTH)]
        rows_b = [shared(f"rows_b{l}", 24.5 + l, [V_LOADED - 72, P]) for l in range(DEPTH)]
        log_steps = shared("log_steps", 26, [P, DEPTH, 2 * S5_PAIRS])
        lam_rows = shared("lam_rows", 28, [P, DEPTH, 4, 64])
        lam_prod = shared("lam_prod", 30, [P, 64])
        x_tok = shared("x_tok", 0, [P, TB, D_MODEL])
        c_row = shared("c_row", 16, [KT, P])
        onehot = shared("onehot", 17, [NUM_BUCKETS + 1, LINE])
        rel33 = shared("rel33", 20, [NUM_BUCKETS + 1, N_MAPS])
        bias_line = shared("bias_line", 21, [N_MAPS, LINE])
        pscr = shared("pscr", 44, [P, 12, DEPTH, S5_PAIRS])
        pint = shared("pint", 46, [P, DEPTH, S5_PAIRS], I32)
        su = shared("su", 0, [P, 4, SEQ])
        s_state = shared("s_state", 0, [P, 2, N_GCH, P])
        gq = shared("gq", 8, [P, 2, SEQ])
        gk = shared("gk", 12, [P, 2, SEQ])
        gv = shared("gv", 16, [P, TB, SEQ])
        gr = shared("gr", 24, [P, 4, SEQ])
        merged = shared("merged", 32, [P, KT, SEQ])
        s5_bt = shared("s5_bt", 48, [P, 2, 4, P])
        s5_ct = shared("s5_ct", 52, [P, 2, 4, P])
        s5_bx = shared("s5_bx", 58, [P, 2, 4, 4, 2, S5_CH])
        s5_cd = shared("s5_cd", 62, [P, 2, 4, 2, 64])
        s5_b = shared("s5_b", 66, [P, 2, S5_PAIRS, S5_CH])
        s5_t = shared("s5_t", 68, [P, 2, S5_PAIRS, S5_CH])
        s5_mask = shared("s5_mask", 70, [P, 4, 2, S5_CH])
        rot = [shared(f"rot{i}", k, [P, 4, SEQ]) for i, k in enumerate((58, 66, 94))]
        tab_c = shared("tab_c", 74, [P, 3, SEQ])
        tab_s = shared("tab_s", 80, [P, 3, SEQ])
        turns = shared("turns", 86, [P, 2, SEQ])
        rounded = shared("rounded", 90, [P, SEQ])
        a_low = shared("a_low", 92, [LOWRANK, SEQ])
        w_alpha = shared("w_alpha", 56, [LOWRANK, 256])
        yg_hi = shared("yg_hi", 58, [P, 4, SEQ], F32R)
        yg_lo = shared("yg_lo", 66, [P, 4, SEQ], F32R)
        z_gate = shared("z_gate", 0, [P, 4, SEQ])
        ys_hi = shared("ys_hi", 74, [P, 4, SEQ], F32R)
        ys_lo = shared("ys_lo", 82, [P, 4, SEQ], F32R)
        la = shared("la", 48, [P, 2, SEQ])
        lb = shared("lb", 52, [P, 2, SEQ])
        eb = shared("eb", 56, [P, 2, SEQ])
        kk_tok = shared("kk_tok", 60, [P, TB, 2 * P])
        att = shared("att", 64, [P, 2, TB, P])
        o_head = [shared(f"o_head{i}", k, [P, SEQ]) for i, k in enumerate((68, 70, 90, 72))]
        o_sq = shared("o_sq", 92, [P, SEQ])
        dq = shared("dq", 74, [P, 4, SEQ])
        dk = shared("dk", 82, [P, 4, SEQ])
        dv = shared("dv", 94, [P, TB, SEQ])
        yga_hi = shared("yga_hi", 48, [P, 4, SEQ], F32R)
        yga_lo = shared("yga_lo", 56, [P, 4, SEQ], F32R)
        sig = shared("sig", 0, [P, 4, SEQ])
        sig_late = shared("sig_late", 64, [P, 4, SEQ])
        bias_tab = shared("bias_tab", 8, [P, N_MAPS, SEQ])
        a_t = shared("a_t", 24, [P, TB, SEQ])
        prob = [shared("prob0", 64, [P, 2, SEQ]), shared("prob1", 68, [P, 2, SEQ])]
        yd_hi = shared("yd_hi", 48, [P, 4, SEQ], F32R)
        yd_lo = shared("yd_lo", 56, [P, 4, SEQ], F32R)
        mg_hi = shared("mg_hi", 8, [P, KT, SEQ], F32R)
        mg_lo = shared("mg_lo", 74, [P, KT, SEQ], F32R)

        bank = [ctx.enter_context(nc.psum_tensor(f"bank{i}", [P, SEQ], F32)) for i in range(8)]
        bias_dram = nc.dram_tensor("bias_line_dram", (N_MAPS, LINE), F32, kind="Internal").ap()
        bias_copies = nc.dram_tensor("bias_copies_dram", (N_MAPS, P, LINE), F32, kind="Internal").ap()

        MS_BANK = (4, 0, 4, 4, 4, 0)

        def signal(name, per_layer, head_start=0):
            return Signal(ctx, nc, name, per_layer, head_start)

        def sem(name):
            return ctx.enter_context(nc.semaphore(name))

        raw_loaded = [signal(f"raw_loaded{s}", 16 * SLOT_USES) for s in range(2)]
        hi_split = [signal(f"hi_split{s}", SLOT_USES, 1) for s in range(2)]
        lo_split = [signal(f"lo_split{s}", SLOT_USES, 1) for s in range(2)]
        chunk_done = [signal(f"chunk_done{s}", SLOT_USES, 1) for s in range(2)]
        tile_ready = signal("tile_ready", READY_PER_LAYER)
        emptied = {"act": signal("emptied_by_act", EMPTIED["act"]), "vec": signal("emptied_by_vec", EMPTIED["vec"])}
        silu_done = signal("silu_done", 2 * FT, 2)
        prod_done = signal("prod_done", 2 * FT, 2)
        g_hi_ready = signal("g_hi_ready", 2 * FT)
        g_lo_ready = signal("g_lo_ready", 2 * FT, 2)
        h_ready = signal("h_ready", 3 * KT, KT)
        sq_ready = signal("sq_ready", 6 * KT)
        sq_summed = signal("sq_summed", 6 * KT, 3)
        ms_ready = signal("ms_ready", 6, 1)
        y_copied = signal("y_copied", 3 * KT)
        root_ready = signal("root_ready", 6)
        inverse_ready = signal("inverse_ready", 6)
        rstd_ready = signal("rstd_ready", 6)
        modulated = signal("modulated", 3 * KT)
        u_hi_ready = signal("u_hi_ready", 3 * KT)
        u_ready = signal("u_ready", 3 * KT)
        vector_steps = signal("vector_steps", VECTOR_STEPS)
        scalar_steps = signal("scalar_steps", SCALAR_STEPS)
        x_loaded, c_loaded, line_loaded = sem("x_loaded"), sem("c_loaded"), sem("line_loaded")
        const_ready, x_turned, c_turned = sem("const_ready"), sem("x_turned"), sem("c_turned")
        rows_loaded, rows_turned, spread_loaded, vec_steps = sem("rows_loaded"), sem("rows_turned"), sem("spread_loaded"), sem("vec_steps")
        theta_ready, sines_ready, lam_sums, lam_exps = sem("theta_ready"), sem("sines_ready"), sem("lam_sums"), sem("lam_exps")
        cond_ready, line_made, line_copied, line_stored = sem("cond_ready"), sem("line_made"), sem("line_copied"), sem("line_stored")
        out_turned, out_half, out_copied, out_stored = sem("out_turned"), sem("out_half"), sem("out_copied"), sem("out_stored")
        pool_start = sem("pool_start")
        ada_loaded = [signal(f"ada_loaded{s}", 16 * ADA_THIRD) for s in range(3)]
        first_ada_loaded = [sem(f"first_ada_loaded{s}") for s in range(6)]
        ada_step = signal("ada_step", 3 * ADA_THIRD * KT, 3 * KT)
        ada_column = signal("ada_column", 3 * ADA_THIRD, 6 + ADA_THIRD)
        ada_kept = signal("ada_kept", 2)
        vec_ready = signal("vec_ready", 1)
        s5w_loaded = signal("s5w_loaded", 16 * 6)
        s5_bx_zero = signal("s5_bx_zero", 1)
        s5_mask_ready = signal("s5_mask_ready", 3)
        s5_bx_ready = signal("s5_bx_ready", 1)
        s5_turned = signal("s5_turned", 2)
        s5_mats_ready = signal("s5_mats_ready", 1)
        turns_ready = signal("turns_ready", S5_PAIRS)
        tables_ready = signal("tables_ready", S5_PAIRS)
        bu_ready = signal("bu_ready", S5_PAIRS)
        front_done = signal("front_done", S5_PAIRS)
        z_in_ready = signal("z_in_ready", 2 * S5_PAIRS)
        back_done = signal("back_done", S5_PAIRS)
        state_ready = signal("state_ready", 2 * S5_PAIRS)
        alpha_loaded = signal("alpha_loaded", 16)
        s5_y_ready = signal("s5_y_ready", S5_PAIRS)
        s5_y_summed = signal("s5_y_summed", 4)
        gelu_done = signal("gelu_done", 4)
        split_hi = signal("split_hi", 4 + 4 + 4 + 4 + 8)
        split_lo = signal("split_lo", 4 + 4 + 4 + 4 + 8)
        YG, YS, YGA, YD, MG = 0, 4, 8, 12, 16
        merged_ready = signal("merged_ready", 16)
        alpha_ready = signal("alpha_ready", 2)
        alpha_read = signal("alpha_read", 2)
        alpha_exps = signal("alpha_exps", 1)
        decay_sum = signal("decay_sum", 2)
        decay_last = signal("decay_last", 2)
        gla_exps = signal("gla_exps", 6)
        gla_keys = signal("gla_keys", 6)
        kk_turned = signal("kk_turned", 1)
        kk_copied = signal("kk_copied", 2)
        ds_ready = signal("ds_ready", 2)
        s_ready = signal("s_ready", 2)
        att_ready = signal("att_ready", 4)
        att_clamped = signal("att_clamped", 4)
        o_ready = signal("o_ready", 8)
        o_copied = signal("o_copied", 8)
        o_squared = signal("o_squared", 8)
        o_ms = signal("o_ms", 8)
        o_ms_kept = signal("o_ms_kept", 8)
        o_roots = signal("o_roots", 2)
        o_inverse = signal("o_inverse", 2)
        o_rstd = signal("o_rstd", 8)
        o_normed = signal("o_normed", 8)
        yga_done = signal("yga_done", 4)
        bias_loaded = signal("bias_loaded", 16)
        scores_ready = signal("scores_ready", 32)
        scores_seen, states_begun, room_seen = signal("scores_seen", 16), signal("states_begun", 2), signal("room_seen", 2)
        max_ready = signal("max_ready", 16)
        prob_ready = signal("prob_ready", 16)
        mix_ready = signal("mix_ready", 16)
        at_ready = signal("at_ready", 16)
        at_copied = signal("at_copied", 16)

        def cols(j, n=1):
            return bass.ds(j, n)

        def flat(ap):
            return ap.rearrange("p a n -> p (a n)")

        def slot_value(sig, L, chunk, extra=0):
            return sig.of(L, chunk // 2 + 1 + extra)

        def chunk_widths(name):
            return P if name in ("su1", "su2", "ga") else 256

        block = ctx.enter_context(nc.Block())

        @block.sync
        def _(sp):
            def load(L, s, n, dst, src):
                sp.wait_ge(hi_split[s].sem, hi_split[s].of(L, n - 1))
                sp.wait_ge(lo_split[s].sem, lo_split[s].of(L, n - 1))
                sp.dma_start(dst, src).then_inc(raw_loaded[s].sem, 16)

            def load_ffn(L, f, c0, w_up, w_down):
                def up(j):
                    for half in range(2):
                        s = (c0 + half) % 2
                        n = (c0 + half) // 2 + j + 1
                        src = w_up[L, :, bass.ds(j * 256 + half * D_FF, 256)].rearrange("(k p) n -> p k n", p=P)
                        load(L, s, n, raw[s][:, :].rearrange("p (k n) -> p k n", k=KT), src)

                with sp.Fori(0, ADA_ROUNDS[f]) as j:
                    up(j)
                    sp.wait_ge(modulated.sem, modulated.of(L, 2 * f * KT + 1))
                    for s in range(3):
                        if s == 2:
                            sp.wait_ge(u_ready.sem, u_ready.of(L, (2 * f + 1) * KT))
                        sp.wait_ge(ada_step.sem, ada_step.of(L, (f * 2 * ADA_THIRD + j * 3 + s - 2) * KT))
                        load_ada(ada_w[s], ada_loaded[s].sem, DEPTH - 1 if f else L, j * (3 * ADA_WIDTH) + (s * ADA_WIDTH + (0 if f else 3 * D_MODEL)))
                with sp.Fori(ADA_ROUNDS[f], FT // 2) as j:
                    up(j)
                c1 = c0 + FT
                s = c1 % 2
                load(L, s, c1 // 2 + 1, raw[s][:, :].rearrange("p (k n) -> p k n", k=2),
                     w_down[L, 0:256, :].rearrange("(k p) n -> p k n", p=P))
                with sp.Fori(0, FT // 4) as j:
                    for half in range(2):
                        s = (c1 + 1 + half) % 2
                        n = (c1 + 1 + half) // 2 + j + 1
                        src = w_down[L, bass.ds(j * 512 + half * 256 + 256, 256), :].rearrange("(k p) n -> p k n", p=P)
                        load(L, s, n, raw[s][:, :].rearrange("p (k n) -> p k n", k=2), src)

            def load_chunk(L, name):
                ch = CHUNK_OF[name]
                s = ch % 2
                i = int(name[-1]) if name[-1].isdigit() else 0
                start = {"su": OFF_SU, "gq": OFF_GQ, "gk": OFF_GK, "ga": OFF_A, "gv": OFF_GV, "gr": OFF_GR,
                         "dq": OFF_DQ, "dk": OFF_DK, "dv": OFF_DV, "gg": OFF_GATE, "gd": OFF_GATE + D_MODEL,
                         "gs": OFF_GATE + 2 * D_MODEL}.get(name[:2])
                if start is not None:
                    w = chunk_widths(name)
                    start += {"su1": 256, "su2": 384}.get(name, 256 * i)
                    load(L, s, ch // 2 + 1, raw[s][:, 0:KT * w].rearrange("p (k n) -> p k n", k=KT),
                         w_in[L, :, start:start + w].rearrange("(k p) n -> p k n", p=P))
                elif name[:2] == "wo":
                    load(L, s, ch // 2 + 1, raw[s][:, :].rearrange("p (k n) -> p k n", k=KT),
                         w_out[L, :, 256 * i:256 * i + 256].rearrange("(k p) n -> p k n", p=P))
                else:
                    src = s5_w_glu[L] if name[:3] == "glu" else w_branch[L, {"bg": 0, "bd": 1, "bs": 2}[name[:2]]]
                    load(L, s, ch // 2 + 1, raw[s][:, :].rearrange("p (k n) -> p k n", k=4),
                         src[:, 512 * i:512 * i + 512].rearrange("(k p) n -> p k n", p=P))

            sp.dma_start(c_row[:, :], c.rearrange("a (k p) -> (a k) p", p=P)).then_inc(c_loaded, 16)
            sp.dma_start(x_tok[:, :, :], x.rearrange("a (b p) d -> p (a b) d", p=P)).then_inc(x_loaded, 16)
            sp.dma_start(onehot[:, :], bucket_onehot).then_inc(line_loaded, 16)
            sp.dma_start(rel33[0:NUM_BUCKETS, :], rel_bias).then_inc(line_loaded, 16)
            for l in range(DEPTH):
                def row(dst, src):
                    sp.dma_start(dst, src).then_inc(rows_loaded, 16)

                def rb(a, b):
                    return rows_b[l][a - 72:b - 72, :]

                row(rows_a[l][:, :], b_ada[l].rearrange("(k p) -> k p", p=P))
                row(rb(V_PRE, V_POST), norm_pre[l].rearrange("a (k p) -> (a k) p", p=P))
                row(rb(V_POST, V_GNORM), norm_post[l].rearrange("a (k p) -> (a k) p", p=P))
                row(rb(V_GNORM, V_DNORM), gla_norm[l].rearrange("(k p) -> k p", p=P))
                row(rb(V_DNORM, V_SD), diff_norm[l].rearrange("(k p) -> k p", p=P))
                row(rb(V_SD, V_BGLU), s5_d[l].rearrange("(k g) n -> k (g n)", k=4))
                row(rb(V_BGLU, V_BALPHA), s5_b_glu[l].rearrange("(k p) -> k p", p=P))
                row(rb(V_BALPHA, V_LRE), gla_b_alpha[l].rearrange("(k p) -> k p", p=P))
                row(rb(V_LRE, V_LIM), s5_lam_re[l].rearrange("(j g) p -> j (g p)", g=2))
                row(rb(V_LIM, V_LSTEP), s5_lam_im[l].rearrange("(j g) p -> j (g p)", g=2))
            sp.dma_start(log_steps[:, :, :], s5_log_step.unsqueeze(0).to_broadcast([P, DEPTH, 2 * S5_PAIRS])).then_inc(spread_loaded, 16)
            sp.dma_start(lam_rows[:, :, :, :], diff_lambda.unsqueeze(0).to_broadcast([P, DEPTH, 4, 64])).then_inc(spread_loaded, 16)

            def load_ada(slot, loaded, layer, start):
                sp.dma_start(slot[:, :, :], w_ada[layer, :, bass.ds(start, ADA_WIDTH)].rearrange("(k p) n -> p k n", p=P))\
                  .then_inc(loaded, 16)

            with sp.Fori(0, ADA_THIRD // 6) as i:
                for s in range(6):
                    sp.wait_ge(ada_column.sem, i * 6 + s + 1)
                    load_ada(first_ada_w[s], first_ada_loaded[s], 0, i * (6 * ADA_WIDTH) + s * ADA_WIDTH)

            sp.wait_ge(line_copied, 2)
            sp.dma_start(bias_dram, bias_line[:, :]).then_inc(line_stored, 16)
            sp.wait_ge(line_stored, 16)
            sp.dma_start(bias_copies, bias_dram.unsqueeze(1).to_broadcast([N_MAPS, P, LINE])).then_inc(line_stored, 16)

            with sp.Fori(0, DEPTH) as L:
                load_ffn(L, 0, 0, ffn1_w_up, ffn1_w_down)
                for name, _, _ in MIXER[:2]:
                    load_chunk(L, name)
                s = (C_MIX - 1) % 2
                sp.wait_ge(chunk_done[s].sem, slot_value(chunk_done[s], L, C_MIX - 1))
                for i, (b, cc) in enumerate(((s5_b_re, s5_c_re), (s5_b_im, s5_c_im))):
                    sp.dma_start(s5_b[:, i, :, :], b[L].rearrange("(j g) p h -> (g p) j h", g=2)).then_inc(s5w_loaded.sem, 16)
                    for d in range(2):
                        sp.dma_start(s5_cd[:, i, :, d, :], cc[L].rearrange("(q g) n p -> (g n) q p", q=4))\
                          .then_inc(s5w_loaded.sem, 16)
                for name, _, _ in MIXER[2:18]:
                    load_chunk(L, name)
                sp.dma_start(w_alpha[:, :], gla_w_alpha[L]).then_inc(alpha_loaded.sem, 16)
                for name, _, _ in MIXER[18:26]:
                    load_chunk(L, name)
                sp.wait_ge(yga_done.sem, yga_done.of(L, 4))
                sp.wait_ge(line_stored, 32)
                lines = bass.AP(tensor=bias_copies.tensor, offset=P - 1, ap=[[LINE - 1, P], [P * LINE, N_MAPS], [1, SEQ]])
                sp.dma_start(bias_tab[:, :, :], lines).then_inc(bias_loaded.sem, 16)
                for name, _, _ in MIXER[26:]:
                    load_chunk(L, name)
                load_ffn(L, 1, C_FFN2, ffn2_w_up, ffn2_w_down)

            for b in range(TB):
                sp.wait_ge(out_copied, b + 1)
                sp.dma_start(out[0, b * P:(b + 1) * P, :], x_tok[:, b, :]).then_inc(out_stored, 16)
            sp.wait_ge(out_stored, 16 * TB)

        @block.tensor
        def _(pe):
            for s in range(2):
                pe.sem_inc(chunk_done[s].sem, 1)
            pe.sem_inc(ada_column.sem, 6)
            pe.sem_inc(sq_summed.sem, 3)
            pe.sem_inc(ms_ready.sem, 1)

            def matmul3(dst, hi, lo, rhi, rlo, first, last):
                pe.matmul(dst, hi, rhi, start=first, stop=False)
                pe.matmul(dst, hi, rlo, start=False, stop=False)
                return pe.matmul(dst, lo, rhi, start=False, stop=last)

            def mean_square(L, r):
                pe.wait_ge(sq_summed.sem, sq_summed.of(L, KT * (r + 1)))
                for b in range(TB):
                    i = pe.matmul(bank[MS_BANK[r]][:, b:b + 1], sq_sum[:, b * P:(b + 1) * P], inv_d[:, 0:1], start=True, stop=True)
                i.then_inc(ms_ready.sem, 1)

            def spread(dst, col):
                for b in range(TB):
                    i = pe.transpose(dst[:, b * P:(b + 1) * P], rstd_tok[:, col + b:col + b + 1].to_broadcast([P, P]), ident[:, :])
                return i

            def rstd_row(L, r):
                pe.wait_ge(inverse_ready.sem, inverse_ready.of(L, r + 1))
                spread(bank[MS_BANK[r] + 1], 0).then_inc(rstd_ready.sem, 1)

            def norm(L, r):
                mean_square(L, r)
                rstd_row(L, r)

            def ffn(L, f, c0):
                ui = 2 * f
                i0 = f * FT

                def up(j):
                    for half in range(2):
                        s = (c0 + half) % 2
                        wh = w_hi[s][:, :].rearrange("p (k n) -> p k n", k=KT)
                        wl = w_lo[s][:, :].rearrange("p (k n) -> p k n", k=KT)
                        pe.wait_ge(lo_split[s].sem, lo_split[s].of(L, (c0 + half) // 2 + j + 1))
                        freed = (silu_done, prod_done)[half]
                        order = [(mt, k) for mt in range(2) for k in range(KT)] if half else \
                            [(mt, k) for k in range(KT) for mt in range(2)]
                        for mt, k in order:
                            if k == 0:
                                pe.wait_ge(freed.sem, freed.of(L, i0 + 2 * j + mt - 1))
                            if half == 0 and mt == 0:
                                pe.wait_ge(u_ready.sem, u_ready.of(L, ui * KT + k + 1))
                            m = matmul3(bank[2 * half + mt][:, :], wh[:, k, mt * P:(mt + 1) * P], wl[:, k, mt * P:(mt + 1) * P],
                                        u_hi[:, k, :], u_lo[:, k, :], k == 0, k == KT - 1)
                            if k == KT - 1:
                                m.then_inc(chunk_done[s].sem if mt else tile_ready.sem, 1)

                with pe.Fori(0, ADA_ROUNDS[f]) as j:
                    up(j)
                    for s in range(3):
                        pe.wait_ge(ada_step.sem, ada_step.of(L, (f * 2 * ADA_THIRD + j * 3 + s + 1) * KT))
                        for t in range(2):
                            m = pe.matmul(bank[7][:, bass.ds(j * 6 + (2 * s + t), 1)], ada_acc[s][:, t * P:(t + 1) * P],
                                          ones[:, 0:1], start=True, stop=True)
                        m.then_inc(ada_column.sem, 1)
                with pe.Fori(ADA_ROUNDS[f], FT // 2) as j:
                    up(j)
                pe.wait_ge(ada_kept.sem, ada_kept.of(L, f + 1))
                c1 = c0 + FT

                def down(s, n, kt, first, last):
                    wh = w_hi[s][:, :].rearrange("p (k n) -> p k n", k=2)
                    wl = w_lo[s][:, :].rearrange("p (k n) -> p k n", k=2)
                    pe.wait_ge(lo_split[s].sem, lo_split[s].of(L, n))
                    pe.wait_ge(g_lo_ready.sem, g_lo_ready.of(L, i0 + kt + 2))
                    order = [(k, m) for m in range(KT) for k in range(2)] if last else \
                        [(k, m) for k in range(2) for m in ((4, 5, 6, 7, 0, 1, 2, 3) if first else range(KT))]
                    for k, m in order:
                        if first and k == 0 and m == 0:
                            pe.wait_ge(silu_done.sem, silu_done.of(L, i0 + FT))
                            pe.wait_ge(prod_done.sem, prod_done.of(L, i0 + FT))
                        if isinstance(kt, int):
                            rh, rl = g_hi[:, kt + k, :], g_lo[:, kt + k, :]
                        else:
                            rh, rl = flat(g_hi[:, cols(kt + k), :]), flat(g_lo[:, cols(kt + k), :])
                        i = matmul3(bank[m][:, :], wh[:, k, m * P:(m + 1) * P], wl[:, k, m * P:(m + 1) * P], rh, rl,
                                    first and k == 0, last and k == 1)
                        if last and k == 1 and m < KT - 1:
                            i.then_inc(tile_ready.sem, 1)
                    i.then_inc(chunk_done[s].sem, 1)
                    if last:
                        norm(L, 4 * f + 1)

                down(c1 % 2, c1 // 2 + 1, 0, True, False)
                with pe.Fori(0, FT // 4 - 1) as j:
                    for half in range(2):
                        cc = c1 + 1 + half
                        down(cc % 2, cc // 2 + j + 1, j * 4 + 2 + 2 * half, False, False)
                for d in (FT // 2 - 2, FT // 2 - 1):
                    down((c1 + d) % 2, (c1 + d) // 2 + 1, 2 * d, False, d == FT // 2 - 1)

            def bank_free(L, t):
                last = t.before
                if last is not None and last.engine == "sub":
                    pe.wait_ge(y_copied.sem, y_copied.of(L, KT + last.emptied))
                elif last is not None:
                    pe.wait_ge(emptied[last.engine].sem, emptied[last.engine].of(L, last.emptied))

            def chunk_tile(L, name, k, src=None):
                ch = CHUNK_OF[name]
                s = ch % 2
                if k == 0:
                    pe.wait_ge(lo_split[s].sem, slot_value(lo_split[s], L, ch))
                t = TILES[name, k]
                bank_free(L, t)
                hi, lo, n, ready = src or (u_hi, u_lo, KT, None)
                w = 512 if n == 4 else chunk_widths(name)
                wh = w_hi[s][:, 0:n * w].rearrange("p (k n) -> p k n", k=n)
                wl = w_lo[s][:, 0:n * w].rearrange("p (k n) -> p k n", k=n)
                for kt in range(n):
                    if k == 0 and ready is not None:
                        pe.wait_ge(split_lo.sem, split_lo.of(L, ready + kt + 1))
                    elif k == 0 and name == "su0":
                        pe.wait_ge(u_ready.sem, u_ready.of(L, KT + kt + 1))
                    m = matmul3(bank[t.bank][:, :], wh[:, kt, k * P:(k + 1) * P], wl[:, kt, k * P:(k + 1) * P],
                                hi[:, kt, :], lo[:, kt, :], kt == 0, kt == n - 1)
                m.then_inc(chunk_done[s].sem if t.last else tile_ready.sem, 1)

            def value_tile(L, name, k):
                ch = CHUNK_OF[name]
                s = ch % 2
                if k == 0:
                    pe.wait_ge(lo_split[s].sem, slot_value(lo_split[s], L, ch))
                t = TILES[name, k]
                bank_free(L, t)
                wh = w_hi[s][:, :].rearrange("p (k n) -> p k n", k=KT)
                wl = w_lo[s][:, :].rearrange("p (k n) -> p k n", k=KT)
                for half in range(2):
                    b = 2 * k + half
                    dst = bank[t.bank][:, half * 256:(half + 1) * 256]
                    tok = slice(b * P, (b + 1) * P)
                    for kt in range(KT):
                        pe.matmul(dst, u_hi[:, kt, tok], wh[:, kt, :], start=kt == 0, stop=False)
                        pe.matmul(dst, u_lo[:, kt, tok], wh[:, kt, :], start=False, stop=False)
                        m = pe.matmul(dst, u_hi[:, kt, tok], wl[:, kt, :], start=False, stop=kt == KT - 1)
                m.then_inc(chunk_done[s].sem if t.last else tile_ready.sem, 1)

            def s5_matrices(L):
                pe.wait_ge(s5_bx_ready.sem, s5_bx_ready.of(L, 1))
                for i in range(2):
                    for q in range(4):
                        m = pe.transpose(bank[4 + i][:, q * P:(q + 1) * P],
                                         s5_bx[:, i, q].rearrange("p a g h -> p (a g h)"), ident[:, :])
                m.then_inc(s5_turned.sem, 1)
                pe.wait_ge(s5w_loaded.sem, s5w_loaded.of(L, 16 * 6))
                for i in range(2):
                    for q in range(4):
                        m = pe.transpose(bank[6 + i][:, q * P:(q + 1) * P],
                                         s5_cd[:, i, q].rearrange("p a n -> p (a n)"), ident[:, :])
                m.then_inc(s5_turned.sem, 1)

            def s5_in(L, j):
                q, i = divmod(j, 4)
                if j == 0:
                    pe.wait_ge(s5_mats_ready.sem, s5_mats_ready.of(L, 1))
                else:
                    pe.wait_ge(front_done.sem, front_done.of(L, j))
                t = TILES[("su0", q) if q < 2 else (f"su{q - 1}", 0)]
                pe.wait_ge(emptied["act"].sem, emptied["act"].of(L, t.emptied))
                rows = slice(32 * i, 32 * i + 32)
                for part in range(2):
                    m = pe.matmul(bank[4 + part][:, :], s5_bt[rows, part, q, :], su[rows, q, :], start=True, stop=True)
                m.then_inc(bu_ready.sem, 1)

            def s5_out(L, j):
                q, i = divmod(j, 4)
                if i == 0 and q >= 2:
                    pe.wait_ge(s5_y_summed.sem, s5_y_summed.of(L, q - 1))
                pe.wait_ge(state_ready.sem, state_ready.of(L, 2 * j + 2))
                for part in range(2):
                    m = pe.matmul(bank[6 + q % 2][32 * i:32 * i + 32, :], s5_ct[:, part, q, 32 * i:32 * i + 32],
                                  rot[j % 3][:, part, :], start=part == 0, stop=part == 1)
                m.then_inc(s5_y_ready.sem, 1)

            def gla_alpha(L):
                pe.wait_ge(alpha_loaded.sem, alpha_loaded.of(L, 16))
                pe.wait_ge(emptied["act"].sem, emptied["act"].of(L, TILES["ga", 0].emptied))
                for t in range(2):
                    pe.matmul(bank[4 + t][:, :], w_alpha[:, t * P:(t + 1) * P], a_low[:, :], start=True, stop=True)\
                      .then_inc(alpha_ready.sem, 1)

            def gla_turn_keys(L):
                pe.wait_ge(gla_keys.sem, gla_keys.of(L, 6))
                for b in range(TB):
                    for t in range(2):
                        m = pe.transpose(bank[4 + b // 2][:, (b % 2) * 256 + t * P:(b % 2) * 256 + (t + 1) * P],
                                         gk[:, t, b * P:(b + 1) * P], ident[:, :])
                m.then_inc(kk_turned.sem, 1)

            def gla_states(L, t):
                if t == 0:
                    pe.wait_ge(kk_copied.sem, kk_copied.of(L, 2))
                else:
                    pe.wait_ge(s_ready.sem, s_ready.of(L, 1))
                pe.sem_inc(states_begun.sem, 1)
                for n in range(N_GCH - 1):
                    b, rows = n // 2, slice(64 * (n % 2), 64 * (n % 2) + 64)
                    for par in range(2):
                        hd = 2 * t + par
                        m = pe.matmul(bank[6 + n % 2][64 * par:64 * par + 64, (n // 2) * P:(n // 2 + 1) * P],
                                      kk_tok[rows, b, t * P + 64 * par:t * P + 64 * par + 64],
                                      gv[rows, b, hd * P:(hd + 1) * P], start=True, stop=True)
                m.then_inc(ds_ready.sem, 1)

            def gla_scores(L, hd):
                t, par = divmod(hd, 2)
                rows = slice(64 * par, 64 * par + 64)
                if hd == 0:
                    pe.wait_ge(kk_copied.sem, kk_copied.of(L, 2))
                else:
                    pe.wait_ge(att_clamped.sem, att_clamped.of(L, hd))
                for b in range(TB):
                    blk = slice(b * P, (b + 1) * P)
                    m = pe.matmul(bank[4][:, blk], la[rows, t, blk], gq[rows, t, blk], start=True, stop=True)
                m.then_inc(att_ready.sem, 1)

            def head_ms(L, hh, bk):
                pe.wait_ge(o_squared.sem, o_squared.of(L, hh + 1))
                pe.wait_ge(o_copied.sem, o_copied.of(L, hh + 1))
                for b in range(TB):
                    m = pe.matmul(bank[bk][:, b:b + 1], o_sq[:, b * P:(b + 1) * P], inv_d[:, 1:2], start=True, stop=True)
                m.then_inc(o_ms.sem, 1)

            def gla_out(L, hd):
                t, par = divmod(hd, 2)
                rows = slice(64 * par, 64 * par + 64)
                bk = 6 + hd % 2
                pe.wait_ge(att_clamped.sem, att_clamped.of(L, hd + 1))
                pe.wait_ge(s_ready.sem, s_ready.of(L, 2))
                if hd >= 2:
                    pe.wait_ge(o_ms_kept.sem, o_ms_kept.of(L, hd - 1))
                for b in range(TB):
                    pe.matmul(bank[bk][:, b * P:(b + 1) * P], gv[:, b, hd * P:(hd + 1) * P], att[:, hd % 2, b, :],
                              start=True, stop=False)
                    for n in (2 * b, 2 * b + 1):
                        if n:
                            tok = slice(n * GLA_CHUNK, (n + 1) * GLA_CHUNK)
                            m = pe.matmul(bank[bk][:, tok], s_state[rows, t, n, :], gq[rows, t, tok], start=False, stop=n % 2 == 1)
                m.then_inc(o_ready.sem, 1)

            def head_rstd(L, hh, bk):
                pe.wait_ge(o_inverse.sem, o_inverse.of(L, hh // 4 + 1))
                if hh % 4 >= 2:
                    pe.wait_ge(o_normed.sem, o_normed.of(L, hh - 1))
                spread(bank[bk], 4 * (hh % 4)).then_inc(o_rstd.sem, 1)

            def diff_scores(L, hd, qb):
                i = hd * TB + qb
                n = (qb + 1) * P
                if i == 0:
                    pe.wait_ge(o_normed.sem, o_normed.of(L, 4))
                else:
                    pe.wait_ge(max_ready.sem, max_ready.of(L, i))
                for par in range(2):
                    rows = slice(64 * par, 64 * par + 64)
                    pe.matmul(bank[4 + par][:, 0:n], dq[rows, hd, qb * P:(qb + 1) * P], dk[rows, hd, 0:n],
                              start=True, stop=True).then_inc(scores_ready.sem, 1)

            def diff_turn(L, hd, qb):
                i = hd * TB + qb
                pe.wait_ge(mix_ready.sem, mix_ready.of(L, i + 1))
                if i:
                    pe.wait_ge(at_copied.sem, at_copied.of(L, i))
                for j in range(qb + 1):
                    m = pe.transpose(bank[6][:, j * P:(j + 1) * P], prob[i % 2][:, 0, j * P:(j + 1) * P], ident[:, :])
                m.then_inc(at_ready.sem, 1)

            def diff_out(L, hd):
                pe.wait_ge(at_copied.sem, at_copied.of(L, (hd + 1) * TB))
                pe.wait_ge(o_ms_kept.sem, o_ms_kept.of(L, 4 + hd))
                for j in range(TB):
                    m = pe.matmul(bank[7][:, j * P:SEQ], dv[:, j, hd * P:(hd + 1) * P], a_t[:, j, j * P:SEQ],
                                  start=j == 0, stop=j == TB - 1)
                m.then_inc(o_ready.sem, 1)

            def mixer(L):
                for name, n, _ in MIXER[:3]:
                    for k in range(n):
                        chunk_tile(L, name, k)
                s5_matrices(L)
                s5_in(L, 0)
                done = 0
                gaps = 0
                for name, n, _ in MIXER[3:14]:
                    for k in range(n):
                        (value_tile if name[:2] == "gv" else chunk_tile)(L, name, k)
                        gaps += 1
                        while done < min(S5_PAIRS, (gaps * S5_PAIRS) // S5_PACE):
                            if done + 1 < S5_PAIRS:
                                s5_in(L, done + 1)
                            if done >= 2:
                                s5_out(L, done - 2)
                            done += 1
                        if gaps in (S5_PACE, S5_PACE + 1):
                            s5_out(L, S5_PAIRS - 2 + gaps - S5_PACE)
                for name in ("glu1", "glu0"):
                    for k in range(4):
                        chunk_tile(L, name, k, (yg_hi, yg_lo, 4, YG))
                for name in ("bs0", "bs1"):
                    for k in range(4):
                        chunk_tile(L, name, k, (ys_hi, ys_lo, 4, YS))
                gla_alpha(L)
                for k in range(2):
                    chunk_tile(L, "dq0", k)
                for k in range(2):
                    chunk_tile(L, "dq1", k)
                gla_turn_keys(L)
                for k in range(2):
                    chunk_tile(L, "dk0", k)
                gla_states(L, 0)
                gla_scores(L, 0)
                for k in range(2):
                    chunk_tile(L, "dk1", k)
                gla_states(L, 1)
                gla_scores(L, 1)
                value_tile(L, "dv0", 0)
                for hd in range(GLA_HEADS):
                    gla_out(L, hd)
                    if hd + 2 < GLA_HEADS:
                        gla_scores(L, hd + 2)
                    if hd < 3:
                        value_tile(L, *(("dv0", 1), ("dv1", 0), ("dv1", 1))[hd])
                    head_ms(L, hd, 6 + hd % 2)
                for k in range(2):
                    chunk_tile(L, "gg0", k)
                for hd in range(GLA_HEADS):
                    head_rstd(L, hd, 4 + hd % 2)
                diff_scores(L, 0, 0)
                for i in range(DIFF_HEADS * TB):
                    hd, qb = divmod(i, TB)
                    if i + 1 < DIFF_HEADS * TB:
                        diff_scores(L, *divmod(i + 1, TB))
                    for name, k in BESIDE_DIFF[i]:
                        chunk_tile(L, name, k, (yga_hi, yga_lo, 4, YGA) if name[0] == "b" else None)
                    diff_turn(L, hd, qb)
                    if qb == TB - 1:
                        diff_out(L, hd)
                        head_ms(L, 4 + hd, 7)
                for k in range(2):
                    chunk_tile(L, "gd1", k)
                for hd in range(DIFF_HEADS):
                    head_rstd(L, 4 + hd, 4 + hd % 2)
                for name, n in (("gd2", 2), ("gd3", 2), ("bd0", 4), ("bd1", 4)):
                    for k in range(n):
                        chunk_tile(L, name, k, (yd_hi, yd_lo, 4, YD) if name[0] == "b" else None)
                for name, n, _ in MIXER[36:]:
                    for k in range(n):
                        chunk_tile(L, name, k, (mg_hi, mg_lo, 8, MG))
                norm(L, 3)

            pe.wait_ge(const_ready, 4)
            pe.wait_ge(c_loaded, 16)
            pe.transpose(bank[7][:, 0:KT], c_row[:, :], ident[0:KT, 0:KT]).then_inc(c_turned, 1)
            pe.wait_ge(x_loaded, 16)
            for m in range(6):
                for b in range(TB):
                    i = pe.transpose(bank[m][:, b * P:(b + 1) * P], x_tok[:, b, m * P:(m + 1) * P], ident[:, :])
                i.then_inc(x_turned, 1)
            pe.wait_ge(line_loaded, 32)
            for m in range(6, 8):
                pe.wait_ge(h_ready.sem, m - 5)
                for b in range(TB):
                    i = pe.transpose(bank[m - 6][:, b * P:(b + 1) * P], x_tok[:, b, m * P:(m + 1) * P], ident[:, :])
                i.then_inc(x_turned, 1)
            pe.matmul(bank[6][0:N_MAPS, :], rel33[:, :], onehot[:, 0:SEQ], start=True, stop=True).then_inc(line_made, 1)
            pe.wait_ge(cond_ready, 1)
            pe.matmul(bank[7][0:N_MAPS, 0:P], rel33[:, :], onehot[:, SEQ:LINE], start=True, stop=True).then_inc(line_made, 1)
            pe.wait_ge(line_copied, 2)
            pe.wait_ge(rows_loaded, 16 * 10 * DEPTH)
            for l in range(DEPTH):
                pe.transpose(bank[6][:, l * V_LOADED:l * V_LOADED + 72], rows_a[l][:, :], ident[0:72, 0:72])
                i = pe.transpose(bank[6][:, l * V_LOADED + 72:(l + 1) * V_LOADED], rows_b[l][:, :],
                                 ident[0:V_LOADED - 72, 0:V_LOADED - 72])
            i.then_inc(rows_turned, 1)
            with pe.Fori(0, ADA_THIRD // 6) as i:
                for s in range(6):
                    pe.wait_ge(first_ada_loaded[s], i * 16 + 16)
                    for t in range(2):
                        for k in range(KT):
                            m = pe.matmul(bank[7][:, bass.ds(i * 12 + (2 * s + t), 1)], first_ada_w[s][:, k, t * P:(t + 1) * P],
                                          cond[:, k:k + 1], start=k == 0, stop=k == KT - 1)
                    m.then_inc(ada_column.sem, 1)

            with pe.Fori(0, DEPTH) as L:
                norm(L, 0)
                ffn(L, 0, 0)
                norm(L, 2)
                mixer(L)
                norm(L, 4)
                ffn(L, 1, C_FFN2)

            pe.wait_ge(h_ready.sem, h_ready.of(DEPTH, 0))
            for b in range(TB):
                for m in range(KT):
                    i = pe.transpose(bank[2 * b + m // 4][:, (m % 4) * P:(m % 4 + 1) * P], h[:, m, b * P:(b + 1) * P], ident[:, :])
                    if m % 4 == 3:
                        i.then_inc(out_turned, 1)

        @block.scalar
        def _(act):
            for s in range(2):
                act.sem_inc(hi_split[s].sem, 1)
            act.sem_inc(silu_done.sem, 2)

            def split(L, s, n, elems=CHUNK_ELEMS):
                act.wait_ge(raw_loaded[s].sem, raw_loaded[s].of(L, 16 * n))
                act.wait_ge(chunk_done[s].sem, chunk_done[s].of(L, n - 1))
                act.activation(w_hi[s][:, 0:elems], raw[s][:, 0:elems], ACT.Copy).then_inc(hi_split[s].sem, 1)

            def split_chunk(L, name):
                ch = CHUNK_OF[name]
                split(L, ch % 2, ch // 2 + 1, KT * P if chunk_widths(name) == P else CHUNK_ELEMS)

            def root(L, r):
                act.wait_ge(ms_ready.sem, ms_ready.of(L, r + 1))
                act.activation(sq_root[:, 0:TB], bank[MS_BANK[r]][:, 0:TB], ACT.Sqrt, bias=EPS_COL).then_inc(root_ready.sem, 1)

            def h_squares(L, ui):
                r = 2 * ui
                for m in range(KT):
                    act.wait_ge(h_ready.sem, h_ready.of(L, (ui - 1) * KT + m + 1))
                    act.wait_ge(sq_summed.sem, sq_summed.of(L, KT * r + m - 2))
                    act.activation(sq_buf[:, m % 3, :], h[:, m, :], ACT.Square).then_inc(sq_ready.sem, 1)
                root(L, r)

            def modulate(L, ui):
                for m in range(KT):
                    act.wait_ge(modulated.sem, modulated.of(L, ui * KT + m + 1))
                    act.activation(u_hi[:, m, :], mod_buf[:, m % 2, :], ACT.Identity,
                                   bias=ada[:, 24 * ui + m:24 * ui + m + 1]).then_inc(u_hi_ready.sem, 1)

            def y_tile(L, ui, m, bk, wait):
                r = 2 * ui + 1
                wait()
                act.wait_ge(sq_summed.sem, sq_summed.of(L, KT * r + m - 2))
                act.activation(sq_buf[:, m % 3, :], bank[bk][:, :], ACT.Square).then_inc(sq_ready.sem, 1)
                act.activation(y_sub[:, m, :], bank[bk][:, :], ACT.Copy).then_inc(y_copied.sem, 1)

            def ffn(L, f, c0):
                i0 = f * FT
                with act.Fori(0, FT // 2) as j:
                    split(L, c0 % 2, (c0 + 2) // 2 + j + 1)
                    for mt in range(2):
                        i = i0 + 2 * j + mt
                        if mt:
                            s = c0 % 2
                            act.wait_ge(chunk_done[s].sem, chunk_done[s].of(L, c0 // 2 + j + 1))
                        else:
                            act.wait_ge(tile_ready.sem, tile_ready.of(L, f * READY_BEFORE_FFN2 + 2 * j + 1))
                        act.wait_ge(g_lo_ready.sem, g_lo_ready.of(L, i - 1))
                        act.activation(silu_buf[:, mt, :], bank[mt][:, :], ACT.Silu).then_inc(silu_done.sem, 1)
                    for mt in range(2):
                        i = i0 + 2 * j + mt
                        act.wait_ge(prod_done.sem, prod_done.of(L, i + 1))
                        act.activation(flat(g_hi[:, cols(j * 2 + mt), :]), silu_buf[:, mt, :], ACT.Copy).then_inc(g_hi_ready.sem, 1)
                    split(L, (c0 + 1) % 2, (c0 + 3) // 2 + j + 1)
                c1 = c0 + FT
                split(L, c1 % 2, (c1 + 2) // 2 + 1)
                with act.Fori(0, (FT // 2 - 3) // 2) as j:
                    for half in range(2):
                        cc = c1 + 3 + half
                        split(L, cc % 2, cc // 2 + j + 1)
                if f == 0:
                    split_chunk(L, "su0")
                s = (c1 + FT // 2 - 1) % 2
                for m in range(KT):
                    def wait():
                        if m < KT - 1:
                            act.wait_ge(tile_ready.sem, tile_ready.of(L, f * READY_BEFORE_FFN2 + FT + m + 1))
                        else:
                            act.wait_ge(chunk_done[s].sem, slot_value(chunk_done[s], L, c1 + FT // 2 - 1))
                    y_tile(L, 2 * f, m, m, wait)
                root(L, 4 * f + 1)

            def tile_wait(L, name, k):
                t = TILES[name, k]
                if t.last:
                    s = t.chunk % 2
                    act.wait_ge(chunk_done[s].sem, slot_value(chunk_done[s], L, t.chunk))
                else:
                    act.wait_ge(tile_ready.sem, tile_ready.of(L, t.ready))
                return bank[t.bank]

            def empty(L, name, k):
                b = tile_wait(L, name, k)
                i = int(name[-1]) if name[-1].isdigit() else 0
                kind = name[:2]
                if kind == "su":
                    q = k if i == 0 else i + 1
                    ins = act.activation(su[:, q, :], b[:, :], ACT.Copy)
                elif kind in ("gq", "gk"):
                    ins = act.activation((gq if kind == "gq" else gk)[:, k, :], b[:, :], ACT.Copy)
                elif kind == "ga":
                    ins = act.activation(a_low[:, :], b[0:LOWRANK, :], ACT.Copy)
                elif kind in ("gv", "dv"):
                    dst = (gv if kind == "gv" else dv)[:, 2 * k:2 * k + 2, i * 256:(i + 1) * 256]
                    ins = act.activation(dst, b[:, :].rearrange("p (a n) -> p a n", a=2), ACT.Copy)
                elif kind == "gr":
                    ins = act.activation(gr[:, 2 * i + k, :], b[:, :], ACT.Silu)
                elif kind == "gs":
                    ins = act.activation(merged[:, 2 * i + k, :], b[:, :], ACT.Sigmoid)
                elif kind == "gl":
                    ins = act.activation(z_gate[:, k, :], b[:, :], ACT.Sigmoid, bias=vec[:, V_BGLU + 4 + k:V_BGLU + 5 + k])
                elif kind == "dq":
                    ins = act.activation(dq[:, 2 * i + k, :], b[:, :], ACT.Copy, scale=0.125)
                elif kind == "dk":
                    ins = act.activation(dk[:, 2 * i + k, :], b[:, :], ACT.Copy)
                else:
                    t4 = (2 * i + k) % 4
                    n = {"gg": 0, "gd": 8}[kind] + (2 * i + k)
                    if 4 <= n < 12:
                        act.wait_ge(merged_ready.sem, merged_ready.of(L, n - 3))
                    ins = act.activation((sig if n < 12 else sig_late)[:, t4, :], b[:, :], ACT.Sigmoid)
                ins.then_inc(emptied["act"].sem, 1)

            def make_tables(L, j):
                act.wait_ge(turns_ready.sem, turns_ready.of(L, j + 1))
                if j >= 3:
                    act.wait_ge(back_done.sem, back_done.of(L, j - 2))
                act.activation(tab_s[:, j % 3, :], turns[:, j % 2, :], ACT.Sin, scale=6.283185)
                st.did(act.activation(turns[:, j % 2, :], turns[:, j % 2, :], ACT.Abs))
                st.wait()
                act.activation(tab_c[:, j % 3, :], turns[:, j % 2, :], ACT.Sin, scale=-6.283185, bias=HALF_PI)\
                   .then_inc(tables_ready.sem, 1)

            def split_tile(L, base, k, dst, src):
                act.activation(dst[:, k, :], src, ACT.Copy).then_inc(split_hi.sem, 1)

            def head_squares(L, hh, bk):
                act.wait_ge(o_ready.sem, o_ready.of(L, hh + 1))
                dst = o_head[hh][:, :] if hh < 4 else dq[:, hh - 4, :]
                act.activation(dst, bank[bk][:, :], ACT.Copy).then_inc(o_copied.sem, 1)
                if hh:
                    act.wait_ge(o_ms.sem, o_ms.of(L, hh))
                act.activation(o_sq[:, :], bank[bk][:, :], ACT.Square).then_inc(o_squared.sem, 1)

            def head_roots(L, g):
                act.wait_ge(o_ms_kept.sem, o_ms_kept.of(L, 4 * g + 4))
                act.activation(sq_root[:, 0:16], ms_heads[:, :], ACT.Sqrt, bias=EPS_COL).then_inc(o_roots.sem, 1)

            def diff_exp(L, i):
                hd, qb = divmod(i, TB)
                n = (qb + 1) * P
                act.wait_ge(max_ready.sem, max_ready.of(L, i + 1))
                sm = smax[:, i % 2, :]
                for par in range(2):
                    ins = act.activation(prob[i % 2][:, par, 0:n], prob[i % 2][:, par, 0:n], ACT.Exp, bias=sm[:, 2 + par:3 + par],
                                         accum_out=sm[:, 4 + par:5 + par])
                    st.did(ins) if par == 0 else ins.then_inc(prob_ready.sem, 1)
                st.wait()

            def diff_copy(L, i):
                hd, qb = divmod(i, TB)
                act.wait_ge(at_ready.sem, at_ready.of(L, i + 1))
                if qb == 0 and hd:
                    act.wait_ge(o_ready.sem, o_ready.of(L, 4 + hd))
                act.activation(a_t[:, 0:qb + 1, qb * P:(qb + 1) * P],
                               bank[6][:, 0:(qb + 1) * P].rearrange("p (a n) -> p a n", n=P), ACT.Copy).then_inc(at_copied.sem, 1)

            act.wait_ge(c_turned, 1)
            act.activation(cond[:, :], bank[7][:, 0:KT], ACT.Silu).then_inc(cond_ready, 1)
            act.wait_ge(line_made, 2)
            act.activation(bias_line[:, 0:SEQ], bank[6][0:N_MAPS, :], ACT.Copy).then_inc(line_copied, 1)
            act.activation(bias_line[:, SEQ:LINE], bank[7][0:N_MAPS, 0:P], ACT.Copy).then_inc(line_copied, 1)

            act.wait_ge(theta_ready, 1)
            act.activation(pscr[:, 8], pscr[:, 3], ACT.Sin).then_inc(sines_ready, 1)
            act.activation(pscr[:, 9], pscr[:, 3], ACT.Sin, scale=0.5).then_inc(sines_ready, 1)
            act.wait_ge(lam_sums, 2 * DEPTH)
            act.activation(small[:, 8:8 + 2 * DEPTH], small[:, 0:2 * DEPTH], ACT.Exp).then_inc(lam_exps, 1)

            with act.Fori(0, DEPTH) as L:
                st = Steps(act, scalar_steps, L)
                split(L, 0, 1)
                h_squares(L, 0)
                split(L, 1, 1)
                modulate(L, 0)
                ffn(L, 0, 0)
                h_squares(L, 1)
                split_chunk(L, "su1")
                modulate(L, 1)
                for i in range(3):
                    if i:
                        split_chunk(L, MIXER[i + 1][0])
                    for k in range(MIXER[i][1]):
                        empty(L, MIXER[i][0], k)
                make_tables(L, 0)
                make_tables(L, 1)
                done = 0
                gaps = 0
                for i in range(3, 14):
                    name, n, _ = MIXER[i]
                    split_chunk(L, MIXER[i + 1][0])
                    for k in range(n):
                        if gaps < S5_SIDE_TILES - 1:
                            empty(L, name, k)
                        gaps += 1
                        while done < min(S5_PAIRS, (gaps * S5_PAIRS) // S5_PACE):
                            if done + 2 < S5_PAIRS:
                                make_tables(L, done + 2)
                            done += 1
                split_chunk(L, "glu0")
                for q in range(4):
                    act.wait_ge(s5_y_summed.sem, s5_y_summed.of(L, q + 1))
                    act.activation(su[:, q, :], su[:, q, :], ACT.Gelu_apprx_tanh).then_inc(gelu_done.sem, 1)
                empty(L, "gs3", 1)
                for q in range(4):
                    act.wait_ge(gelu_done.sem, gelu_done.of(L, q + 1))
                    split_tile(L, YG, q, yg_hi, su[:, q, :])
                for k in range(4):
                    act.wait_ge(split_lo.sem, split_lo.of(L, YG + k + 1))
                    empty(L, "glu1", k)
                split_chunk(L, "bs0")
                for q in range(4):
                    act.wait_ge(emptied["vec"].sem, emptied["vec"].of(L, TILES["glu0", q].emptied))
                    split_tile(L, YS, q, ys_hi, z_gate[:, q, :])
                split_chunk(L, "bs1")
                split_chunk(L, "dq0")
                for t in range(2):
                    act.wait_ge(alpha_read.sem, alpha_read.of(L, t + 1))
                    st.did(act.activation(la[:, t, :], bank[4 + t][:, :], ACT.Abs, bias=vec[:, V_BALPHA + t:V_BALPHA + t + 1]))
                st.wait()
                st.did(act.activation(la[:, :, :], la[:, :, :], ACT.Exp, scale=-1.0))
                st.wait()
                act.activation(la[:, :, :], la[:, :, :], ACT.Ln, bias=1.0).then_inc(alpha_exps.sem, 1)
                split_chunk(L, "dq1")
                for t in range(2):
                    act.wait_ge(decay_sum.sem, decay_sum.of(L, t + 1))
                    act.activation(eb[:, t, :], lb[:, t, :], ACT.Exp, scale=1.0 / GLA_TAU).then_inc(gla_exps.sem, 1)
                    act.activation(la[:, t, :], lb[:, t, :], ACT.Exp, scale=-1.0 / GLA_TAU).then_inc(gla_exps.sem, 1)
                for t in range(2):
                    act.wait_ge(decay_last.sem, decay_last.of(L, t + 1))
                    act.activation(lb[:, t, :], lb[:, t, :], ACT.Exp, scale=1.0 / GLA_TAU).then_inc(gla_exps.sem, 1)
                for k in range(2):
                    empty(L, "dq0", k)
                split_chunk(L, "dk0")
                for k in range(2):
                    empty(L, "dq1", k)
                act.wait_ge(kk_turned.sem, kk_turned.of(L, 1))
                for i in range(2):
                    act.activation(kk_tok[:, 2 * i:2 * i + 2, :], bank[4 + i][:, :].rearrange("p (a n) -> p a n", a=2),
                                   ACT.Copy).then_inc(kk_copied.sem, 1)
                split_chunk(L, "dk1")
                for k in range(2):
                    empty(L, "dk0", k)
                split_chunk(L, "dv0")
                for k in range(2):
                    empty(L, "dk1", k)
                split_chunk(L, "dv1")
                empty(L, "dv0", 0)
                for hd in range(GLA_HEADS):
                    head_squares(L, hd, 6 + hd % 2)
                    if hd < 3:
                        empty(L, *(("dv0", 1), ("dv1", 0), ("dv1", 1))[hd])
                    if hd == 1:
                        split_chunk(L, "gg0")
                head_roots(L, 0)
                split_chunk(L, "gg1")
                for k in range(2):
                    empty(L, "gg0", k)
                act.wait_ge(yga_done.sem, yga_done.of(L, 4))
                for k in range(4):
                    split_tile(L, YGA, k, yga_hi, gr[:, k, :])
                splits = {0: "bg0", 2: "gg2", 6: "gg3", 8: "bg1", 10: "gd0", 14: "gd1"}
                diff_exp(L, 0)
                for i in range(DIFF_HEADS * TB):
                    hd, qb = divmod(i, TB)
                    if i in splits:
                        split_chunk(L, splits[i])
                    if i + 1 < DIFF_HEADS * TB:
                        diff_exp(L, i + 1)
                    for name, k in BESIDE_DIFF[i]:
                        if name[0] == "g":
                            empty(L, name, k)
                    diff_copy(L, i)
                    if qb == TB - 1:
                        head_squares(L, 4 + hd, 7)
                head_roots(L, 1)
                split_chunk(L, "gd2")
                for k in range(2):
                    empty(L, "gd1", k)
                split_chunk(L, "gd3")
                for k in range(4):
                    act.wait_ge(o_normed.sem, o_normed.of(L, 4 + k + 1))
                    if k == 0:
                        t = TILES["bg1", 3]
                        act.wait_ge(chunk_done[t.chunk % 2].sem, slot_value(chunk_done[t.chunk % 2], L, t.chunk))
                    split_tile(L, YD, k, yd_hi, dq[:, k, :])
                for k in range(2):
                    empty(L, "gd2", k)
                split_chunk(L, "bd0")
                for k in range(2):
                    empty(L, "gd3", k)
                split_chunk(L, "bd1")
                split_chunk(L, "wo0")
                for m in range(KT):
                    act.wait_ge(merged_ready.sem, merged_ready.of(L, 8 + m + 1))
                    if m == 0:
                        act.wait_ge(split_lo.sem, split_lo.of(L, YD + 4))
                    split_tile(L, MG, m, mg_hi, merged[:, m, :])
                split_chunk(L, "wo1")
                for i in range(4):
                    if i >= 1 and i + 1 < 4:
                        split_chunk(L, f"wo{i + 1}")
                    if i == 3:
                        split(L, C_FFN2 % 2, C_FFN2 // 2 + 1)
                    for k in range(2):
                        t = TILES[f"wo{i}", k]
                        y_tile(L, 1, 2 * i + k, t.bank, lambda: tile_wait(L, f"wo{i}", k))
                root(L, 3)
                h_squares(L, 2)
                split(L, (C_FFN2 + 1) % 2, (C_FFN2 + 1) // 2 + 1)
                modulate(L, 2)
                ffn(L, 1, C_FFN2)
                assert st.n == SCALAR_STEPS, st.n

            for b in range(TB):
                act.wait_ge(out_turned, 2 * b + 1)
                act.activation(x_tok[:, b, 0:SEQ], bank[2 * b][:, :], ACT.Copy).then_inc(out_half, 1)

        @block.vector
        def _(v):
            for s in range(2):
                v.sem_inc(lo_split[s].sem, 1)
            v.sem_inc(prod_done.sem, 2)
            v.sem_inc(g_lo_ready.sem, 2)
            v.sem_inc(ada_step.sem, 3 * KT)

            def stt(o, a, s, b, op0, op1):
                return v.scalar_tensor_tensor(out=o, in0=a, scalar=s, in1=b, op0=op0, op1=op1)

            MUL, ADD, SUB = ALU.mult, ALU.add, ALU.subtract

            def split(L, s, n):
                v.wait_ge(hi_split[s].sem, hi_split[s].of(L, n))
                v.tensor_tensor(w_lo[s][:, :], raw[s][:, :], w_hi[s][:, :].bitcast(F32), SUB).then_inc(lo_split[s].sem, 1)

            def rstd(L, r):
                v.wait_ge(root_ready.sem, root_ready.of(L, r + 1))
                v.reciprocal(rstd_tok[:, 0:TB], sq_root[:, 0:TB]).then_inc(inverse_ready.sem, 1)
                v.wait_ge(rstd_ready.sem, rstd_ready.of(L, r + 1))

            def modulate(L, ui):
                rstd(L, 2 * ui)
                for m in range(KT + 1):
                    if m < KT:
                        if m >= 2:
                            v.wait_ge(u_ready.sem, u_ready.of(L, ui * KT + m - 1))
                        stt(mod_buf[:, m % 2, :], h[:, m, :], pre_gain[:, KT * ui + m:KT * ui + m + 1], bank[MS_BANK[2 * ui] + 1][:, :],
                            MUL, MUL).then_inc(modulated.sem, 1)
                    if m:
                        i = m - 1
                        v.wait_ge(u_hi_ready.sem, u_hi_ready.of(L, ui * KT + i + 1))
                        stt(u_lo[:, i, :], mod_buf[:, i % 2, :], ada[:, 24 * ui + i:24 * ui + i + 1],
                            u_hi[:, i, :].bitcast(F32), ADD, SUB).then_inc(u_ready.sem, 1)

            def post(L, ui):
                rstd(L, 2 * ui + 1)
                for m in range(KT + 1):
                    if m < KT:
                        v.wait_ge(y_copied.sem, y_copied.of(L, ui * KT + m + 1))
                        st.did(stt(y_sub[:, m, :], y_sub[:, m, :], post_gain[:, KT * ui + m:KT * ui + m + 1], bank[MS_BANK[2 * ui + 1] + 1][:, :], MUL, MUL))
                    if m:
                        st.wait(back=1 if m < KT else 0)
                        v.tensor_tensor(h[:, m - 1, :], h[:, m - 1, :], y_sub[:, m - 1, :], ADD).then_inc(h_ready.sem, 1)

            def ffn(L, f, c0):
                i0 = f * FT

                def up(j, with_ada):
                    if with_ada:
                        for s in range(3):
                            ada_chunk(L, f, j, s)
                    split(L, c0 % 2, (c0 + 2) // 2 + j + 1)
                    for mt in range(2):
                        i = i0 + 2 * j + mt
                        v.wait_ge(silu_done.sem, silu_done.of(L, i + 1))
                        if mt:
                            s = (c0 + 1) % 2
                            v.wait_ge(chunk_done[s].sem, chunk_done[s].of(L, (c0 + 1) // 2 + j + 1))
                        else:
                            v.wait_ge(tile_ready.sem, tile_ready.of(L, f * READY_BEFORE_FFN2 + 2 * j + 2))
                        v.tensor_tensor(silu_buf[:, mt, :], silu_buf[:, mt, :], bank[2 + mt][:, :], MUL).then_inc(prod_done.sem, 1)
                    for mt in range(2):
                        i = i0 + 2 * j + mt
                        v.wait_ge(g_hi_ready.sem, g_hi_ready.of(L, i + 1))
                        v.tensor_tensor(flat(g_lo[:, cols(j * 2 + mt), :]), silu_buf[:, mt, :],
                                        flat(g_hi[:, cols(j * 2 + mt), :]).bitcast(F32), SUB).then_inc(g_lo_ready.sem, 1)
                    split(L, (c0 + 1) % 2, (c0 + 3) // 2 + j + 1)

                with v.Fori(0, ADA_ROUNDS[f]) as j:
                    up(j, True)
                ada_keep(L, f)
                with v.Fori(ADA_ROUNDS[f], FT // 2) as j:
                    up(j, False)
                c1 = c0 + FT
                split(L, c1 % 2, (c1 + 2) // 2 + 1)
                with v.Fori(0, (FT // 2 - 3) // 2) as j:
                    for half in range(2):
                        cc = c1 + 3 + half
                        split(L, cc % 2, cc // 2 + j + 1)

            def tile_wait(L, name, k):
                t = TILES[name, k]
                if t.last:
                    s = t.chunk % 2
                    v.wait_ge(chunk_done[s].sem, slot_value(chunk_done[s], L, t.chunk))
                else:
                    v.wait_ge(tile_ready.sem, tile_ready.of(L, t.ready))
                return bank[t.bank]

            def all_vectors():
                v.wait_ge(rows_turned, 1)
                v.tensor_copy(vec_all[:, :, 0:V_LOADED], bank[6][:, 0:DEPTH * V_LOADED].rearrange("p (l n) -> p l n", l=DEPTH))\
                 .then_inc(vec_steps, 1)
                v.wait_ge(spread_loaded, 32)
                steps = [1]
                for g in range(2):
                    rows = slice(64 * g, 64 * g + 64)
                    v.tensor_copy(vec_all[rows, :, V_LSTEP:V_PHASE],
                                  log_steps[rows, :, :].rearrange("p l (j g) -> p l j g", g=2)[:, :, :, g]).then_inc(vec_steps, 1)
                    steps[0] += 1
                v.wait_ge(vec_steps, steps[0])

                def part(a):
                    return vec_all[:, :, a:a + S5_PAIRS]

                phase, mag, f_re, f_im = part(V_PHASE), part(V_MAG), part(V_FRE), part(V_FIM)
                lre, lim, lst = part(V_LRE), part(V_LIM), part(V_LSTEP)
                R = [pscr[:, i] for i in range(12)]

                def do(ins):
                    ins.then_inc(vec_steps, 1)
                    steps[0] += 1
                    v.wait_ge(vec_steps, steps[0])

                def ts(o, a, s1, s2, op0, op1):
                    do(v.tensor_scalar(o, a, s1, s2, op0, op1))

                def stv(o, a, s, b, op0, op1):
                    do(stt(o, a, s, b, op0, op1))

                def tt(o, a, b, op):
                    do(v.tensor_tensor(o, a, b, op))

                ts(R[0], lst, 1.0 / math.log(2.0), MAGIC, MUL, ADD)
                ts(R[0], R[0], -MAGIC, None, ADD, ALU.bypass)
                stv(R[1], R[0], -LN2_A, lst, MUL, ADD)
                stv(R[1], R[0], -LN2_B, R[1], MUL, ADD)
                ts(R[2], R[1], 1.0 / 5040, None, MUL, ALU.bypass)
                for d in (720, 120, 24, 6, 2, 1):
                    stv(R[2], R[2], 1.0 / d, R[1], ADD, MUL)
                ts(R[2], R[2], 1.0, None, ADD, ALU.bypass)
                ts(R[0], R[0], 127.0, 1.0, ADD, ALU.max)
                do(v.tensor_scalar(pint[:, :, :], R[0], 254.0, 8388608.0, ALU.min, MUL))
                tt(R[2], R[2], pint[:, :, :].bitcast(F32), MUL)
                tt(R[3], lim, R[2], MUL)
                ts(R[0], R[3], 1.0 / TWO_PI, MAGIC, MUL, ADD)
                ts(R[0], R[0], -MAGIC, None, ADD, ALU.bypass)
                for part in (TWO_PI_A, TWO_PI_B, TWO_PI_C):
                    stv(R[3], R[0], -part, R[3], MUL, ADD)
                v.tensor_scalar(R[3], R[3], 3.1415925, -3.1415925, ALU.min, ALU.max).then_inc(theta_ready, 1)
                v.wait_ge(theta_ready, 1)
                ts(phase, R[3], 1.0 / TWO_PI, None, MUL, ALU.bypass)
                tt(R[4], lre, R[2], MUL)
                ts(R[4], R[4], 1.0 / 1024, -1.0, MUL, ALU.max)
                ts(R[5], R[4], 1.0 / 24, None, MUL, ALU.bypass)
                for d in (6, 2, 1):
                    stv(R[5], R[5], 1.0 / d, R[4], ADD, MUL)
                for _ in range(10):
                    stv(R[5], R[5], 2.0, R[5], ADD, MUL)
                ts(mag, R[5], 1.0, None, ADD, ALU.bypass)
                v.wait_ge(sines_ready, 2)
                stv(R[6], R[9], -2.0, R[9], MUL, MUL)
                stv(R[7], R[6], 1.0, R[5], ADD, MUL)
                tt(R[7], R[7], R[6], ADD)
                tt(R[8], mag, R[8], MUL)
                tt(R[10], lre, lre, MUL)
                tt(R[11], lim, lim, MUL)
                tt(R[10], R[10], R[11], ADD)
                do(v.reciprocal(R[10], R[10]))
                tt(f_re, R[7], lre, MUL)
                tt(R[11], R[8], lim, MUL)
                tt(f_re, f_re, R[11], ADD)
                tt(f_re, f_re, R[10], MUL)
                tt(f_im, R[8], lre, MUL)
                tt(R[11], R[7], lim, MUL)
                tt(f_im, f_im, R[11], SUB)
                tt(f_im, f_im, R[10], MUL)
                for l in range(DEPTH):
                    for i in range(2):
                        n = 2 * l + i
                        if n:
                            v.wait_ge(lam_sums, n)
                        v.tensor_tensor_reduce(lam_prod[:, :], lam_rows[:, l, 2 * i, :], lam_rows[:, l, 2 * i + 1, :], 1.0, 0.0,
                                               MUL, ADD, small[:, n:n + 1]).then_inc(lam_sums, 1)
                v.wait_ge(lam_exps, 1)
                for l in range(DEPTH):
                    lam_init = 0.8 - 0.6 * math.exp(-0.3 * l)
                    stv(small[:, 16 + l:17 + l], small[:, 8 + 2 * l:9 + 2 * l], -1.0, small[:, 9 + 2 * l:10 + 2 * l], MUL, ADD)
                    ts(vec_all[:, l, V_NEGLAM:V_END], small[:, 16 + l:17 + l], -lam_init, None, ADD, ALU.bypass)
                    ts(vec_all[:, l, V_DNORM:V_SD], vec_all[:, l, V_DNORM:V_SD], 1.0 - lam_init, None, MUL, ALU.bypass)
                return steps[0]

            def ada_chunk(L, f, j, s):
                n = f * 2 * ADA_THIRD + j * 3 + s
                v.wait_ge(ada_loaded[s].sem, ada_loaded[s].of(L, f * 16 * (2 * ADA_THIRD // 3) + j * 16 + 16))
                v.wait_ge(ada_column.sem, ada_column.of(L, n - 2))
                acc = ada_acc[s][:, :]
                for k in range(KT):
                    w = ada_w[s][:, k, :]
                    if k == 0:
                        ins = v.tensor_scalar(acc, w, cond[:, 0:1], None, MUL, ALU.bypass)
                    else:
                        v.wait_ge(ada_step.sem, ada_step.of(L, n * KT + k))
                        ins = stt(acc, w, cond[:, k:k + 1], acc, MUL, ADD)
                    ins.then_inc(ada_step.sem, 1)

            def gains(ui):
                k8 = slice(KT * ui, KT * ui + KT)
                st.did(stt(pre_gain[:, k8], ada[:, 24 * ui + 8:24 * ui + 16], 1.0, vec[:, V_PRE + KT * ui:V_PRE + KT * ui + KT], ADD, MUL))
                st.did(stt(post_gain[:, k8], ada[:, 24 * ui + 16:24 * ui + 24], 1.0 if ui == 1 else 0.5,
                           vec[:, V_POST + KT * ui:V_POST + KT * ui + KT], MUL, MUL))

            def ada_keep(L, f):
                v.wait_ge(ada_column.sem, ada_column.of(L, (2 + f) * ADA_THIRD))
                if f == 0:
                    v.tensor_tensor(ada[:, 24:72], bank[7][:, 0:48], vec[:, 24:72], ADD).then_inc(ada_kept.sem, 1)
                    v.wait_ge(ada_kept.sem, ada_kept.of(L, 1))
                    gains(1)
                    gains(2)
                else:
                    v.tensor_copy(ada[:, 0:24], bank[7][:, 0:24]).then_inc(ada_kept.sem, 1)

            def split_chunk(L, name):
                ch = CHUNK_OF[name]
                split(L, ch % 2, ch // 2 + 1)

            def layer_start(L):
                st.did(v.tensor_copy(vec[:, :], flat(vec_all[:, cols(L), :])))
                st.wait()
                st.did(v.tensor_tensor(ada[:, 0:24], ada[:, 0:24], vec[:, 0:24], ADD))
                st.wait()
                gains(0)
                st.wait()

            def s5_matrices(L):
                b, t = s5_b, s5_t

                def bc(f):
                    return f.unsqueeze(2).to_broadcast([P, S5_PAIRS, S5_CH])

                v.wait_ge(s5w_loaded.sem, s5w_loaded.of(L, 16 * 6))
                st.did(v.tensor_tensor(t[:, 0], b[:, 1], bc(f_im), MUL))
                st.did(v.tensor_tensor(t[:, 1], b[:, 0], bc(f_im), MUL))
                st.wait()
                st.did(v.tensor_tensor(b[:, 0], b[:, 0], bc(f_re), MUL))
                st.did(v.tensor_tensor(b[:, 1], b[:, 1], bc(f_re), MUL))
                st.wait()
                v.wait_ge(s5_bx_zero.sem, s5_bx_zero.of(L, 1))
                for g in range(2):
                    rows = slice(64 * g, 64 * g + 64)
                    for part in range(2):
                        dst = s5_bx[rows, part, :, :, g, :].rearrange("p q i h -> p (q i) h")
                        ins = v.tensor_tensor(dst, b[rows, part], t[rows, part], ADD if part else SUB)
                        if g == 0 or part == 0:
                            st.did(ins)
                st.wait()
                ins.then_inc(s5_bx_ready.sem, 1)
                v.wait_ge(s5_turned.sem, s5_turned.of(L, 1))
                for part in range(2):
                    st.did(v.tensor_copy(flat(s5_bt[:, part]), bank[4 + part][:, :]))
                v.wait_ge(s5_turned.sem, s5_turned.of(L, 2))
                v.wait_ge(s5_mask_ready.sem, s5_mask_ready.of(L, 3))
                mask = s5_mask[:, :, :, :].rearrange("p a g n -> p (a g n)").unsqueeze(1).to_broadcast([P, 4, P])
                for part in range(2):
                    ins = stt(s5_ct[:, part], bank[6 + part][:, :].rearrange("p (q n) -> p q n", q=4), -1.0 if part else 1.0,
                              mask, MUL, MUL)
                    if part == 0:
                        st.did(ins)
                st.wait()
                ins.then_inc(s5_mats_ready.sem, 1)

            def s5_turns_and_front(L, jt, jf):
                if jt is not None:
                    ph = phase[:, jt:jt + 1]
                    if jt >= 1:
                        v.wait_ge(turns_ready.sem, turns_ready.of(L, jt))
                    st.did(v.tensor_scalar(rounded[:, :], time_row[:, :], ph, MAGIC, MUL, ADD))
                if jf is not None:
                    r = [rot[jf % 3][:, i, :] for i in range(4)]
                    cs, sn = tab_c[:, jf % 3, :], tab_s[:, jf % 3, :]
                    v.wait_ge(bu_ready.sem, bu_ready.of(L, jf + 1))
                    v.wait_ge(tables_ready.sem, tables_ready.of(L, jf + 1))
                    if jf >= 3:
                        v.wait_ge(s5_y_ready.sem, s5_y_ready.of(L, jf - 2))
                    st.did(v.tensor_tensor(r[0], bank[4][:, :], cs, MUL))
                if jt is not None:
                    st.wait(back=1 if jf is not None else 0)
                    st.did(v.tensor_scalar(rounded[:, :], rounded[:, :], -MAGIC, None, ADD, ALU.bypass))
                if jf is not None:
                    st.did(v.tensor_tensor(r[1], bank[5][:, :], sn, MUL))
                if jt is not None:
                    st.wait(back=1 if jf is not None else 0)
                    if jt >= 2:
                        v.wait_ge(tables_ready.sem, tables_ready.of(L, jt - 1))
                    stt(turns[:, jt % 2, :], time_row[:, :], ph, rounded[:, :], MUL, SUB).then_inc(turns_ready.sem, 1)
                if jf is not None:
                    v.tensor_tensor(r[2], bank[5][:, :], cs, MUL)
                    v.tensor_tensor(r[3], bank[4][:, :], sn, MUL).then_inc(front_done.sem, 1)

            def s5_back(L, j):
                r = [rot[j % 3][:, i, :] for i in range(4)]
                cs, sn = tab_c[:, j % 3, :], tab_s[:, j % 3, :]
                m = mag[:, j:j + 1].to_broadcast([P, SEQ])
                v.wait_ge(z_in_ready.sem, z_in_ready.of(L, 2 * j + 2))
                st.did(v.tensor_tensor_scan(r[1], m, r[0], 0.0, MUL, ADD))
                st.did(v.tensor_tensor_scan(r[3], m, r[2], 0.0, MUL, ADD))
                st.wait()
                v.tensor_tensor(r[0], r[1], cs, MUL)
                v.tensor_tensor(r[2], r[3], sn, MUL)
                v.tensor_tensor(r[1], r[1], sn, MUL)
                v.tensor_tensor(r[3], r[3], cs, MUL).then_inc(back_done.sem, 1)

            def s5_y(L, q):
                v.wait_ge(s5_y_ready.sem, s5_y_ready.of(L, 4 * q + 4))
                stt(su[:, q, :], su[:, q, :], vec[:, V_SD + q:V_SD + q + 1], bank[6 + q % 2][:, :], MUL, ADD)\
                    .then_inc(s5_y_summed.sem, 1)

            def split_tile(L, base, k, lo, hi, src):
                v.wait_ge(split_hi.sem, split_hi.of(L, base + k + 1))
                v.tensor_tensor(lo[:, k, :], src, hi[:, k, :].bitcast(F32), SUB).then_inc(split_lo.sem, 1)

            def head_keep(L, hh, bk):
                v.wait_ge(o_ms.sem, o_ms.of(L, hh + 1))
                v.tensor_copy(ms_heads[:, (hh % 4) * 4:(hh % 4) * 4 + 4], bank[bk][:, 0:TB]).then_inc(o_ms_kept.sem, 1)

            def heads_norm(L, g):
                v.wait_ge(o_roots.sem, o_roots.of(L, g + 1))
                v.reciprocal(rstd_tok[:, :], sq_root[:, :]).then_inc(o_inverse.sem, 1)
                for hd in range(4):
                    hh = 4 * g + hd
                    v.wait_ge(o_rstd.sem, o_rstd.of(L, hh + 1))
                    bk = bank[4 + hd % 2]
                    if g == 0:
                        stt(o_head[hd][:, :], o_head[hd][:, :], vec[:, V_GNORM + hd:V_GNORM + hd + 1], bk[:, :], MUL, MUL)\
                            .then_inc(o_normed.sem, 1)
                        v.wait_ge(o_normed.sem, o_normed.of(L, hh + 1))
                        v.tensor_tensor(gr[:, hd, :], gr[:, hd, :], o_head[hd][:, :], MUL).then_inc(yga_done.sem, 1)
                    else:
                        stt(dq[:, hd, :], dq[:, hd, :], vec[:, V_DNORM + hd:V_DNORM + hd + 1], bk[:, :], MUL, MUL).then_inc(o_normed.sem, 1)

            def branch_tile(L, name, k, n):
                b = tile_wait(L, name, k)
                m = n % 8
                gate = TILES[f"g{name[1]}{m // 2}", m % 2]
                v.wait_ge(emptied["act"].sem, emptied["act"].of(L, gate.emptied))
                g = (sig if n < 12 else sig_late)[:, n % 4, :]
                v.tensor_tensor(g, g, b[:, :], MUL).then_inc(emptied["vec"].sem, 1)
                v.wait_ge(emptied["vec"].sem, emptied["vec"].of(L, TILES[name, k].emptied))
                if n >= 8:
                    v.wait_ge(merged_ready.sem, merged_ready.of(L, n - 7))
                v.tensor_tensor(merged[:, m, :], merged[:, m, :], g, ADD).then_inc(merged_ready.sem, 1)

            def diff_max(L, i):
                hd, qb = divmod(i, TB)
                n = (qb + 1) * P
                sm = smax[:, i % 2, :]
                if i >= 2:
                    v.wait_ge(at_ready.sem, at_ready.of(L, i - 1))
                v.wait_ge(scores_ready.sem, scores_ready.of(L, 2 * i + 2))
                v.sem_inc(scores_seen.sem, 1)
                for par in range(2):
                    st.did(v.tensor_tensor_reduce(prob[i % 2][:, par, 0:n], bank[4 + par][:, 0:n],
                                                  bias_tab[:, 2 * hd + par, SEQ - n:SEQ], 1.0, -3.4e38, ADD, ALU.max,
                                                  sm[:, par:par + 1]))
                st.wait()
                v.tensor_scalar(sm[:, 2:4], sm[:, 0:2], -1.0, None, MUL, ALU.bypass).then_inc(max_ready.sem, 1)

            def diff_mix(L, i):
                hd, qb = divmod(i, TB)
                n = (qb + 1) * P
                sm = smax[:, i % 2, :]
                pr = prob[i % 2]
                v.wait_ge(prob_ready.sem, prob_ready.of(L, i + 1))
                st.did(v.reciprocal(sm[:, 6:8], sm[:, 4:6]))
                st.wait()
                st.did(v.tensor_tensor(sm[:, 7:8], sm[:, 7:8], neg_lam, MUL))
                st.did(v.tensor_scalar(pr[:, 0, 0:n], pr[:, 0, 0:n], sm[:, 6:7], None, MUL, ALU.bypass))
                st.wait()
                stt(pr[:, 0, 0:n], pr[:, 1, 0:n], sm[:, 7:8], pr[:, 0, 0:n], MUL, ADD).then_inc(mix_ready.sem, 1)

            v.memset(rel33[NUM_BUCKETS:NUM_BUCKETS + 1, :], MASKED).then_inc(const_ready, 1)
            for m in range(KT):
                v.wait_ge(x_turned, m + 1)
                v.tensor_copy(h[:, m, :], bank[m if m < 6 else m - 6][:, :]).then_inc(h_ready.sem, 1)

            steps = all_vectors()
            v.wait_ge(ada_column.sem, 6 + ADA_THIRD)
            v.tensor_copy(ada[:, 0:24], bank[7][:, 0:24]).then_inc(vec_steps, 1)
            v.wait_ge(vec_steps, steps + 1)
            v.wait_ge(line_copied, 2)
            v.wait_ge(const_ready, 4)
            with v.Fori(0, DEPTH) as L:
                st = Steps(v, vector_steps, L)
                layer_start(L)
                modulate(L, 0)
                ffn(L, 0, 0)
                post(L, 0)
                modulate(L, 1)
                s5_matrices(L)
                s5_turns_and_front(L, 0, None)
                s5_turns_and_front(L, 1, 0)
                for j in range(S5_PAIRS):
                    s5_turns_and_front(L, j + 2 if j + 2 < S5_PAIRS else None, j + 1 if j + 1 < S5_PAIRS else None)
                    for n, name in enumerate(S5_SIDE):
                        if n and S5_SPLIT_AT[n] == j:
                            split_chunk(L, name)
                    s5_back(L, j)
                    if j >= 4 and j % 4 == 2:
                        s5_y(L, j // 4 - 1)
                s5_y(L, 3)
                for q in range(4):
                    v.wait_ge(gelu_done.sem, gelu_done.of(L, q + 1))
                    split_tile(L, YG, q, yg_lo, yg_hi, su[:, q, :])
                for k in range(4):
                    b = tile_wait(L, "glu0", k)
                    v.wait_ge(emptied["act"].sem, emptied["act"].of(L, TILES["glu1", k].emptied))
                    stt(z_gate[:, k, :], b[:, :], vec[:, V_BGLU + k:V_BGLU + k + 1], z_gate[:, k, :], ADD, MUL)\
                        .then_inc(emptied["vec"].sem, 1)
                v.wait_ge(emptied["vec"].sem, emptied["vec"].of(L, 4))
                for k in range(4):
                    split_tile(L, YS, k, ys_lo, ys_hi, z_gate[:, k, :])
                for k in range(8):
                    b = tile_wait(L, f"bs{k // 4}", k % 4)
                    v.wait_ge(emptied["act"].sem, emptied["act"].of(L, TILES[f"gs{k // 2}", k % 2].emptied))
                    v.tensor_tensor(merged[:, k, :], merged[:, k, :], b[:, :], MUL).then_inc(emptied["vec"].sem, 1)
                for t in range(2):
                    v.wait_ge(alpha_ready.sem, alpha_ready.of(L, t + 1))
                    v.tensor_scalar(lb[:, t, :], bank[4 + t][:, :], vec[:, V_BALPHA + t:V_BALPHA + t + 1], 0.0, ADD, ALU.min)\
                     .then_inc(alpha_read.sem, 1)
                for t in range(2):
                    v.wait_ge(alpha_exps.sem, alpha_exps.of(L, 1))
                    v.wait_ge(alpha_read.sem, alpha_read.of(L, t + 1))
                    st.did(v.tensor_tensor(la[:, t, :], lb[:, t, :], la[:, t, :], SUB))
                    st.wait()
                    v.tensor_tensor_scan(lb[:, t, :], chunk_mask[:, :], la[:, t, :], 0.0, MUL, ADD).then_inc(decay_sum.sem, 1)
                for t in range(2):
                    b3 = lb[:, t, :].rearrange("p (n i) -> p n i", i=GLA_CHUNK)
                    v.wait_ge(gla_exps.sem, gla_exps.of(L, 2 * t + 2))
                    st.did(v.tensor_copy(small[:, 8 * t:8 * t + 8], b3[:, :, GLA_CHUNK - 1]))
                    st.wait()
                    v.tensor_tensor(b3, small[:, 8 * t:8 * t + 8].unsqueeze(2).to_broadcast([P, N_GCH, GLA_CHUNK]), b3, SUB)\
                     .then_inc(decay_last.sem, 1)
                for t in range(2):
                    v.wait_ge(gla_exps.sem, gla_exps.of(L, 2 * t + 2))
                    stt(gq[:, t, :], gq[:, t, :], GLA_DK ** -0.5, eb[:, t, :], MUL, MUL).then_inc(gla_keys.sem, 1)
                    v.tensor_tensor(la[:, t, :], la[:, t, :], gk[:, t, :], MUL).then_inc(gla_keys.sem, 1)
                for t in range(2):
                    v.wait_ge(gla_exps.sem, gla_exps.of(L, 4 + t + 1))
                    v.wait_ge(gla_keys.sem, gla_keys.of(L, 2 * t + 2))
                    v.tensor_tensor(gk[:, t, :], gk[:, t, :], lb[:, t, :], MUL).then_inc(gla_keys.sem, 1)

                def clamp(hd):
                    v.wait_ge(att_ready.sem, att_ready.of(L, hd + 1))
                    a = att[:, hd % 2, :, :]
                    if hd >= 2:
                        v.wait_ge(o_ready.sem, o_ready.of(L, hd - 1))
                    st.did(v.tensor_tensor(a, bank[4][:, :].rearrange("p (b n) -> p b n", b=TB),
                                           clamp_hi[:, :].unsqueeze(1).to_broadcast([P, TB, P]), ALU.min))
                    st.wait()
                    v.tensor_tensor(a, a, clamp_lo[:, :].unsqueeze(1).to_broadcast([P, TB, P]), ALU.max)\
                     .then_inc(att_clamped.sem, 1)

                for t in range(2):
                    v.wait_ge(ds_ready.sem, ds_ready.of(L, t + 1))
                    for n in range(N_GCH - 1):
                        d = bank[6 + n % 2][:, (n // 2) * P:(n // 2 + 1) * P]
                        if n == 0:
                            ins = v.tensor_copy(s_state[:, t, 1, :], d)
                        else:
                            e = n * GLA_CHUNK + GLA_CHUNK - 1
                            ins = stt(s_state[:, t, n + 1, :], s_state[:, t, n, :], eb[:, t, e:e + 1], d, MUL, ADD)
                        if n < N_GCH - 2:
                            st.did(ins)
                            st.wait()
                    ins.then_inc(s_ready.sem, 1)
                    clamp(t)
                for hd in range(GLA_HEADS):
                    if hd + 2 < GLA_HEADS:
                        clamp(hd + 2)
                    head_keep(L, hd, 6 + hd % 2)
                heads_norm(L, 0)
                for k in range(4):
                    split_tile(L, YGA, k, yga_lo, yga_hi, gr[:, k, :])
                v.wait_ge(bias_loaded.sem, bias_loaded.of(L, 16))
                diff_max(L, 0)
                for i in range(DIFF_HEADS * TB):
                    hd, qb = divmod(i, TB)
                    for name, k in BESIDE_DIFF[i - 1] if i else ():
                        if name[0] == "b":
                            branch_tile(L, name, k, 4 * int(name[-1]) + k)
                    if i + 1 < DIFF_HEADS * TB:
                        diff_max(L, i + 1)
                    diff_mix(L, i)
                    if qb == TB - 1:
                        head_keep(L, 4 + hd, 7)
                heads_norm(L, 1)
                for k in range(4):
                    split_tile(L, YD, k, yd_lo, yd_hi, dq[:, k, :])
                for k in range(8):
                    branch_tile(L, f"bd{k // 4}", k % 4, 8 + k)
                for m in range(KT):
                    split_tile(L, MG, m, mg_lo, mg_hi, merged[:, m, :])
                post(L, 1)
                modulate(L, 2)
                ffn(L, 1, C_FFN2)
                post(L, 2)
                assert st.n == VECTOR_STEPS, st.n

            for b in range(TB):
                v.wait_ge(out_turned, 2 * b + 2)
                v.wait_ge(out_half, b + 1)
                v.tensor_copy(x_tok[:, b, SEQ:D_MODEL], bank[2 * b + 1][:, :]).then_inc(out_copied, 1)

        @block.gpsimd
        def _(pool):
            pool.memset(ident[:, :], 0.0).then_inc(pool_start, 1)
            pool.memset(ones[:, :], 1.0).then_inc(pool_start, 1)
            pool.memset(chunk_mask[:, :], 1.0).then_inc(pool_start, 1)
            pool.memset(clamp_hi[:, :], BIG).then_inc(pool_start, 1)
            pool.memset(clamp_lo[:, :], -BIG).then_inc(pool_start, 1)
            pool.memset(inv_d[:, 0:1], 1.0 / D_MODEL).then_inc(pool_start, 1)
            pool.memset(inv_d[:, 1:2], 1.0 / P).then_inc(pool_start, 1)
            pool.memset(cst[:, 0:1], EPS).then_inc(pool_start, 1)
            pool.memset(cst[:, 1:2], math.pi / 2).then_inc(pool_start, 1)
            pool.iota(time_row[:, :], [[1, SEQ]], base=0, channel_multiplier=0, allow_small_or_imprecise_dtypes=True)\
                .then_inc(pool_start, 1)
            pool.wait_ge(pool_start, 10)
            pool.affine_select(out=ident[:, :], in_=ident[:, :], compare_op=ALU.not_equal, fill=1.0, base=0,
                               pattern=[[-1, P]], channel_multiplier=1).then_inc(const_ready, 1)
            pool.affine_select(out=chunk_mask[:, :], in_=chunk_mask[:, :], compare_op=ALU.not_equal, fill=0.0, base=0,
                               pattern=[[0, N_GCH], [1, GLA_CHUNK]], channel_multiplier=0).then_inc(const_ready, 1)
            for m in (clamp_hi, clamp_lo):
                pool.affine_select(out=m[:, :], in_=m[:, :], compare_op=ALU.is_ge, fill=0.0, base=0,
                                   pattern=[[1, P]], channel_multiplier=-1).then_inc(pool_start, 1)
            pool.wait_ge(pool_start, 12)
            for m in (clamp_hi, clamp_lo):
                pool.memset(m[0:64, 64:128], 0.0).then_inc(pool_start, 1)
            pool.wait_ge(pool_start, 14)
            pool.sem_inc(const_ready, 1)

            def squares(L, r, tiles=range(1, KT)):
                for m in tiles:
                    pool.wait_ge(sq_ready.sem, sq_ready.of(L, KT * r + m + 1))
                    if m == 1:
                        pool.wait_ge(ms_ready.sem, ms_ready.of(L, r))
                        pool.tensor_tensor(sq_sum[:, :], sq_buf[:, 0, :], sq_buf[:, 1, :], ALU.add).then_inc(sq_summed.sem, 2)
                    else:
                        pool.wait_ge(sq_summed.sem, sq_summed.of(L, KT * r + m))
                        pool.tensor_tensor(sq_sum[:, :], sq_sum[:, :], sq_buf[:, m % 3, :], ALU.add).then_inc(sq_summed.sem, 1)

            def split_low(L, ch, n=CHUNK_ELEMS):
                s = ch % 2
                pool.wait_ge(hi_split[s].sem, slot_value(hi_split[s], L, ch))
                pool.tensor_tensor(w_lo[s][:, 0:n], raw[s][:, 0:n], w_hi[s][:, 0:n].bitcast(F32), ALU.subtract)\
                    .then_inc(lo_split[s].sem, 1)

            def split(L, name):
                split_low(L, CHUNK_OF[name], KT * P if chunk_widths(name) == P else CHUNK_ELEMS)

            with pool.Fori(0, DEPTH) as L:
                split_low(L, 0)
                squares(L, 0)
                split_low(L, 1)
                split(L, "su0")
                squares(L, 1)
                squares(L, 2)
                split(L, "su1")
                s = (C_MIX - 1) % 2
                pool.wait_ge(chunk_done[s].sem, slot_value(chunk_done[s], L, C_MIX - 1))
                pool.sem_inc(room_seen.sem, 1)
                pool.memset(s5_bx[:, :, :, :, :, :].rearrange("p a q i g h -> p (a q i g h)"), 0.0).then_inc(s5_bx_zero.sem, 1)
                pool.memset(s5_mask[:, :, :, :], 0.0).then_inc(s5_mask_ready.sem, 1)
                pool.wait_ge(s5_mask_ready.sem, s5_mask_ready.of(L, 1))
                pool.sem_inc(room_seen.sem, 1)
                for g in range(2):
                    pool.memset(s5_mask[64 * g:64 * g + 64, :, g, :], 1.0).then_inc(s5_mask_ready.sem, 1)
                pool.wait_ge(s5_mask_ready.sem, s5_mask_ready.of(L, 3))
                split(L, "su2")
                split(L, "gq")
                for j in range(S5_PAIRS):
                    r = [rot[j % 3][:, i, :] for i in range(4)]
                    pool.wait_ge(front_done.sem, front_done.of(L, j + 1))
                    pool.tensor_tensor(r[0], r[0], r[1], ALU.add).then_inc(z_in_ready.sem, 1)
                    pool.tensor_tensor(r[2], r[2], r[3], ALU.subtract).then_inc(z_in_ready.sem, 1)
                    pool.wait_ge(back_done.sem, back_done.of(L, j + 1))
                    pool.tensor_tensor(r[0], r[0], r[2], ALU.subtract).then_inc(state_ready.sem, 1)
                    pool.tensor_tensor(r[1], r[1], r[3], ALU.add).then_inc(state_ready.sem, 1)
                for name, _, _ in MIXER[14:-1]:
                    split(L, name)
                squares(L, 3, (1, 2))
                split(L, "wo3")
                squares(L, 3, (3, 4))
                split_low(L, C_FFN2)
                squares(L, 3, (5, 6, 7))
                squares(L, 4)
                split_low(L, C_FFN2 + 1)
                squares(L, 5)


_NAMES = ["x", "c", "rel_bias", "w_ada", "b_ada", "norm_pre", "norm_post", "ffn1_w_up", "ffn1_w_down", "ffn2_w_up",
          "ffn2_w_down", "w_in", "gla_w_alpha", "gla_b_alpha", "gla_norm", "diff_lambda", "diff_norm", "s5_lam_re",
          "s5_lam_im", "s5_log_step", "s5_b_re", "s5_b_im", "s5_c_re", "s5_c_im", "s5_d", "s5_w_glu", "s5_b_glu",
          "w_branch", "w_out"]


def bucket_onehot():
    hot = np.zeros((NUM_BUCKETS + 1, LINE), np.float32)
    exact = NUM_BUCKETS // 2
    for y in range(LINE):
        d = SEQ - 1 - y
        if d < 0:
            hot[NUM_BUCKETS, y] = 1.0
        elif d < exact:
            hot[d, y] = 1.0
        else:
            scaled = np.log(np.float32(d) / np.float32(exact)) / np.float32(math.log(MAX_DISTANCE / exact))
            hot[min(exact + int(np.float32(scaled * np.float32(NUM_BUCKETS - exact))), NUM_BUCKETS - 1), y] = 1.0
    return hot


def kernel(**inputs):
    import concourse.bacc as bacc
    from concourse.bass_utils import run_bass_kernel_spmd

    nc = bacc.Bacc("TRN2", target_bir_lowering=False, num_devices=1)
    nc.disable_value_cache = True
    arrays = {"in_" + name: np.ascontiguousarray(inputs[name]) for name in _NAMES}
    arrays["in_bucket_onehot"] = bucket_onehot()
    args = [nc.dram_tensor(name, a.shape, mybir.dt.from_np(a.dtype), kind="ExternalInput").ap() for name, a in arrays.items()]
    args.append(nc.dram_tensor("out", (1, SEQ, D_MODEL), F32, kind="ExternalOutput").ap())
    build(nc, *args)
    return run_bass_kernel_spmd(nc, [arrays], core_ids=[0]).results[0]["out"]
```

```python
import math
from contextlib import ExitStack

import numpy as np
import concourse.bass as bass
from concourse import mybir

F32 = mybir.dt.float32
F32R = mybir.dt.float32r
BF16 = mybir.dt.bfloat16
I32 = mybir.dt.int32
ALU = mybir.AluOpType
ACT = mybir.ActivationFunctionType
AX_X = mybir.AxisListType.X

P = 128
D_MODEL, SEQ, DEPTH, D_FF = 1024, 512, 2, 2816
KT = D_MODEL // P
FT = D_FF // P
TB = SEQ // P
EPS = 1e-6
CHUNK_ELEMS = 2048
GLA_HEADS, GLA_DK, GLA_CHUNK, LOWRANK, GLA_TAU = 4, 64, 64, 16, 16.0
N_GCH = SEQ // GLA_CHUNK
DIFF_HEADS, N_MAPS = 4, 8
NUM_BUCKETS, MAX_DISTANCE = 32, 128
S5_PAIRS, S5_CH = 16, 16
LINE = SEQ + P
BIAS_COPIES = 16
MAGIC = 1.5 * 2.0 ** 23
BIG = 3.0e38
MASKED = -1.0e30
TWO_PI = 2.0 * math.pi
TWO_PI_A, TWO_PI_B = 6.28125, 0.0019340515136718750
TWO_PI_C = TWO_PI - TWO_PI_A - TWO_PI_B
LN2_A = 0.693359375
LN2_B = math.log(2.0) - LN2_A

OFF_GQ, OFF_GK, OFF_GV, OFF_GR, OFF_A = 0, 256, 512, 1024, 1536
OFF_DQ, OFF_DK, OFF_DV, OFF_SU, OFF_GATE = 1552, 2064, 2576, 3088, 3600

MIXER = [("su0", 2, "act"), ("su1", 1, "act"), ("su2", 1, "act"),
         ("gq", 2, "act"), ("gk", 2, "act"), ("ga", 1, "act"), ("gv0", 2, "act"), ("gv1", 2, "act"),
         ("gr0", 2, "act"), ("gr1", 2, "act")] + [(f"gs{i}", 2, "act") for i in range(4)] + \
        [("glu1", 4, "act"), ("glu0", 4, "vec"), ("bs0", 4, "vec"), ("bs1", 4, "vec")] + \
        [(f"d{x}{i}", 2, "act") for x in "qkv" for i in range(2)] + \
        [("gg0", 2, "act"), ("gg1", 2, "act"), ("bg0", 4, "vec"), ("gg2", 2, "act"), ("gg3", 2, "act"), ("bg1", 4, "vec")] + \
        [(f"gd{i}", 2, "act") for i in range(4)] + [("bd0", 4, "vec"), ("bd1", 4, "vec")] + \
        [(f"wo{i}", 2, "sub") for i in range(4)]
FFN_CHUNKS = 2 * FT // 2 + FT // 2
C_MIX, C_FFN2 = FFN_CHUNKS, FFN_CHUNKS + len(MIXER)
CHUNKS = 2 * FFN_CHUNKS + len(MIXER)
assert CHUNKS % 2 == 0 and C_MIX % 2 == 1
SLOT_USES = CHUNKS // 2
ADA_WIDTH = 256
ADA_CHUNKS = 9 * D_MODEL // ADA_WIDTH
ADA_ROUNDS = (8, 4)
ADA_AHEAD = 2 * D_MODEL // ADA_WIDTH
assert 3 * sum(ADA_ROUNDS) == 9 * D_MODEL // ADA_WIDTH and ADA_ROUNDS[1] * ADA_WIDTH == D_MODEL
FFN_TILES = FT + KT - 1


class Tile:
    pass


def mixer_tiles():
    tiles, evac = {}, {"act": 0, "vec": 0, "sub": 0}
    t, ready = 0, FFN_TILES
    order = []
    for i, (name, n, engine) in enumerate(MIXER):
        for k in range(n):
            x = Tile()
            x.chunk, x.bank, x.engine = C_MIX + i, t % 4, engine
            x.last = k == n - 1
            if not x.last:
                ready += 1
            x.ready = ready
            evac[engine] += 1
            x.emptied = evac[engine]
            x.before = order[t - 4] if t >= 4 else None
            order.append(x)
            tiles[name, k] = x
            t += 1
    return tiles, evac, ready


TILES, EMPTIED, READY_BEFORE_FFN2 = mixer_tiles()
S5_SIDE = [name for name, _, _ in MIXER[3:14]]
S5_SIDE_TILES = sum(n for _, n, _ in MIXER[3:14])
S5_FIRST = [sum(n for _, n, _ in MIXER[3:3 + i]) for i in range(len(S5_SIDE))]
S5_PACE = S5_SIDE_TILES - 3
S5_SPLIT_AT = [max(0, min(S5_PAIRS - 1, first * S5_PAIRS // S5_PACE - 2)) for first in S5_FIRST]
S5_BY_POOL = (1, 3, 5)
DIFF_BLOCKS = DIFF_HEADS * TB
BESIDE = [t for t in TILES if t[0] in ("gg1", "bg0", "gg2", "gg3", "bg1", "gd0")]
BESIDE_DIFF = [[t for n, t in enumerate(BESIDE) if n * DIFF_BLOCKS // len(BESIDE) == i] for i in range(DIFF_BLOCKS)]
CHUNK_OF = {name: C_MIX + i for i, (name, _, _) in enumerate(MIXER)}
READY_PER_LAYER = READY_BEFORE_FFN2 + FFN_TILES
VECTOR_STEPS, SCALAR_STEPS = 239, 35

V_BADA, V_PRE, V_POST, V_GNORM, V_DNORM, V_SD, V_BGLU, V_BALPHA, V_LRE, V_LIM, V_LSTEP, \
    V_PHASE, V_MAG, V_FRE, V_FIM, V_NEGLAM, V_END = \
    0, 72, 96, 120, 124, 128, 132, 140, 142, 158, 174, 190, 206, 222, 238, 254, 255
V_LOADED = V_LSTEP
assert DEPTH == 2
ADDED_BY_POOL = (2, 4)
ADDED_BY_VECTOR = tuple(m for m in range(KT) if m not in ADDED_BY_POOL)
H_SUMMED = KT - 3


class Signal:

    def __init__(self, ctx, nc, name, per_layer, head_start=0):
        self.sem = ctx.enter_context(nc.semaphore(name))
        self.per_layer, self.head_start = per_layer, head_start

    def of(self, layer, k):
        return layer * self.per_layer + k + self.head_start


class Steps:

    def __init__(self, engine, counter, layer):
        self.engine, self.counter, self.layer, self.n = engine, counter, layer, 0

    def did(self, instruction):
        instruction.then_inc(self.counter.sem, 1)
        self.n += 1

    def wait(self, back=0):
        if self.n - back > 0:
            self.engine.wait_ge(self.counter.sem, self.counter.of(self.layer, self.n - back))


def build(nc, x, c, rel_bias, w_ada, b_ada, norm_pre, norm_post, ffn1_w_up, ffn1_w_down, ffn2_w_up, ffn2_w_down,
          w_in, gla_w_alpha, gla_b_alpha, gla_norm, diff_lambda, diff_norm, s5_lam_re, s5_lam_im, s5_log_step,
          s5_b_re, s5_b_im, s5_c_re, s5_c_im, s5_d, s5_w_glu, s5_b_glu, w_branch, w_out, bucket_onehot, out):
    ctx = ExitStack()
    with ctx:
        BASE = 16512
        X0 = 105

        def at(name, kib, shape, dt=F32):
            return nc.alloc_sbuf_tensor_at(name, shape, dt, offset=BASE + int(round(kib * 1024)))

        def shared(name, kib, shape, dt=F32):
            return at(name, X0 + kib, shape, dt)

        h = at("h", 0, [P, KT, SEQ])
        u_hi = at("u_hi", 16, [P, KT, SEQ], F32R)
        u_lo = at("u_lo", 32, [P, KT, SEQ], F32R)
        y_sub = at("y_sub", 16, [P, KT, SEQ])
        raw = [at(f"raw{s}", 48 + 8 * s, [P, CHUNK_ELEMS]) for s in range(2)]
        w_hi = [at(f"w_hi{s}", 64 + 8 * s, [P, CHUNK_ELEMS], F32R) for s in range(2)]
        w_lo = [at(f"w_lo{s}", 80 + 8 * s, [P, CHUNK_ELEMS], F32R) for s in range(2)]
        ident = at("ident", 96, [P, P])
        ones = at("ones", 96.5, [P, P])
        time_row = at("time_row", 97, [P, SEQ])
        chunk_mask = at("chunk_mask", 99, [P, SEQ], BF16)
        clamp_hi = at("clamp_hi", 100, [P, P])
        clamp_lo = at("clamp_lo", 100.5, [P, P])
        vec_all = at("vec_all", 101, [P, DEPTH, V_END])
        vec = at("vec", 103, [P, V_END])
        ada = at("ada", 104, [P, 72])
        pre_gain = at("pre_gain", 104.28125, [P, 24])
        post_gain = at("post_gain", 104.375, [P, 24])
        small = at("small", 104.46875, [P, 48])
        cond = at("cond", 104.65625, [P, KT])
        sq_root = at("sq_root", 104.6875, [P, 16])
        rstd_tok = at("rstd_tok", 104.75, [P, 16])
        ms_heads = at("ms_heads", 104.8125, [P, 16])
        smax = at("smax", 104.875, [P, 2, 8])
        inv_d = at("inv_d", 104.9375, [P, 2])
        cst = at("cst", 104.96875, [P, 2])
        EPS_COL, HALF_PI = cst[:, 0:1], cst[:, 1:2]
        neg_lam = vec[:, V_NEGLAM:V_END]
        phase, mag, f_re, f_im = (vec[:, i:i + S5_PAIRS] for i in (V_PHASE, V_MAG, V_FRE, V_FIM))

        g_hi = shared("g_hi", 0, [P, FT, SEQ], F32R)
        g_lo = shared("g_lo", 44, [P, FT, SEQ], F32R)
        silu_buf = shared("silu_buf", 88, [P, 2, SEQ])
        mod_buf = shared("mod_buf", 92, [P, 2, SEQ])
        sq_buf = shared("sq_buf", 94, [P, 3, SEQ])
        sq_sum = shared("sq_sum", 100, [P, SEQ])
        ada_w = [shared(f"ada_w{s}", k, [P, KT, ADA_WIDTH]) for s, k in enumerate((32, 76, 92))]
        first_ada_w = [shared(f"first_ada_w{s}", k, [P, KT, ADA_WIDTH]) for s, k in enumerate((32, 50, 58, 66, 74, 82))]
        first_ada_acc = [shared(f"first_ada_acc{s}", 40 + s, [P, ADA_WIDTH]) for s in range(3)]
        ada_acc = [shared(f"ada_acc{s}", 40 + s, [P, ADA_WIDTH]) for s in range(3)]
        rows_a = [shared(f"rows_a{l}", 24 + l, [72, P]) for l in range(DEPTH)]
        rows_b = [shared(f"rows_b{l}", 24.5 + l, [V_LOADED - 72, P]) for l in range(DEPTH)]
        log_steps = shared("log_steps", 26, [P, DEPTH, 2 * S5_PAIRS])
        lam_rows = shared("lam_rows", 28, [P, DEPTH, 4, 64])
        lam_prod = shared("lam_prod", 30, [P, 64])
        x_tok = shared("x_tok", 0, [P, TB, D_MODEL])
        c_row = shared("c_row", 16, [KT, P])
        onehot = shared("onehot", 17, [NUM_BUCKETS + 1, LINE])
        rel33 = shared("rel33", 20, [NUM_BUCKETS + 1, N_MAPS])
        bias_line = shared("bias_line", 21, [N_MAPS, LINE])
        pscr = shared("pscr", 44, [P, 12, DEPTH, S5_PAIRS])
        pint = shared("pint", 46, [P, DEPTH, S5_PAIRS], I32)
        su = shared("su", 0, [P, 4, SEQ])
        s_state = shared("s_state", 0, [P, 2, N_GCH, P])
        gq = shared("gq", 8, [P, 2, SEQ])
        gk = shared("gk", 12, [P, 2, SEQ])
        gv = shared("gv", 16, [P, TB, SEQ])
        gr = shared("gr", 24, [P, 4, SEQ])
        merged = shared("merged", 32, [P, KT, SEQ])
        s5_bt = shared("s5_bt", 48, [P, 2, 4, P])
        s5_ct = shared("s5_ct", 52, [P, 2, 4, P])
        s5_bx = shared("s5_bx", 58, [P, 2, 4, 4, 2, S5_CH])
        s5_cd = shared("s5_cd", 62, [P, 2, 4, 2, 64])
        s5_b = shared("s5_b", 66, [P, 2, S5_PAIRS, S5_CH])
        s5_t = shared("s5_t", 68, [P, 2, S5_PAIRS, S5_CH])
        s5_mask = shared("s5_mask", 70, [P, 4, 2, S5_CH])
        rot = [shared(f"rot{i}", k, [P, 4, SEQ]) for i, k in enumerate((58, 66, 94))]
        tab_c = shared("tab_c", 74, [P, 3, SEQ])
        tab_s = shared("tab_s", 80, [P, 3, SEQ])
        turns = shared("turns", 86, [P, 2, SEQ])
        rounded = shared("rounded", 90, [P, SEQ])
        a_low = shared("a_low", 92, [LOWRANK, SEQ])
        w_alpha = shared("w_alpha", 56, [LOWRANK, 256])
        yg_hi = shared("yg_hi", 58, [P, 4, SEQ], F32R)
        yg_lo = shared("yg_lo", 66, [P, 4, SEQ], F32R)
        z_gate = shared("z_gate", 0, [P, 4, SEQ])
        ys_hi = shared("ys_hi", 74, [P, 4, SEQ], F32R)
        ys_lo = shared("ys_lo", 82, [P, 4, SEQ], F32R)
        la = shared("la", 48, [P, 2, SEQ])
        lb = shared("lb", 52, [P, 2, SEQ])
        eb = shared("eb", 56, [P, 2, SEQ])
        kk_tok = shared("kk_tok", 60, [P, TB, 2 * P])
        att = shared("att", 64, [P, 2, TB, P])
        o_head = [shared(f"o_head{i}", k, [P, SEQ]) for i, k in enumerate((68, 70, 90, 72))]
        o_sq = shared("o_sq", 92, [P, SEQ])
        dq = shared("dq", 74, [P, 4, SEQ])
        dk = shared("dk", 82, [P, 4, SEQ])
        dv = shared("dv", 94, [P, TB, SEQ])
        yga_hi = shared("yga_hi", 48, [P, 4, SEQ], F32R)
        yga_lo = shared("yga_lo", 56, [P, 4, SEQ], F32R)
        sig = shared("sig", 0, [P, 4, SEQ])
        sig_late = shared("sig_late", 64, [P, 4, SEQ])
        bias_tab = shared("bias_tab", 8, [P, N_MAPS, SEQ])
        a_t = shared("a_t", 24, [P, TB, SEQ])
        prob = [shared("prob0", 64, [P, 2, SEQ]), shared("prob1", 68, [P, 2, SEQ])]
        yd_hi = shared("yd_hi", 48, [P, 4, SEQ], F32R)
        yd_lo = shared("yd_lo", 56, [P, 4, SEQ], F32R)
        mg_hi = shared("mg_hi", 8, [P, KT, SEQ], F32R)
        mg_lo = shared("mg_lo", 74, [P, KT, SEQ], F32R)

        bank = [ctx.enter_context(nc.psum_tensor(f"bank{i}", [P, SEQ], F32)) for i in range(8)]
        bias_dram = nc.dram_tensor("bias_line_dram", (N_MAPS, LINE), F32, kind="Internal").ap()
        bias_copies = nc.dram_tensor("bias_copies_dram", (N_MAPS, BIAS_COPIES, LINE), F32, kind="Internal").ap()

        MS_BANK = (4, 0, 4, 4, 4, 0)

        def signal(name, per_layer, head_start=0):
            return Signal(ctx, nc, name, per_layer, head_start)

        def sem(name):
            return ctx.enter_context(nc.semaphore(name))

        raw_loaded = [signal(f"raw_loaded{s}", 16 * SLOT_USES) for s in range(2)]
        hi_split = [signal(f"hi_split{s}", SLOT_USES, 1) for s in range(2)]
        lo_split = [signal(f"lo_split{s}", SLOT_USES, 1) for s in range(2)]
        chunk_done = [signal(f"chunk_done{s}", SLOT_USES, 1) for s in range(2)]
        tile_ready = signal("tile_ready", READY_PER_LAYER)
        emptied = {"act": signal("emptied_by_act", EMPTIED["act"]), "vec": signal("emptied_by_vec", EMPTIED["vec"])}
        silu_done = signal("silu_done", 2 * FT, 2)
        prod_done = signal("prod_done", 2 * FT, 2)
        g_hi_ready = signal("g_hi_ready", 2 * FT)
        g_lo_ready = signal("g_lo_ready", 2 * FT, 2)
        h_by_vector = signal("h_by_vector", 3 * len(ADDED_BY_VECTOR), len(ADDED_BY_VECTOR))
        h_by_pool = signal("h_by_pool", 3 * len(ADDED_BY_POOL), len(ADDED_BY_POOL))
        y_scaled = signal("y_scaled", 3 * len(ADDED_BY_POOL))
        h_sq_summed = signal("h_sq_summed", 3 * H_SUMMED)
        h_sq_total = signal("h_sq_total", 3)
        h_ms_ready = signal("h_ms_ready", 3)
        sq_ready = signal("sq_ready", 6 * KT)
        sq_summed = signal("sq_summed", 3 * (KT - 1))
        y_ms_ready = signal("y_ms_ready", 3)
        y_copied = signal("y_copied", 3 * KT)
        root_ready = signal("root_ready", 6)
        inverse_ready = signal("inverse_ready", 6)
        rstd_ready = signal("rstd_ready", 6)
        modulated = signal("modulated", 3 * KT)
        u_hi_ready = signal("u_hi_ready", 3 * KT)
        u_ready = signal("u_ready", 3 * KT)
        vector_steps = signal("vector_steps", VECTOR_STEPS)
        scalar_steps = signal("scalar_steps", SCALAR_STEPS)
        x_loaded, c_loaded, line_loaded = sem("x_loaded"), sem("c_loaded"), sem("line_loaded")
        const_ready, x_turned, c_turned = sem("const_ready"), sem("x_turned"), sem("c_turned")
        rows_loaded, rows_turned, spread_loaded, vec_steps = sem("rows_loaded"), sem("rows_turned"), sem("spread_loaded"), sem("vec_steps")
        theta_ready, sines_ready, lam_sums, lam_exps = sem("theta_ready"), sem("sines_ready"), sem("lam_sums"), sem("lam_exps")
        cond_ready, line_made, line_copied, line_stored = sem("cond_ready"), sem("line_made"), sem("line_copied"), sem("line_stored")
        out_turned, out_by_act, out_by_vec, out_stored = sem("out_turned"), sem("out_by_act"), sem("out_by_vec"), sem("out_stored")
        pool_start = sem("pool_start")
        ada_loaded = [signal(f"ada_loaded{s}", 16 * sum(ADA_ROUNDS)) for s in range(3)]
        first_ada_loaded = [sem(f"first_ada_loaded{s}") for s in range(6)]
        first_ada_step, first_column = sem("first_ada_step"), sem("first_column")
        ada_step = signal("ada_step", ADA_CHUNKS * KT, 3 * KT)
        ada_column = signal("ada_column", ADA_CHUNKS, 3)
        ada_kept = signal("ada_kept", 2)
        s5w_loaded = signal("s5w_loaded", 16 * 6)
        s5_bx_zero = signal("s5_bx_zero", 1)
        s5_mask_ready = signal("s5_mask_ready", 3)
        s5_bx_ready = signal("s5_bx_ready", 1)
        s5_turned = signal("s5_turned", 2)
        s5_mats_ready = signal("s5_mats_ready", 1)
        turns_ready = signal("turns_ready", S5_PAIRS)
        tables_ready = signal("tables_ready", S5_PAIRS)
        bu_ready = signal("bu_ready", S5_PAIRS)
        front_done = signal("front_done", S5_PAIRS)
        z_in_ready = signal("z_in_ready", 2 * S5_PAIRS)
        back_done = signal("back_done", S5_PAIRS)
        state_ready = signal("state_ready", 2 * S5_PAIRS)
        alpha_loaded = signal("alpha_loaded", 16)
        s5_y_ready = signal("s5_y_ready", S5_PAIRS)
        s5_y_summed = signal("s5_y_summed", 4)
        gelu_done = signal("gelu_done", 4)
        split_hi = signal("split_hi", 4 + 4 + 4 + 4 + 8)
        split_lo = signal("split_lo", 4 + 4 + 4 + 4 + 8)
        YG, YS, YGA, YD, MG = 0, 4, 8, 12, 16
        merged_ready = signal("merged_ready", 16)
        alpha_ready = signal("alpha_ready", 2)
        alpha_read = signal("alpha_read", 2)
        alpha_exps = signal("alpha_exps", 1)
        decay_sum = signal("decay_sum", 2)
        decay_last = signal("decay_last", 2)
        gla_exps = signal("gla_exps", 6)
        gla_keys = signal("gla_keys", 6)
        kk_turned = signal("kk_turned", 1)
        kk_copied = signal("kk_copied", 2)
        ds_ready = signal("ds_ready", 2)
        s_ready = signal("s_ready", 2)
        att_ready = signal("att_ready", 4)
        att_clamped = signal("att_clamped", 4)
        o_ready = signal("o_ready", 8)
        o_copied = signal("o_copied", 8)
        o_squared = signal("o_squared", 8)
        o_ms = signal("o_ms", 8)
        o_ms_kept = signal("o_ms_kept", 8)
        o_roots = signal("o_roots", 2)
        o_inverse = signal("o_inverse", 2)
        o_rstd = signal("o_rstd", 8)
        o_normed = signal("o_normed", 8)
        yga_done = signal("yga_done", 4)
        bias_loaded = signal("bias_loaded", 16 * P // BIAS_COPIES)
        scores_ready = signal("scores_ready", 32)
        scores_seen, states_begun, room_seen = signal("scores_seen", 16), signal("states_begun", 2), signal("room_seen", 2)
        max_ready = signal("max_ready", 16)
        prob_ready = signal("prob_ready", 16)
        mix_ready = signal("mix_ready", 16)
        at_ready = signal("at_ready", 16)
        at_copied = signal("at_copied", 16)

        def cols(j, n=1):
            return bass.ds(j, n)

        def flat(ap):
            return ap.rearrange("p a n -> p (a n)")

        def slot_value(sig, L, chunk, extra=0):
            return sig.of(L, chunk // 2 + 1 + extra)

        def chunk_widths(name):
            return P if name in ("su1", "su2", "ga") else 256

        block = ctx.enter_context(nc.Block())

        @block.sync
        def _(sp):
            def load(L, s, n, dst, src):
                sp.wait_ge(hi_split[s].sem, hi_split[s].of(L, n - 1))
                sp.wait_ge(lo_split[s].sem, lo_split[s].of(L, n - 1))
                sp.dma_start(dst, src).then_inc(raw_loaded[s].sem, 16)

            def load_ffn(L, f, c0, w_up, w_down):
                def up(j):
                    for half in range(2):
                        s = (c0 + half) % 2
                        n = (c0 + half) // 2 + j + 1
                        src = w_up[L, :, bass.ds(j * 256 + half * D_FF, 256)].rearrange("(k p) n -> p k n", p=P)
                        load(L, s, n, raw[s][:, :].rearrange("p (k n) -> p k n", k=KT), src)

                with sp.Fori(0, ADA_ROUNDS[f]) as j:
                    up(j)
                    sp.wait_ge(modulated.sem, modulated.of(L, 2 * f * KT + 1))
                    for s in range(3):
                        if s == 2:
                            sp.wait_ge(u_ready.sem, u_ready.of(L, (2 * f + 1) * KT))
                        sp.wait_ge(ada_step.sem, ada_step.of(L, (f * 3 * ADA_ROUNDS[0] + j * 3 + s - 2) * KT))
                        if f == 0:
                            load_ada(ada_w[s], ada_loaded[s].sem, L, j * (3 * ADA_WIDTH) + (s * ADA_WIDTH + 2 * D_MODEL))
                        elif s == 0:
                            load_ada(ada_w[s], ada_loaded[s].sem, L, j * ADA_WIDTH + 8 * D_MODEL)
                        else:
                            load_ada(ada_w[s], ada_loaded[s].sem, DEPTH - 1, j * (2 * ADA_WIDTH) + (s - 1) * ADA_WIDTH)
                with sp.Fori(ADA_ROUNDS[f], FT // 2) as j:
                    up(j)
                c1 = c0 + FT
                s = c1 % 2
                load(L, s, c1 // 2 + 1, raw[s][:, :].rearrange("p (k n) -> p k n", k=2),
                     w_down[L, 0:256, :].rearrange("(k p) n -> p k n", p=P))
                with sp.Fori(0, FT // 4) as j:
                    for half in range(2):
                        s = (c1 + 1 + half) % 2
                        n = (c1 + 1 + half) // 2 + j + 1
                        src = w_down[L, bass.ds(j * 512 + half * 256 + 256, 256), :].rearrange("(k p) n -> p k n", p=P)
                        load(L, s, n, raw[s][:, :].rearrange("p (k n) -> p k n", k=2), src)

            def load_chunk(L, name):
                ch = CHUNK_OF[name]
                s = ch % 2
                i = int(name[-1]) if name[-1].isdigit() else 0
                start = {"su": OFF_SU, "gq": OFF_GQ, "gk": OFF_GK, "ga": OFF_A, "gv": OFF_GV, "gr": OFF_GR,
                         "dq": OFF_DQ, "dk": OFF_DK, "dv": OFF_DV, "gg": OFF_GATE, "gd": OFF_GATE + D_MODEL,
                         "gs": OFF_GATE + 2 * D_MODEL}.get(name[:2])
                if start is not None:
                    w = chunk_widths(name)
                    start += {"su1": 256, "su2": 384}.get(name, 256 * i)
                    load(L, s, ch // 2 + 1, raw[s][:, 0:KT * w].rearrange("p (k n) -> p k n", k=KT),
                         w_in[L, :, start:start + w].rearrange("(k p) n -> p k n", p=P))
                elif name[:2] == "wo":
                    load(L, s, ch // 2 + 1, raw[s][:, :].rearrange("p (k n) -> p k n", k=KT),
                         w_out[L, :, 256 * i:256 * i + 256].rearrange("(k p) n -> p k n", p=P))
                else:
                    src = s5_w_glu[L] if name[:3] == "glu" else w_branch[L, {"bg": 0, "bd": 1, "bs": 2}[name[:2]]]
                    load(L, s, ch // 2 + 1, raw[s][:, :].rearrange("p (k n) -> p k n", k=4),
                         src[:, 512 * i:512 * i + 512].rearrange("(k p) n -> p k n", p=P))

            sp.dma_start(c_row[:, :], c.rearrange("a (k p) -> (a k) p", p=P)).then_inc(c_loaded, 16)
            sp.dma_start(x_tok[:, :, :], x.rearrange("a (b p) d -> p (a b) d", p=P)).then_inc(x_loaded, 16)
            sp.dma_start(onehot[:, :], bucket_onehot).then_inc(line_loaded, 16)
            sp.dma_start(rel33[0:NUM_BUCKETS, :], rel_bias).then_inc(line_loaded, 16)
            for l in range(DEPTH):
                def row(dst, src):
                    sp.dma_start(dst, src).then_inc(rows_loaded, 16)

                def rb(a, b):
                    return rows_b[l][a - 72:b - 72, :]

                row(rows_a[l][:, :], b_ada[l].rearrange("(k p) -> k p", p=P))
                row(rb(V_PRE, V_POST), norm_pre[l].rearrange("a (k p) -> (a k) p", p=P))
                row(rb(V_POST, V_GNORM), norm_post[l].rearrange("a (k p) -> (a k) p", p=P))
                row(rb(V_GNORM, V_DNORM), gla_norm[l].rearrange("(k p) -> k p", p=P))
                row(rb(V_DNORM, V_SD), diff_norm[l].rearrange("(k p) -> k p", p=P))
                row(rb(V_SD, V_BGLU), s5_d[l].rearrange("(k g) n -> k (g n)", k=4))
                row(rb(V_BGLU, V_BALPHA), s5_b_glu[l].rearrange("(k p) -> k p", p=P))
                row(rb(V_BALPHA, V_LRE), gla_b_alpha[l].rearrange("(k p) -> k p", p=P))
                row(rb(V_LRE, V_LIM), s5_lam_re[l].rearrange("(j g) p -> j (g p)", g=2))
                row(rb(V_LIM, V_LSTEP), s5_lam_im[l].rearrange("(j g) p -> j (g p)", g=2))
            sp.dma_start(log_steps[:, :, :], s5_log_step.unsqueeze(0).to_broadcast([P, DEPTH, 2 * S5_PAIRS])).then_inc(spread_loaded, 16)
            sp.dma_start(lam_rows[:, :, :, :], diff_lambda.unsqueeze(0).to_broadcast([P, DEPTH, 4, 64])).then_inc(spread_loaded, 16)

            def load_ada(slot, loaded, layer, start):
                columns = slice(start, start + ADA_WIDTH) if isinstance(start, int) else bass.ds(start, ADA_WIDTH)
                sp.dma_start(slot[:, :, :], w_ada[layer, :, columns].rearrange("(k p) n -> p k n", p=P))\
                  .then_inc(loaded, 16)

            for n in range(ADA_AHEAD):
                if n >= 6:
                    sp.wait_ge(first_column, n - 5)
                load_ada(first_ada_w[n % 6], first_ada_loaded[n % 6], 0, n * ADA_WIDTH)

            with sp.Fori(0, DEPTH) as L:
                load_ffn(L, 0, 0, ffn1_w_up, ffn1_w_down)
                for name, _, _ in MIXER[:2]:
                    load_chunk(L, name)
                s = (C_MIX - 1) % 2
                sp.wait_ge(chunk_done[s].sem, slot_value(chunk_done[s], L, C_MIX - 1))
                for i, (b, cc) in enumerate(((s5_b_re, s5_c_re), (s5_b_im, s5_c_im))):
                    sp.dma_start(s5_b[:, i, :, :], b[L].rearrange("(j g) p h -> (g p) j h", g=2)).then_inc(s5w_loaded.sem, 16)
                    for d in range(2):
                        sp.dma_start(s5_cd[:, i, :, d, :], cc[L].rearrange("(q g) n p -> (g n) q p", q=4))\
                          .then_inc(s5w_loaded.sem, 16)
                for name, _, _ in MIXER[2:18]:
                    load_chunk(L, name)
                sp.dma_start(w_alpha[:, :], gla_w_alpha[L]).then_inc(alpha_loaded.sem, 16)
                for name, _, _ in MIXER[18:26]:
                    load_chunk(L, name)
                sp.wait_ge(o_ready.sem, o_ready.of(L, GLA_HEADS))
                sp.wait_ge(line_stored, 32)
                for a in range(P // BIAS_COPIES):
                    lines = bass.AP(tensor=bias_copies.tensor, offset=P - 1 - BIAS_COPIES * a,
                                    ap=[[LINE - 1, BIAS_COPIES], [BIAS_COPIES * LINE, N_MAPS], [1, SEQ]])
                    sp.dma_start(bias_tab[BIAS_COPIES * a:BIAS_COPIES * (a + 1), :, :], lines).then_inc(bias_loaded.sem, 16)
                for name, _, _ in MIXER[26:]:
                    load_chunk(L, name)
                load_ffn(L, 1, C_FFN2, ffn2_w_up, ffn2_w_down)

            for b, copied, n in ((1, out_by_vec, 1), (2, out_by_act, 5), (3, out_by_vec, 2), (0, out_by_act, 6)):
                sp.wait_ge(out_by_act, 4)
                sp.wait_ge(copied, n)
                sp.dma_start(out[0, b * P:(b + 1) * P, :], x_tok[:, b, :]).then_inc(out_stored, 16)
            sp.wait_ge(out_stored, 16 * TB)

        @block.tensor
        def _(pe):
            for s in range(2):
                pe.sem_inc(chunk_done[s].sem, 1)
            pe.sem_inc(ada_column.sem, 3)

            def matmul3(dst, hi, lo, rhi, rlo, first, last):
                pe.matmul(dst, hi, rhi, start=first, stop=False)
                pe.matmul(dst, hi, rlo, start=False, stop=False)
                return pe.matmul(dst, lo, rhi, start=False, stop=last)

            def h_mean_squares(L, ui):
                pe.wait_ge(h_sq_total.sem, h_sq_total.of(L, ui + 1))
                for b in range(TB):
                    i = pe.matmul(bank[MS_BANK[2 * ui]][:, b:b + 1], sq_sum[:, b * P:(b + 1) * P], inv_d[:, 0:1], start=True, stop=True)
                i.then_inc(h_ms_ready.sem, 1)

            def y_mean_squares(L, ui):
                r = 2 * ui + 1
                ms = bank[MS_BANK[r]]
                pe.wait_ge(sq_summed.sem, sq_summed.of(L, (KT - 1) * (ui + 1)))
                pe.wait_ge(sq_ready.sem, sq_ready.of(L, KT * (r + 1)))
                for b in range(TB):
                    pe.matmul(ms[:, b:b + 1], sq_sum[:, b * P:(b + 1) * P], inv_d[:, 0:1], start=True, stop=False)
                    i = pe.matmul(ms[:, b:b + 1], sq_buf[:, (KT - 1) % 3, b * P:(b + 1) * P], inv_d[:, 0:1], start=False, stop=True)
                i.then_inc(y_ms_ready.sem, 1)

            def spread(dst, col):
                for b in range(TB):
                    i = pe.transpose(dst[:, b * P:(b + 1) * P], rstd_tok[:, col + b:col + b + 1].to_broadcast([P, P]), ident[:, :])
                return i

            def rstd_row(L, r):
                pe.wait_ge(inverse_ready.sem, inverse_ready.of(L, r + 1))
                spread(bank[MS_BANK[r] + 1], 0).then_inc(rstd_ready.sem, 1)

            def h_norm(L, ui):
                h_mean_squares(L, ui)
                rstd_row(L, 2 * ui)

            def y_norm(L, ui):
                y_mean_squares(L, ui)
                rstd_row(L, 2 * ui + 1)

            def ffn(L, f, c0):
                ui = 2 * f
                i0 = f * FT

                def up(j):
                    for half in range(2):
                        s = (c0 + half) % 2
                        wh = w_hi[s][:, :].rearrange("p (k n) -> p k n", k=KT)
                        wl = w_lo[s][:, :].rearrange("p (k n) -> p k n", k=KT)
                        pe.wait_ge(lo_split[s].sem, lo_split[s].of(L, (c0 + half) // 2 + j + 1))
                        freed = (silu_done, prod_done)[half]
                        order = [(mt, k) for mt in range(2) for k in range(KT)] if half else \
                            [(mt, k) for k in range(KT) for mt in range(2)]
                        for mt, k in order:
                            if k == 0:
                                pe.wait_ge(freed.sem, freed.of(L, i0 + 2 * j + mt - 1))
                            if half == 0 and mt == 0:
                                pe.wait_ge(u_ready.sem, u_ready.of(L, ui * KT + k + 1))
                            m = matmul3(bank[2 * half + mt][:, :], wh[:, k, mt * P:(mt + 1) * P], wl[:, k, mt * P:(mt + 1) * P],
                                        u_hi[:, k, :], u_lo[:, k, :], k == 0, k == KT - 1)
                            if k == KT - 1:
                                m.then_inc(chunk_done[s].sem if mt else tile_ready.sem, 1)

                with pe.Fori(0, ADA_ROUNDS[f]) as j:
                    up(j)
                    for s in range(3):
                        pe.wait_ge(ada_step.sem, ada_step.of(L, (f * 3 * ADA_ROUNDS[0] + j * 3 + s + 1) * KT))
                        for t in range(2):
                            if f == 0:
                                column = j * 6 + (2 * s + t)
                            else:
                                column = j * 2 + (16 + t) if s == 0 else j * 4 + (2 * (s - 1) + t)
                            m = pe.matmul(bank[7][:, bass.ds(column, 1)], ada_acc[s][:, t * P:(t + 1) * P],
                                          ones[:, 0:1], start=True, stop=True)
                        m.then_inc(ada_column.sem, 1)
                with pe.Fori(ADA_ROUNDS[f], FT // 2) as j:
                    up(j)
                pe.wait_ge(ada_kept.sem, ada_kept.of(L, f + 1))
                c1 = c0 + FT

                def down(s, n, kt, first, last):
                    wh = w_hi[s][:, :].rearrange("p (k n) -> p k n", k=2)
                    wl = w_lo[s][:, :].rearrange("p (k n) -> p k n", k=2)
                    pe.wait_ge(lo_split[s].sem, lo_split[s].of(L, n))
                    pe.wait_ge(g_lo_ready.sem, g_lo_ready.of(L, i0 + kt + 2))
                    order = [(k, m) for m in range(KT) for k in range(2)] if last else \
                        [(k, m) for k in range(2) for m in ((4, 5, 6, 7, 0, 1, 2, 3) if first else range(KT))]
                    for k, m in order:
                        if first and k == 0 and m == 0:
                            pe.wait_ge(silu_done.sem, silu_done.of(L, i0 + FT))
                            pe.wait_ge(prod_done.sem, prod_done.of(L, i0 + FT))
                        if isinstance(kt, int):
                            rh, rl = g_hi[:, kt + k, :], g_lo[:, kt + k, :]
                        else:
                            rh, rl = flat(g_hi[:, cols(kt + k), :]), flat(g_lo[:, cols(kt + k), :])
                        i = matmul3(bank[m][:, :], wh[:, k, m * P:(m + 1) * P], wl[:, k, m * P:(m + 1) * P], rh, rl,
                                    first and k == 0, last and k == 1)
                        if last and k == 1 and m < KT - 1:
                            i.then_inc(tile_ready.sem, 1)
                    i.then_inc(chunk_done[s].sem, 1)
                    if last:
                        y_norm(L, 2 * f)

                down(c1 % 2, c1 // 2 + 1, 0, True, False)
                with pe.Fori(0, FT // 4 - 1) as j:
                    for half in range(2):
                        cc = c1 + 1 + half
                        down(cc % 2, cc // 2 + j + 1, j * 4 + 2 + 2 * half, False, False)
                for d in (FT // 2 - 2, FT // 2 - 1):
                    down((c1 + d) % 2, (c1 + d) // 2 + 1, 2 * d, False, d == FT // 2 - 1)

            def bank_free(L, t):
                last = t.before
                if last is not None and last.engine == "sub":
                    pe.wait_ge(y_copied.sem, y_copied.of(L, KT + last.emptied))
                elif last is not None:
                    pe.wait_ge(emptied[last.engine].sem, emptied[last.engine].of(L, last.emptied))

            def chunk_tile(L, name, k, src=None):
                ch = CHUNK_OF[name]
                s = ch % 2
                if k == 0:
                    pe.wait_ge(lo_split[s].sem, slot_value(lo_split[s], L, ch))
                t = TILES[name, k]
                bank_free(L, t)
                hi, lo, n, ready = src or (u_hi, u_lo, KT, None)
                w = 512 if n == 4 else chunk_widths(name)
                wh = w_hi[s][:, 0:n * w].rearrange("p (k n) -> p k n", k=n)
                wl = w_lo[s][:, 0:n * w].rearrange("p (k n) -> p k n", k=n)
                for kt in range(n):
                    if k == 0 and ready is not None:
                        pe.wait_ge(split_lo.sem, split_lo.of(L, ready + kt + 1))
                    m = matmul3(bank[t.bank][:, :], wh[:, kt, k * P:(k + 1) * P], wl[:, kt, k * P:(k + 1) * P],
                                hi[:, kt, :], lo[:, kt, :], kt == 0, kt == n - 1)
                m.then_inc(chunk_done[s].sem if t.last else tile_ready.sem, 1)

            def first_chunk(L, name):
                ch = CHUNK_OF[name]
                s = ch % 2
                wh = w_hi[s][:, :].rearrange("p (k n) -> p k n", k=KT)
                wl = w_lo[s][:, :].rearrange("p (k n) -> p k n", k=KT)
                pe.wait_ge(lo_split[s].sem, slot_value(lo_split[s], L, ch))
                for kt in range(KT):
                    pe.wait_ge(u_ready.sem, u_ready.of(L, KT + kt + 1))
                    for k in range(2):
                        m = matmul3(bank[TILES[name, k].bank][:, :], wh[:, kt, k * P:(k + 1) * P], wl[:, kt, k * P:(k + 1) * P],
                                    u_hi[:, kt, :], u_lo[:, kt, :], kt == 0, kt == KT - 1)
                        if kt == KT - 1:
                            m.then_inc(chunk_done[s].sem if k else tile_ready.sem, 1)

            def value_tile(L, name, k):
                ch = CHUNK_OF[name]
                s = ch % 2
                if k == 0:
                    pe.wait_ge(lo_split[s].sem, slot_value(lo_split[s], L, ch))
                t = TILES[name, k]
                bank_free(L, t)
                wh = w_hi[s][:, :].rearrange("p (k n) -> p k n", k=KT)
                wl = w_lo[s][:, :].rearrange("p (k n) -> p k n", k=KT)
                for half in range(2):
                    b = 2 * k + half
                    dst = bank[t.bank][:, half * 256:(half + 1) * 256]
                    tok = slice(b * P, (b + 1) * P)
                    for kt in range(KT):
                        pe.matmul(dst, u_hi[:, kt, tok], wh[:, kt, :], start=kt == 0, stop=False)
                        pe.matmul(dst, u_lo[:, kt, tok], wh[:, kt, :], start=False, stop=False)
                        m = pe.matmul(dst, u_hi[:, kt, tok], wl[:, kt, :], start=False, stop=kt == KT - 1)
                m.then_inc(chunk_done[s].sem if t.last else tile_ready.sem, 1)

            def s5_matrices(L):
                pe.wait_ge(s5_bx_ready.sem, s5_bx_ready.of(L, 1))
                for i in range(2):
                    for q in range(4):
                        m = pe.transpose(bank[4 + i][:, q * P:(q + 1) * P],
                                         s5_bx[:, i, q].rearrange("p a g h -> p (a g h)"), ident[:, :])
                m.then_inc(s5_turned.sem, 1)
                pe.wait_ge(s5w_loaded.sem, s5w_loaded.of(L, 16 * 6))
                for i in range(2):
                    for q in range(4):
                        m = pe.transpose(bank[6 + i][:, q * P:(q + 1) * P],
                                         s5_cd[:, i, q].rearrange("p a n -> p (a n)"), ident[:, :])
                m.then_inc(s5_turned.sem, 1)

            def s5_in(L, j):
                q, i = divmod(j, 4)
                if j == 0:
                    pe.wait_ge(s5_mats_ready.sem, s5_mats_ready.of(L, 1))
                else:
                    pe.wait_ge(front_done.sem, front_done.of(L, j))
                t = TILES[("su0", q) if q < 2 else (f"su{q - 1}", 0)]
                pe.wait_ge(emptied["act"].sem, emptied["act"].of(L, t.emptied))
                rows = slice(32 * i, 32 * i + 32)
                for part in range(2):
                    m = pe.matmul(bank[4 + part][:, :], s5_bt[rows, part, q, :], su[rows, q, :], start=True, stop=True)
                m.then_inc(bu_ready.sem, 1)

            def s5_out(L, j):
                q, i = divmod(j, 4)
                if i == 0 and q >= 2:
                    pe.wait_ge(s5_y_summed.sem, s5_y_summed.of(L, q - 1))
                pe.wait_ge(state_ready.sem, state_ready.of(L, 2 * j + 2))
                for part in range(2):
                    m = pe.matmul(bank[6 + q % 2][32 * i:32 * i + 32, :], s5_ct[:, part, q, 32 * i:32 * i + 32],
                                  rot[j % 3][:, part, :], start=part == 0, stop=part == 1)
                m.then_inc(s5_y_ready.sem, 1)

            def gla_alpha(L):
                pe.wait_ge(alpha_loaded.sem, alpha_loaded.of(L, 16))
                pe.wait_ge(emptied["act"].sem, emptied["act"].of(L, TILES["ga", 0].emptied))
                for t in range(2):
                    pe.matmul(bank[4 + t][:, :], w_alpha[:, t * P:(t + 1) * P], a_low[:, :], start=True, stop=True)\
                      .then_inc(alpha_ready.sem, 1)

            def gla_turn_keys(L):
                pe.wait_ge(gla_keys.sem, gla_keys.of(L, 6))
                for b in range(TB):
                    for t in range(2):
                        m = pe.transpose(bank[4 + b // 2][:, (b % 2) * 256 + t * P:(b % 2) * 256 + (t + 1) * P],
                                         gk[:, t, b * P:(b + 1) * P], ident[:, :])
                m.then_inc(kk_turned.sem, 1)

            def gla_states(L, t):
                if t == 0:
                    pe.wait_ge(kk_copied.sem, kk_copied.of(L, 2))
                else:
                    pe.wait_ge(s_ready.sem, s_ready.of(L, 1))
                pe.sem_inc(states_begun.sem, 1)
                for n in range(N_GCH - 1):
                    b, rows = n // 2, slice(64 * (n % 2), 64 * (n % 2) + 64)
                    for par in range(2):
                        hd = 2 * t + par
                        m = pe.matmul(bank[6 + n % 2][64 * par:64 * par + 64, (n // 2) * P:(n // 2 + 1) * P],
                                      kk_tok[rows, b, t * P + 64 * par:t * P + 64 * par + 64],
                                      gv[rows, b, hd * P:(hd + 1) * P], start=True, stop=True)
                m.then_inc(ds_ready.sem, 1)

            def gla_scores(L, hd):
                t, par = divmod(hd, 2)
                rows = slice(64 * par, 64 * par + 64)
                if hd == 0:
                    pe.wait_ge(kk_copied.sem, kk_copied.of(L, 2))
                else:
                    pe.wait_ge(att_clamped.sem, att_clamped.of(L, hd))
                for b in range(TB):
                    blk = slice(b * P, (b + 1) * P)
                    m = pe.matmul(bank[4][:, blk], la[rows, t, blk], gq[rows, t, blk], start=True, stop=True)
                m.then_inc(att_ready.sem, 1)

            def head_ms(L, hh, bk):
                pe.wait_ge(o_squared.sem, o_squared.of(L, hh + 1))
                pe.wait_ge(o_copied.sem, o_copied.of(L, hh + 1))
                for b in range(TB):
                    m = pe.matmul(bank[bk][:, b:b + 1], o_sq[:, b * P:(b + 1) * P], inv_d[:, 1:2], start=True, stop=True)
                m.then_inc(o_ms.sem, 1)

            def gla_out(L, hd):
                t, par = divmod(hd, 2)
                rows = slice(64 * par, 64 * par + 64)
                bk = 6 + hd % 2
                pe.wait_ge(att_clamped.sem, att_clamped.of(L, hd + 1))
                pe.wait_ge(s_ready.sem, s_ready.of(L, 2))
                if hd >= 2:
                    pe.wait_ge(o_ms_kept.sem, o_ms_kept.of(L, hd - 1))
                for b in range(TB):
                    pe.matmul(bank[bk][:, b * P:(b + 1) * P], gv[:, b, hd * P:(hd + 1) * P], att[:, hd % 2, b, :],
                              start=True, stop=False)
                    for n in (2 * b, 2 * b + 1):
                        if n:
                            tok = slice(n * GLA_CHUNK, (n + 1) * GLA_CHUNK)
                            m = pe.matmul(bank[bk][:, tok], s_state[rows, t, n, :], gq[rows, t, tok], start=False, stop=n % 2 == 1)
                m.then_inc(o_ready.sem, 1)

            def head_rstd(L, hh, bk):
                pe.wait_ge(o_inverse.sem, o_inverse.of(L, hh // 4 + 1))
                if hh % 4 >= 2:
                    pe.wait_ge(o_normed.sem, o_normed.of(L, hh - 1))
                spread(bank[bk], 4 * (hh % 4)).then_inc(o_rstd.sem, 1)

            def diff_scores(L, hd, qb):
                i = hd * TB + qb
                n = (qb + 1) * P
                if i == 0:
                    pe.wait_ge(o_normed.sem, o_normed.of(L, 4))
                else:
                    pe.wait_ge(max_ready.sem, max_ready.of(L, i))
                for par in range(2):
                    rows = slice(64 * par, 64 * par + 64)
                    pe.matmul(bank[4 + par][:, 0:n], dq[rows, hd, qb * P:(qb + 1) * P], dk[rows, hd, 0:n],
                              start=True, stop=True).then_inc(scores_ready.sem, 1)

            def diff_turn(L, hd, qb):
                i = hd * TB + qb
                pe.wait_ge(mix_ready.sem, mix_ready.of(L, i + 1))
                if i:
                    pe.wait_ge(at_copied.sem, at_copied.of(L, i))
                for j in range(qb + 1):
                    m = pe.transpose(bank[6][:, j * P:(j + 1) * P], prob[i % 2][:, 0, j * P:(j + 1) * P], ident[:, :])
                m.then_inc(at_ready.sem, 1)

            def diff_out(L, hd):
                pe.wait_ge(at_copied.sem, at_copied.of(L, (hd + 1) * TB))
                pe.wait_ge(o_ms_kept.sem, o_ms_kept.of(L, 4 + hd))
                for j in range(TB):
                    m = pe.matmul(bank[7][:, j * P:SEQ], dv[:, j, hd * P:(hd + 1) * P], a_t[:, j, j * P:SEQ],
                                  start=j == 0, stop=j == TB - 1)
                m.then_inc(o_ready.sem, 1)

            def mixer(L):
                first_chunk(L, "su0")
                chunk_tile(L, "su1", 0)
                chunk_tile(L, "su2", 0)
                s5_matrices(L)
                s5_in(L, 0)
                done = 0
                gaps = 0
                for name, n, _ in MIXER[3:14]:
                    for k in range(n):
                        (value_tile if name[:2] == "gv" else chunk_tile)(L, name, k)
                        gaps += 1
                        while done < min(S5_PAIRS, (gaps * S5_PAIRS) // S5_PACE):
                            if done + 1 < S5_PAIRS:
                                s5_in(L, done + 1)
                            if done >= 2:
                                s5_out(L, done - 2)
                            done += 1
                s5_out(L, S5_PAIRS - 2)
                s5_out(L, S5_PAIRS - 1)
                for name in ("glu1", "glu0"):
                    for k in range(4):
                        chunk_tile(L, name, k, (yg_hi, yg_lo, 4, YG))
                for name in ("bs0", "bs1"):
                    for k in range(4):
                        chunk_tile(L, name, k, (ys_hi, ys_lo, 4, YS))
                gla_alpha(L)
                for k in range(2):
                    chunk_tile(L, "dq0", k)
                for k in range(2):
                    chunk_tile(L, "dq1", k)
                gla_turn_keys(L)
                for k in range(2):
                    chunk_tile(L, "dk0", k)
                gla_states(L, 0)
                gla_scores(L, 0)
                for k in range(2):
                    chunk_tile(L, "dk1", k)
                gla_states(L, 1)
                gla_scores(L, 1)
                value_tile(L, "dv0", 0)
                for hd in range(GLA_HEADS):
                    gla_out(L, hd)
                    if hd + 2 < GLA_HEADS:
                        gla_scores(L, hd + 2)
                    if hd < 3:
                        value_tile(L, *(("dv0", 1), ("dv1", 0), ("dv1", 1))[hd])
                    head_ms(L, hd, 6 + hd % 2)
                for k in range(2):
                    chunk_tile(L, "gg0", k)
                for hd in range(GLA_HEADS):
                    head_rstd(L, hd, 4 + hd % 2)
                diff_scores(L, 0, 0)
                for i in range(DIFF_HEADS * TB):
                    hd, qb = divmod(i, TB)
                    if i + 1 < DIFF_HEADS * TB:
                        diff_scores(L, *divmod(i + 1, TB))
                    if hd and qb == 0:
                        diff_out(L, hd - 1)
                    for name, k in BESIDE_DIFF[i]:
                        chunk_tile(L, name, k, (yga_hi, yga_lo, 4, YGA) if name[0] == "b" else None)
                    if hd and qb == 0:
                        head_ms(L, 4 + hd - 1, 7)
                    diff_turn(L, hd, qb)
                chunk_tile(L, "gd1", 0)
                diff_out(L, DIFF_HEADS - 1)
                chunk_tile(L, "gd1", 1)
                head_ms(L, 4 + DIFF_HEADS - 1, 7)
                for hd in range(DIFF_HEADS):
                    head_rstd(L, 4 + hd, 4 + hd % 2)
                for name, n in (("gd2", 2), ("gd3", 2), ("bd0", 4), ("bd1", 4)):
                    for k in range(n):
                        chunk_tile(L, name, k, (yd_hi, yd_lo, 4, YD) if name[0] == "b" else None)
                for name, n, _ in MIXER[36:]:
                    for k in range(n):
                        chunk_tile(L, name, k, (mg_hi, mg_lo, 8, MG))
                y_norm(L, 1)

            pe.wait_ge(const_ready, 4)
            pe.wait_ge(c_loaded, 16)
            pe.transpose(bank[7][:, 0:KT], c_row[:, :], ident[0:KT, 0:KT]).then_inc(c_turned, 1)
            pe.wait_ge(x_loaded, 16)
            for m in range(6):
                for b in range(TB):
                    i = pe.transpose(bank[m][:, b * P:(b + 1) * P], x_tok[:, b, m * P:(m + 1) * P], ident[:, :])
                i.then_inc(x_turned, 1)
            pe.wait_ge(line_loaded, 32)
            for m in range(6, 8):
                pe.wait_ge(h_by_vector.sem, m - 5)
                for b in range(TB):
                    i = pe.transpose(bank[m - 6][:, b * P:(b + 1) * P], x_tok[:, b, m * P:(m + 1) * P], ident[:, :])
                i.then_inc(x_turned, 1)
            pe.matmul(bank[6][0:N_MAPS, :], rel33[:, :], onehot[:, 0:SEQ], start=True, stop=True).then_inc(line_made, 1)
            pe.wait_ge(cond_ready, 1)
            pe.matmul(bank[7][0:N_MAPS, 0:P], rel33[:, :], onehot[:, SEQ:LINE], start=True, stop=True).then_inc(line_made, 1)
            pe.wait_ge(line_copied, 2)
            pe.wait_ge(rows_loaded, 16 * 10 * DEPTH)
            for l in range(DEPTH):
                pe.transpose(bank[6][:, l * V_LOADED:l * V_LOADED + 72], rows_a[l][:, :], ident[0:72, 0:72])
                i = pe.transpose(bank[6][:, l * V_LOADED + 72:(l + 1) * V_LOADED], rows_b[l][:, :],
                                 ident[0:V_LOADED - 72, 0:V_LOADED - 72])
            i.then_inc(rows_turned, 1)
            for n in (0, 1, 2, 6, 7):
                pe.wait_ge(first_ada_loaded[n % 6], 16 * (n // 6 + 1))
                for t in range(2):
                    for k in range(KT):
                        m = pe.matmul(bank[7][:, 2 * n + t:2 * n + t + 1], first_ada_w[n % 6][:, k, t * P:(t + 1) * P],
                                      cond[:, k:k + 1], start=k == 0, stop=k == KT - 1)
                m.then_inc(first_column, 1)
            for n in (3, 4, 5):
                pe.wait_ge(first_ada_step, (n - 2) * KT)
                for t in range(2):
                    m = pe.matmul(bank[7][:, 2 * n + t:2 * n + t + 1], first_ada_acc[n - 3][:, t * P:(t + 1) * P], ones[:, 0:1],
                                  start=True, stop=True)
                m.then_inc(first_column, 1)

            pe.wait_ge(h_by_vector.sem, len(ADDED_BY_VECTOR))
            with pe.Fori(0, DEPTH) as L:
                h_norm(L, 0)
                ffn(L, 0, 0)
                h_norm(L, 1)
                mixer(L)
                h_norm(L, 2)
                ffn(L, 1, C_FFN2)

            def out_turn(m, b):
                return pe.transpose(bank[2 * b + m // 4][:, (m % 4) * P:(m % 4 + 1) * P], h[:, m, b * P:(b + 1) * P], ident[:, :])

            for m in range(KT):
                for tiles, added in ((ADDED_BY_VECTOR, h_by_vector), (ADDED_BY_POOL, h_by_pool)):
                    if m in tiles:
                        pe.wait_ge(added.sem, added.of(DEPTH, tiles.index(m) + 1 - len(tiles)))
                for b in range(TB) if m < 4 else (1, 2, 3):
                    i = out_turn(m, b)
                    if m % 4 == 3:
                        i.then_inc(out_turned, 1)
            for m in range(4, KT):
                i = out_turn(m, 0)
            i.then_inc(out_turned, 1)

        @block.scalar
        def _(act):
            for s in range(2):
                act.sem_inc(hi_split[s].sem, 1)
            act.sem_inc(silu_done.sem, 2)

            def split(L, s, n, elems=CHUNK_ELEMS):
                act.wait_ge(raw_loaded[s].sem, raw_loaded[s].of(L, 16 * n))
                act.wait_ge(chunk_done[s].sem, chunk_done[s].of(L, n - 1))
                act.activation(w_hi[s][:, 0:elems], raw[s][:, 0:elems], ACT.Copy).then_inc(hi_split[s].sem, 1)

            def split_chunk(L, name):
                ch = CHUNK_OF[name]
                split(L, ch % 2, ch // 2 + 1, KT * P if chunk_widths(name) == P else CHUNK_ELEMS)

            def root(ready, L, ui, r):
                act.wait_ge(ready.sem, ready.of(L, ui + 1))
                act.activation(sq_root[:, 0:TB], bank[MS_BANK[r]][:, 0:TB], ACT.Sqrt, bias=EPS_COL).then_inc(root_ready.sem, 1)

            def h_squares(L, ui):
                for m in range(KT):
                    for tiles, added in ((ADDED_BY_VECTOR, h_by_vector), (ADDED_BY_POOL, h_by_pool)):
                        if m in tiles:
                            act.wait_ge(added.sem, added.of(L, (ui - 1) * len(tiles) + tiles.index(m) + 1))
                    if m >= 3:
                        act.wait_ge(h_sq_summed.sem, h_sq_summed.of(L, H_SUMMED * ui + m - 2))
                    act.activation(sq_buf[:, m % 3, :], h[:, m, :], ACT.Square).then_inc(sq_ready.sem, 1)
                root(h_ms_ready, L, ui, 2 * ui)

            def modulate(L, ui):
                for m in range(KT):
                    act.wait_ge(modulated.sem, modulated.of(L, ui * KT + m + 1))
                    act.activation(u_hi[:, m, :], mod_buf[:, m % 2, :], ACT.Identity,
                                   bias=ada[:, 24 * ui + m:24 * ui + m + 1]).then_inc(u_hi_ready.sem, 1)

            def y_tile(L, ui, m, bk, wait):
                r = 2 * ui + 1
                wait()
                if m >= 3:
                    act.wait_ge(sq_summed.sem, sq_summed.of(L, (KT - 1) * ui + m - 2))
                act.activation(sq_buf[:, m % 3, :], bank[bk][:, :], ACT.Square).then_inc(sq_ready.sem, 1)
                act.activation(y_sub[:, m, :], bank[bk][:, :], ACT.Copy).then_inc(y_copied.sem, 1)

            def ffn(L, f, c0):
                i0 = f * FT
                with act.Fori(0, FT // 2) as j:
                    split(L, c0 % 2, (c0 + 2) // 2 + j + 1)
                    for mt in range(2):
                        i = i0 + 2 * j + mt
                        if mt:
                            s = c0 % 2
                            act.wait_ge(chunk_done[s].sem, chunk_done[s].of(L, c0 // 2 + j + 1))
                        else:
                            act.wait_ge(tile_ready.sem, tile_ready.of(L, f * READY_BEFORE_FFN2 + 2 * j + 1))
                        act.wait_ge(g_lo_ready.sem, g_lo_ready.of(L, i - 1))
                        act.activation(silu_buf[:, mt, :], bank[mt][:, :], ACT.Silu).then_inc(silu_done.sem, 1)
                    for mt in range(2):
                        i = i0 + 2 * j + mt
                        act.wait_ge(prod_done.sem, prod_done.of(L, i + 1))
                        act.activation(flat(g_hi[:, cols(j * 2 + mt), :]), silu_buf[:, mt, :], ACT.Copy).then_inc(g_hi_ready.sem, 1)
                    split(L, (c0 + 1) % 2, (c0 + 3) // 2 + j + 1)
                c1 = c0 + FT
                split(L, c1 % 2, (c1 + 2) // 2 + 1)
                with act.Fori(0, (FT // 2 - 3) // 2) as j:
                    for half in range(2):
                        cc = c1 + 3 + half
                        split(L, cc % 2, cc // 2 + j + 1)
                if f == 0:
                    split_chunk(L, "su0")
                s = (c1 + FT // 2 - 1) % 2
                for m in range(KT):
                    def wait():
                        if m < KT - 1:
                            act.wait_ge(tile_ready.sem, tile_ready.of(L, f * READY_BEFORE_FFN2 + FT + m + 1))
                        else:
                            act.wait_ge(chunk_done[s].sem, slot_value(chunk_done[s], L, c1 + FT // 2 - 1))
                    y_tile(L, 2 * f, m, m, wait)
                root(y_ms_ready, L, 2 * f, 4 * f + 1)

            def tile_wait(L, name, k):
                t = TILES[name, k]
                if t.last:
                    s = t.chunk % 2
                    act.wait_ge(chunk_done[s].sem, slot_value(chunk_done[s], L, t.chunk))
                else:
                    act.wait_ge(tile_ready.sem, tile_ready.of(L, t.ready))
                return bank[t.bank]

            def empty(L, name, k):
                b = tile_wait(L, name, k)
                i = int(name[-1]) if name[-1].isdigit() else 0
                kind = name[:2]
                if kind == "su":
                    q = k if i == 0 else i + 1
                    ins = act.activation(su[:, q, :], b[:, :], ACT.Copy)
                elif kind in ("gq", "gk"):
                    ins = act.activation((gq if kind == "gq" else gk)[:, k, :], b[:, :], ACT.Copy)
                elif kind == "ga":
                    ins = act.activation(a_low[:, :], b[0:LOWRANK, :], ACT.Copy)
                elif kind in ("gv", "dv"):
                    dst = (gv if kind == "gv" else dv)[:, 2 * k:2 * k + 2, i * 256:(i + 1) * 256]
                    ins = act.activation(dst, b[:, :].rearrange("p (a n) -> p a n", a=2), ACT.Copy)
                elif kind == "gr":
                    ins = act.activation(gr[:, 2 * i + k, :], b[:, :], ACT.Silu)
                elif kind == "gs":
                    ins = act.activation(merged[:, 2 * i + k, :], b[:, :], ACT.Sigmoid)
                elif kind == "gl":
                    ins = act.activation(z_gate[:, k, :], b[:, :], ACT.Sigmoid, bias=vec[:, V_BGLU + 4 + k:V_BGLU + 5 + k])
                elif kind == "dq":
                    ins = act.activation(dq[:, 2 * i + k, :], b[:, :], ACT.Copy, scale=0.125)
                elif kind == "dk":
                    ins = act.activation(dk[:, 2 * i + k, :], b[:, :], ACT.Copy)
                else:
                    t4 = (2 * i + k) % 4
                    n = {"gg": 0, "gd": 8}[kind] + (2 * i + k)
                    if 4 <= n < 12:
                        act.wait_ge(merged_ready.sem, merged_ready.of(L, n - 3))
                    ins = act.activation((sig if n < 12 else sig_late)[:, t4, :], b[:, :], ACT.Sigmoid)
                ins.then_inc(emptied["act"].sem, 1)

            def make_tables(L, j):
                act.wait_ge(turns_ready.sem, turns_ready.of(L, j + 1))
                if j >= 3:
                    act.wait_ge(back_done.sem, back_done.of(L, j - 2))
                act.activation(tab_s[:, j % 3, :], turns[:, j % 2, :], ACT.Sin, scale=6.283185)
                st.did(act.activation(turns[:, j % 2, :], turns[:, j % 2, :], ACT.Abs))
                st.wait()
                act.activation(tab_c[:, j % 3, :], turns[:, j % 2, :], ACT.Sin, scale=-6.283185, bias=HALF_PI)\
                   .then_inc(tables_ready.sem, 1)

            def split_tile(L, base, k, dst, src):
                act.activation(dst[:, k, :], src, ACT.Copy).then_inc(split_hi.sem, 1)

            def head_squares(L, hh, bk):
                act.wait_ge(o_ready.sem, o_ready.of(L, hh + 1))
                dst = o_head[hh][:, :] if hh < 4 else dq[:, hh - 4, :]
                act.activation(dst, bank[bk][:, :], ACT.Copy).then_inc(o_copied.sem, 1)
                if hh:
                    act.wait_ge(o_ms.sem, o_ms.of(L, hh))
                act.activation(o_sq[:, :], bank[bk][:, :], ACT.Square).then_inc(o_squared.sem, 1)

            def head_roots(L, g):
                act.wait_ge(o_ms_kept.sem, o_ms_kept.of(L, 4 * g + 4))
                act.activation(sq_root[:, 0:16], ms_heads[:, :], ACT.Sqrt, bias=EPS_COL).then_inc(o_roots.sem, 1)

            def diff_exp(L, i):
                hd, qb = divmod(i, TB)
                n = (qb + 1) * P
                act.wait_ge(max_ready.sem, max_ready.of(L, i + 1))
                sm = smax[:, i % 2, :]
                for par in range(2):
                    ins = act.activation(prob[i % 2][:, par, 0:n], prob[i % 2][:, par, 0:n], ACT.Exp, bias=sm[:, 2 + par:3 + par],
                                         accum_out=sm[:, 4 + par:5 + par])
                    st.did(ins) if par == 0 else ins.then_inc(prob_ready.sem, 1)
                st.wait()

            def diff_copy(L, i):
                hd, qb = divmod(i, TB)
                act.wait_ge(at_ready.sem, at_ready.of(L, i + 1))
                if qb == 0 and hd:
                    act.wait_ge(o_ready.sem, o_ready.of(L, 4 + hd))
                act.activation(a_t[:, 0:qb + 1, qb * P:(qb + 1) * P],
                               bank[6][:, 0:(qb + 1) * P].rearrange("p (a n) -> p a n", n=P), ACT.Copy).then_inc(at_copied.sem, 1)

            act.wait_ge(c_turned, 1)
            act.activation(cond[:, :], bank[7][:, 0:KT], ACT.Silu).then_inc(cond_ready, 1)
            act.wait_ge(line_made, 2)
            act.activation(bias_line[:, 0:SEQ], bank[6][0:N_MAPS, :], ACT.Copy).then_inc(line_copied, 1)
            act.activation(bias_line[:, SEQ:LINE], bank[7][0:N_MAPS, 0:P], ACT.Copy).then_inc(line_copied, 1)
            act.wait_ge(line_copied, 2)
            act.dma_start(bias_dram, bias_line[:, :]).then_inc(line_stored, 16)
            act.wait_ge(theta_ready, 1)
            act.activation(pscr[:, 8], pscr[:, 3], ACT.Sin).then_inc(sines_ready, 1)
            act.activation(pscr[:, 9], pscr[:, 3], ACT.Sin, scale=0.5).then_inc(sines_ready, 1)
            act.wait_ge(lam_sums, 2 * DEPTH)
            act.activation(small[:, 8:8 + 2 * DEPTH], small[:, 0:2 * DEPTH], ACT.Exp).then_inc(lam_exps, 1)

            act.wait_ge(line_stored, 16)
            act.dma_start(bias_copies, bias_dram.unsqueeze(1).to_broadcast([N_MAPS, BIAS_COPIES, LINE])).then_inc(line_stored, 16)

            with act.Fori(0, DEPTH) as L:
                st = Steps(act, scalar_steps, L)
                h_squares(L, 0)
                split(L, 0, 1)
                split(L, 1, 1)
                modulate(L, 0)
                ffn(L, 0, 0)
                h_squares(L, 1)
                split_chunk(L, "su1")
                modulate(L, 1)
                for i in range(3):
                    if i:
                        split_chunk(L, MIXER[i + 1][0])
                    for k in range(MIXER[i][1]):
                        empty(L, MIXER[i][0], k)
                make_tables(L, 0)
                make_tables(L, 1)
                done = 0
                gaps = 0
                for i in range(3, 14):
                    name, n, _ = MIXER[i]
                    split_chunk(L, MIXER[i + 1][0])
                    for k in range(n):
                        if gaps < S5_SIDE_TILES - 1:
                            empty(L, name, k)
                        gaps += 1
                        while done < min(S5_PAIRS, (gaps * S5_PAIRS) // S5_PACE):
                            if done + 2 < S5_PAIRS:
                                make_tables(L, done + 2)
                            done += 1
                for q in range(4):
                    act.wait_ge(s5_y_summed.sem, s5_y_summed.of(L, q + 1))
                    act.activation(su[:, q, :], su[:, q, :], ACT.Gelu_apprx_tanh).then_inc(gelu_done.sem, 1)
                for q in range(4):
                    act.wait_ge(gelu_done.sem, gelu_done.of(L, q + 1))
                    split_tile(L, YG, q, yg_hi, su[:, q, :])
                empty(L, "gs3", 1)
                split_chunk(L, "glu0")
                for k in range(4):
                    act.wait_ge(split_lo.sem, split_lo.of(L, YG + k + 1))
                    empty(L, "glu1", k)
                split_chunk(L, "bs0")
                for q in range(4):
                    act.wait_ge(emptied["vec"].sem, emptied["vec"].of(L, TILES["glu0", q].emptied))
                    split_tile(L, YS, q, ys_hi, z_gate[:, q, :])
                split_chunk(L, "bs1")
                split_chunk(L, "dq0")
                for t in range(2):
                    act.wait_ge(alpha_read.sem, alpha_read.of(L, t + 1))
                    st.did(act.activation(la[:, t, :], bank[4 + t][:, :], ACT.Abs, bias=vec[:, V_BALPHA + t:V_BALPHA + t + 1]))
                st.wait()
                st.did(act.activation(la[:, :, :], la[:, :, :], ACT.Exp, scale=-1.0))
                st.wait()
                act.activation(la[:, :, :], la[:, :, :], ACT.Ln, bias=1.0).then_inc(alpha_exps.sem, 1)
                split_chunk(L, "dq1")
                for t in range(2):
                    act.wait_ge(decay_sum.sem, decay_sum.of(L, t + 1))
                    act.activation(eb[:, t, :], lb[:, t, :], ACT.Exp, scale=1.0 / GLA_TAU).then_inc(gla_exps.sem, 1)
                    act.activation(la[:, t, :], lb[:, t, :], ACT.Exp, scale=-1.0 / GLA_TAU).then_inc(gla_exps.sem, 1)
                for t in range(2):
                    act.wait_ge(decay_last.sem, decay_last.of(L, t + 1))
                    act.activation(lb[:, t, :], lb[:, t, :], ACT.Exp, scale=1.0 / GLA_TAU).then_inc(gla_exps.sem, 1)
                for k in range(2):
                    empty(L, "dq0", k)
                split_chunk(L, "dk0")
                for k in range(2):
                    empty(L, "dq1", k)
                act.wait_ge(kk_turned.sem, kk_turned.of(L, 1))
                for i in range(2):
                    act.activation(kk_tok[:, 2 * i:2 * i + 2, :], bank[4 + i][:, :].rearrange("p (a n) -> p a n", a=2),
                                   ACT.Copy).then_inc(kk_copied.sem, 1)
                split_chunk(L, "dk1")
                for k in range(2):
                    empty(L, "dk0", k)
                split_chunk(L, "dv0")
                for k in range(2):
                    empty(L, "dk1", k)
                split_chunk(L, "dv1")
                empty(L, "dv0", 0)
                for hd in range(GLA_HEADS):
                    head_squares(L, hd, 6 + hd % 2)
                    if hd < 3:
                        empty(L, *(("dv0", 1), ("dv1", 0), ("dv1", 1))[hd])
                    if hd == 1:
                        split_chunk(L, "gg0")
                head_roots(L, 0)
                split_chunk(L, "gg1")
                for k in range(2):
                    empty(L, "gg0", k)
                act.wait_ge(yga_done.sem, yga_done.of(L, 4))
                for k in range(4):
                    split_tile(L, YGA, k, yga_hi, gr[:, k, :])
                splits = {0: "bg0", 2: "gg2", 6: "gg3", 8: "bg1", 10: "gd0", 14: "gd1"}
                diff_exp(L, 0)
                for i in range(DIFF_HEADS * TB):
                    hd, qb = divmod(i, TB)
                    if i in splits:
                        split_chunk(L, splits[i])
                    if i + 1 < DIFF_HEADS * TB:
                        diff_exp(L, i + 1)
                    if hd and qb == 0:
                        head_squares(L, 4 + hd - 1, 7)
                    for name, k in BESIDE_DIFF[i]:
                        if name[0] == "g":
                            empty(L, name, k)
                    diff_copy(L, i)
                split_chunk(L, "gd2")
                empty(L, "gd1", 0)
                head_squares(L, 4 + DIFF_HEADS - 1, 7)
                empty(L, "gd1", 1)
                head_roots(L, 1)
                split_chunk(L, "gd3")
                for k in range(4):
                    act.wait_ge(o_normed.sem, o_normed.of(L, 4 + k + 1))
                    if k == 0:
                        t = TILES["bg1", 3]
                        act.wait_ge(chunk_done[t.chunk % 2].sem, slot_value(chunk_done[t.chunk % 2], L, t.chunk))
                    split_tile(L, YD, k, yd_hi, dq[:, k, :])
                for k in range(2):
                    empty(L, "gd2", k)
                split_chunk(L, "bd0")
                for k in range(2):
                    empty(L, "gd3", k)
                split_chunk(L, "bd1")
                split_chunk(L, "wo0")
                for m in range(KT):
                    act.wait_ge(merged_ready.sem, merged_ready.of(L, 8 + m + 1))
                    if m == 0:
                        act.wait_ge(split_lo.sem, split_lo.of(L, YD + 4))
                    split_tile(L, MG, m, mg_hi, merged[:, m, :])
                split_chunk(L, "wo1")
                for i in range(4):
                    if i >= 1 and i + 1 < 4:
                        split_chunk(L, f"wo{i + 1}")
                    if i == 3:
                        split(L, C_FFN2 % 2, C_FFN2 // 2 + 1)
                    for k in range(2):
                        t = TILES[f"wo{i}", k]
                        y_tile(L, 1, 2 * i + k, t.bank, lambda: tile_wait(L, f"wo{i}", k))
                root(y_ms_ready, L, 1, 3)
                h_squares(L, 2)
                split(L, (C_FFN2 + 1) % 2, (C_FFN2 + 1) // 2 + 1)
                modulate(L, 2)
                ffn(L, 1, C_FFN2)
                assert st.n == SCALAR_STEPS, st.n

            for b in range(TB):
                act.wait_ge(out_turned, b + 1)
                act.activation(x_tok[:, b, 0:SEQ], bank[2 * b][:, :], ACT.Copy).then_inc(out_by_act, 1)
            for b, n in ((2, 6), (0, 8)):
                act.wait_ge(out_turned, n)
                act.activation(x_tok[:, b, SEQ:D_MODEL], bank[2 * b + 1][:, :], ACT.Copy).then_inc(out_by_act, 1)

        @block.vector
        def _(v):
            for s in range(2):
                v.sem_inc(lo_split[s].sem, 1)
            v.sem_inc(prod_done.sem, 2)
            v.sem_inc(g_lo_ready.sem, 2)
            v.sem_inc(ada_step.sem, 3 * KT)

            def stt(o, a, s, b, op0, op1):
                return v.scalar_tensor_tensor(out=o, in0=a, scalar=s, in1=b, op0=op0, op1=op1)

            MUL, ADD, SUB = ALU.mult, ALU.add, ALU.subtract

            def split(L, s, n):
                v.wait_ge(hi_split[s].sem, hi_split[s].of(L, n))
                v.tensor_tensor(w_lo[s][:, :], raw[s][:, :], w_hi[s][:, :].bitcast(F32), SUB).then_inc(lo_split[s].sem, 1)

            def rstd(L, r):
                v.wait_ge(root_ready.sem, root_ready.of(L, r + 1))
                v.reciprocal(rstd_tok[:, 0:TB], sq_root[:, 0:TB]).then_inc(inverse_ready.sem, 1)
                v.wait_ge(rstd_ready.sem, rstd_ready.of(L, r + 1))

            def modulate(L, ui):
                a, b, c = (sq_buf[:, m % 3, :] for m in range(H_SUMMED, KT))
                v.wait_ge(sq_ready.sem, sq_ready.of(L, KT * 2 * ui + KT - 1))
                st.did(v.tensor_tensor(a, a, b, ADD))
                v.wait_ge(sq_ready.sem, sq_ready.of(L, KT * 2 * ui + KT))
                st.wait()
                st.did(v.tensor_tensor(a, a, c, ADD))
                v.wait_ge(h_sq_summed.sem, h_sq_summed.of(L, H_SUMMED * (ui + 1)))
                st.wait()
                v.tensor_tensor(sq_sum[:, :], sq_sum[:, :], a, ADD).then_inc(h_sq_total.sem, 1)
                rstd(L, 2 * ui)
                for m in range(KT + 1):
                    if m < KT:
                        if m >= 2:
                            v.wait_ge(u_ready.sem, u_ready.of(L, ui * KT + m - 1))
                        stt(mod_buf[:, m % 2, :], h[:, m, :], pre_gain[:, KT * ui + m:KT * ui + m + 1], bank[MS_BANK[2 * ui] + 1][:, :],
                            MUL, MUL).then_inc(modulated.sem, 1)
                    if m:
                        i = m - 1
                        v.wait_ge(u_hi_ready.sem, u_hi_ready.of(L, ui * KT + i + 1))
                        stt(u_lo[:, i, :], mod_buf[:, i % 2, :], ada[:, 24 * ui + i:24 * ui + i + 1],
                            u_hi[:, i, :].bitcast(F32), ADD, SUB).then_inc(u_ready.sem, 1)

            def post(L, ui):
                rstd(L, 2 * ui + 1)
                for m in range(KT + 1):
                    if m < KT:
                        v.wait_ge(y_copied.sem, y_copied.of(L, ui * KT + m + 1))
                        scaled = stt(y_sub[:, m, :], y_sub[:, m, :], post_gain[:, KT * ui + m:KT * ui + m + 1],
                                     bank[MS_BANK[2 * ui + 1] + 1][:, :], MUL, MUL)
                        if m in ADDED_BY_POOL:
                            scaled.then_inc(y_scaled.sem, 1)
                        else:
                            st.did(scaled)
                    if m - 1 in ADDED_BY_VECTOR:
                        st.wait(back=1 if m in ADDED_BY_VECTOR else 0)
                        v.tensor_tensor(h[:, m - 1, :], h[:, m - 1, :], y_sub[:, m - 1, :], ADD).then_inc(h_by_vector.sem, 1)

            def ffn(L, f, c0):
                i0 = f * FT

                def up(j, with_ada):
                    if with_ada:
                        for s in range(3):
                            ada_chunk(L, f, j, s)
                    split(L, c0 % 2, (c0 + 2) // 2 + j + 1)
                    for mt in range(2):
                        i = i0 + 2 * j + mt
                        v.wait_ge(silu_done.sem, silu_done.of(L, i + 1))
                        if mt:
                            s = (c0 + 1) % 2
                            v.wait_ge(chunk_done[s].sem, chunk_done[s].of(L, (c0 + 1) // 2 + j + 1))
                        else:
                            v.wait_ge(tile_ready.sem, tile_ready.of(L, f * READY_BEFORE_FFN2 + 2 * j + 2))
                        v.tensor_tensor(silu_buf[:, mt, :], silu_buf[:, mt, :], bank[2 + mt][:, :], MUL).then_inc(prod_done.sem, 1)
                    for mt in range(2):
                        i = i0 + 2 * j + mt
                        v.wait_ge(g_hi_ready.sem, g_hi_ready.of(L, i + 1))
                        v.tensor_tensor(flat(g_lo[:, cols(j * 2 + mt), :]), silu_buf[:, mt, :],
                                        flat(g_hi[:, cols(j * 2 + mt), :]).bitcast(F32), SUB).then_inc(g_lo_ready.sem, 1)
                    split(L, (c0 + 1) % 2, (c0 + 3) // 2 + j + 1)

                with v.Fori(0, ADA_ROUNDS[f]) as j:
                    up(j, True)
                ada_keep(L, f)
                with v.Fori(ADA_ROUNDS[f], FT // 2) as j:
                    up(j, False)
                c1 = c0 + FT
                split(L, c1 % 2, (c1 + 2) // 2 + 1)
                with v.Fori(0, (FT // 2 - 3) // 2) as j:
                    for half in range(2):
                        cc = c1 + 3 + half
                        split(L, cc % 2, cc // 2 + j + 1)

            def tile_wait(L, name, k):
                t = TILES[name, k]
                if t.last:
                    s = t.chunk % 2
                    v.wait_ge(chunk_done[s].sem, slot_value(chunk_done[s], L, t.chunk))
                else:
                    v.wait_ge(tile_ready.sem, tile_ready.of(L, t.ready))
                return bank[t.bank]

            def all_vectors():
                v.wait_ge(rows_turned, 1)
                v.tensor_copy(vec_all[:, :, 0:V_LOADED], bank[6][:, 0:DEPTH * V_LOADED].rearrange("p (l n) -> p l n", l=DEPTH))\
                 .then_inc(vec_steps, 1)
                v.wait_ge(spread_loaded, 32)
                steps = [1]
                for g in range(2):
                    rows = slice(64 * g, 64 * g + 64)
                    v.tensor_copy(vec_all[rows, :, V_LSTEP:V_PHASE],
                                  log_steps[rows, :, :].rearrange("p l (j g) -> p l j g", g=2)[:, :, :, g]).then_inc(vec_steps, 1)
                    steps[0] += 1
                v.wait_ge(vec_steps, steps[0])

                def part(a):
                    return vec_all[:, :, a:a + S5_PAIRS]

                phase, mag, f_re, f_im = part(V_PHASE), part(V_MAG), part(V_FRE), part(V_FIM)
                lre, lim, lst = part(V_LRE), part(V_LIM), part(V_LSTEP)
                R = [pscr[:, i] for i in range(12)]

                def do(ins):
                    ins.then_inc(vec_steps, 1)
                    steps[0] += 1
                    v.wait_ge(vec_steps, steps[0])

                def ts(o, a, s1, s2, op0, op1):
                    do(v.tensor_scalar(o, a, s1, s2, op0, op1))

                def stv(o, a, s, b, op0, op1):
                    do(stt(o, a, s, b, op0, op1))

                def tt(o, a, b, op):
                    do(v.tensor_tensor(o, a, b, op))

                ts(R[0], lst, 1.0 / math.log(2.0), MAGIC, MUL, ADD)
                ts(R[0], R[0], -MAGIC, None, ADD, ALU.bypass)
                stv(R[1], R[0], -LN2_A, lst, MUL, ADD)
                stv(R[1], R[0], -LN2_B, R[1], MUL, ADD)
                ts(R[2], R[1], 1.0 / 5040, None, MUL, ALU.bypass)
                for d in (720, 120, 24, 6, 2, 1):
                    stv(R[2], R[2], 1.0 / d, R[1], ADD, MUL)
                ts(R[2], R[2], 1.0, None, ADD, ALU.bypass)
                ts(R[0], R[0], 127.0, 1.0, ADD, ALU.max)
                do(v.tensor_scalar(pint[:, :, :], R[0], 254.0, 8388608.0, ALU.min, MUL))
                tt(R[2], R[2], pint[:, :, :].bitcast(F32), MUL)
                tt(R[3], lim, R[2], MUL)
                ts(R[0], R[3], 1.0 / TWO_PI, MAGIC, MUL, ADD)
                ts(R[0], R[0], -MAGIC, None, ADD, ALU.bypass)
                for part in (TWO_PI_A, TWO_PI_B, TWO_PI_C):
                    stv(R[3], R[0], -part, R[3], MUL, ADD)
                v.tensor_scalar(R[3], R[3], 3.1415925, -3.1415925, ALU.min, ALU.max).then_inc(theta_ready, 1)
                v.wait_ge(theta_ready, 1)
                ts(phase, R[3], 1.0 / TWO_PI, None, MUL, ALU.bypass)
                tt(R[4], lre, R[2], MUL)
                ts(R[4], R[4], 1.0 / 1024, -1.0, MUL, ALU.max)
                ts(R[5], R[4], 1.0 / 24, None, MUL, ALU.bypass)
                for d in (6, 2, 1):
                    stv(R[5], R[5], 1.0 / d, R[4], ADD, MUL)
                for _ in range(10):
                    stv(R[5], R[5], 2.0, R[5], ADD, MUL)
                ts(mag, R[5], 1.0, None, ADD, ALU.bypass)
                v.wait_ge(sines_ready, 2)
                stv(R[6], R[9], -2.0, R[9], MUL, MUL)
                stv(R[7], R[6], 1.0, R[5], ADD, MUL)
                tt(R[7], R[7], R[6], ADD)
                tt(R[8], mag, R[8], MUL)
                tt(R[10], lre, lre, MUL)
                tt(R[11], lim, lim, MUL)
                tt(R[10], R[10], R[11], ADD)
                do(v.reciprocal(R[10], R[10]))
                tt(f_re, R[7], lre, MUL)
                tt(R[11], R[8], lim, MUL)
                tt(f_re, f_re, R[11], ADD)
                tt(f_re, f_re, R[10], MUL)
                tt(f_im, R[8], lre, MUL)
                tt(R[11], R[7], lim, MUL)
                tt(f_im, f_im, R[11], SUB)
                tt(f_im, f_im, R[10], MUL)
                for l in range(DEPTH):
                    for i in range(2):
                        n = 2 * l + i
                        if n:
                            v.wait_ge(lam_sums, n)
                        v.tensor_tensor_reduce(lam_prod[:, :], lam_rows[:, l, 2 * i, :], lam_rows[:, l, 2 * i + 1, :], 1.0, 0.0,
                                               MUL, ADD, small[:, n:n + 1]).then_inc(lam_sums, 1)
                v.wait_ge(lam_exps, 1)
                for l in range(DEPTH):
                    lam_init = 0.8 - 0.6 * math.exp(-0.3 * l)
                    stv(small[:, 16 + l:17 + l], small[:, 8 + 2 * l:9 + 2 * l], -1.0, small[:, 9 + 2 * l:10 + 2 * l], MUL, ADD)
                    ts(vec_all[:, l, V_NEGLAM:V_END], small[:, 16 + l:17 + l], -lam_init, None, ADD, ALU.bypass)
                    ts(vec_all[:, l, V_DNORM:V_SD], vec_all[:, l, V_DNORM:V_SD], 1.0 - lam_init, None, MUL, ALU.bypass)
                return steps[0]

            def weighted_sum(slot, acc, wait, step):
                for k in range(KT):
                    w = slot[:, k, :]
                    if k == 0:
                        ins = v.tensor_scalar(acc, w, cond[:, 0:1], None, MUL, ALU.bypass)
                    else:
                        wait(k)
                        ins = stt(acc, w, cond[:, k:k + 1], acc, MUL, ADD)
                    ins.then_inc(step, 1)

            def ada_chunk(L, f, j, s):
                n = f * 3 * ADA_ROUNDS[0] + j * 3 + s
                v.wait_ge(ada_loaded[s].sem, ada_loaded[s].of(L, f * 16 * ADA_ROUNDS[0] + j * 16 + 16))
                v.wait_ge(ada_column.sem, ada_column.of(L, n - 2))
                weighted_sum(ada_w[s], ada_acc[s][:, :], lambda k: v.wait_ge(ada_step.sem, ada_step.of(L, n * KT + k)), ada_step.sem)

            def pre(ui):
                k8 = slice(KT * ui, KT * ui + KT)
                st.did(stt(pre_gain[:, k8], ada[:, 24 * ui + 8:24 * ui + 16], 1.0, vec[:, V_PRE + KT * ui:V_PRE + KT * ui + KT], ADD, MUL))

            def gate(ui):
                k8 = slice(KT * ui, KT * ui + KT)
                st.did(stt(post_gain[:, k8], ada[:, 24 * ui + 16:24 * ui + 24], 1.0 if ui == 1 else 0.5,
                           vec[:, V_POST + KT * ui:V_POST + KT * ui + KT], MUL, MUL))

            def ada_keep(L, f):
                v.wait_ge(ada_column.sem, ada_column.of(L, 3 * (ADA_ROUNDS[0] + (ADA_ROUNDS[1] if f else 0))))
                if f == 0:
                    v.tensor_tensor(ada[:, 16:64], bank[7][:, 0:48], vec[:, 16:64], ADD).then_inc(ada_kept.sem, 1)
                    v.wait_ge(ada_kept.sem, ada_kept.of(L, 1))
                    gate(0)
                    pre(1)
                    gate(1)
                    pre(2)
                else:
                    st.did(v.tensor_copy(ada[:, 0:16], bank[7][:, 0:16]))
                    v.tensor_tensor(ada[:, 64:72], bank[7][:, 16:24], vec[:, 64:72], ADD).then_inc(ada_kept.sem, 1)
                    v.wait_ge(ada_kept.sem, ada_kept.of(L, 2))
                    gate(2)

            def split_chunk(L, name):
                ch = CHUNK_OF[name]
                split(L, ch % 2, ch // 2 + 1)

            def layer_start(L):
                st.did(v.tensor_copy(vec[:, :], flat(vec_all[:, cols(L), :])))
                st.wait()
                st.did(v.tensor_tensor(ada[:, 0:16], ada[:, 0:16], vec[:, 0:16], ADD))
                st.wait()
                pre(0)
                st.wait()

            def s5_matrices(L):
                b, t = s5_b, s5_t

                def bc(f):
                    return f.unsqueeze(2).to_broadcast([P, S5_PAIRS, S5_CH])

                v.wait_ge(s5w_loaded.sem, s5w_loaded.of(L, 16 * 6))
                st.did(v.tensor_tensor(t[:, 0], b[:, 1], bc(f_im), MUL))
                st.did(v.tensor_tensor(t[:, 1], b[:, 0], bc(f_im), MUL))
                st.wait()
                st.did(v.tensor_tensor(b[:, 0], b[:, 0], bc(f_re), MUL))
                st.did(v.tensor_tensor(b[:, 1], b[:, 1], bc(f_re), MUL))
                st.wait()
                v.wait_ge(s5_bx_zero.sem, s5_bx_zero.of(L, 1))
                for g in range(2):
                    rows = slice(64 * g, 64 * g + 64)
                    for part in range(2):
                        dst = s5_bx[rows, part, :, :, g, :].rearrange("p q i h -> p (q i) h")
                        ins = v.tensor_tensor(dst, b[rows, part], t[rows, part], ADD if part else SUB)
                        if g == 0 or part == 0:
                            st.did(ins)
                st.wait()
                ins.then_inc(s5_bx_ready.sem, 1)
                v.wait_ge(s5_turned.sem, s5_turned.of(L, 1))
                for part in range(2):
                    st.did(v.tensor_copy(flat(s5_bt[:, part]), bank[4 + part][:, :]))
                v.wait_ge(s5_turned.sem, s5_turned.of(L, 2))
                v.wait_ge(s5_mask_ready.sem, s5_mask_ready.of(L, 3))
                mask = s5_mask[:, :, :, :].rearrange("p a g n -> p (a g n)").unsqueeze(1).to_broadcast([P, 4, P])
                for part in range(2):
                    ins = stt(s5_ct[:, part], bank[6 + part][:, :].rearrange("p (q n) -> p q n", q=4), -1.0 if part else 1.0,
                              mask, MUL, MUL)
                    if part == 0:
                        st.did(ins)
                st.wait()
                ins.then_inc(s5_mats_ready.sem, 1)

            def s5_turns_and_front(L, jt, jf):
                if jt is not None:
                    ph = phase[:, jt:jt + 1]
                    if jt >= 1:
                        v.wait_ge(turns_ready.sem, turns_ready.of(L, jt))
                    st.did(v.tensor_scalar(rounded[:, :], time_row[:, :], ph, MAGIC, MUL, ADD))
                if jf is not None:
                    r = [rot[jf % 3][:, i, :] for i in range(4)]
                    cs, sn = tab_c[:, jf % 3, :], tab_s[:, jf % 3, :]
                    v.wait_ge(bu_ready.sem, bu_ready.of(L, jf + 1))
                    v.wait_ge(tables_ready.sem, tables_ready.of(L, jf + 1))
                    if jf >= 3:
                        v.wait_ge(s5_y_ready.sem, s5_y_ready.of(L, jf - 2))
                    st.did(v.tensor_tensor(r[0], bank[4][:, :], cs, MUL))
                if jt is not None:
                    st.wait(back=1 if jf is not None else 0)
                    st.did(v.tensor_scalar(rounded[:, :], rounded[:, :], -MAGIC, None, ADD, ALU.bypass))
                if jf is not None:
                    st.did(v.tensor_tensor(r[1], bank[5][:, :], sn, MUL))
                if jt is not None:
                    st.wait(back=1 if jf is not None else 0)
                    if jt >= 2:
                        v.wait_ge(tables_ready.sem, tables_ready.of(L, jt - 1))
                    stt(turns[:, jt % 2, :], time_row[:, :], ph, rounded[:, :], MUL, SUB).then_inc(turns_ready.sem, 1)
                if jf is not None:
                    v.tensor_tensor(r[2], bank[5][:, :], cs, MUL)
                    v.tensor_tensor(r[3], bank[4][:, :], sn, MUL).then_inc(front_done.sem, 1)

            def s5_back(L, j):
                r = [rot[j % 3][:, i, :] for i in range(4)]
                cs, sn = tab_c[:, j % 3, :], tab_s[:, j % 3, :]
                m = mag[:, j:j + 1].to_broadcast([P, SEQ])
                v.wait_ge(z_in_ready.sem, z_in_ready.of(L, 2 * j + 2))
                st.did(v.tensor_tensor_scan(r[1], m, r[0], 0.0, MUL, ADD))
                st.did(v.tensor_tensor_scan(r[3], m, r[2], 0.0, MUL, ADD))
                st.wait()
                v.tensor_tensor(r[0], r[1], cs, MUL)
                v.tensor_tensor(r[2], r[3], sn, MUL)
                v.tensor_tensor(r[1], r[1], sn, MUL)
                v.tensor_tensor(r[3], r[3], cs, MUL).then_inc(back_done.sem, 1)

            def s5_y(L, q):
                v.wait_ge(s5_y_ready.sem, s5_y_ready.of(L, 4 * q + 4))
                stt(su[:, q, :], su[:, q, :], vec[:, V_SD + q:V_SD + q + 1], bank[6 + q % 2][:, :], MUL, ADD)\
                    .then_inc(s5_y_summed.sem, 1)

            def split_tile(L, base, k, lo, hi, src):
                v.wait_ge(split_hi.sem, split_hi.of(L, base + k + 1))
                v.tensor_tensor(lo[:, k, :], src, hi[:, k, :].bitcast(F32), SUB).then_inc(split_lo.sem, 1)

            def head_keep(L, hh, bk):
                v.wait_ge(o_ms.sem, o_ms.of(L, hh + 1))
                v.tensor_copy(ms_heads[:, (hh % 4) * 4:(hh % 4) * 4 + 4], bank[bk][:, 0:TB]).then_inc(o_ms_kept.sem, 1)

            def heads_norm(L, g):
                v.wait_ge(o_roots.sem, o_roots.of(L, g + 1))
                v.reciprocal(rstd_tok[:, :], sq_root[:, :]).then_inc(o_inverse.sem, 1)
                for hd in range(4):
                    hh = 4 * g + hd
                    v.wait_ge(o_rstd.sem, o_rstd.of(L, hh + 1))
                    bk = bank[4 + hd % 2]
                    if g == 0:
                        stt(o_head[hd][:, :], o_head[hd][:, :], vec[:, V_GNORM + hd:V_GNORM + hd + 1], bk[:, :], MUL, MUL)\
                            .then_inc(o_normed.sem, 1)
                        v.wait_ge(o_normed.sem, o_normed.of(L, hh + 1))
                        v.tensor_tensor(gr[:, hd, :], gr[:, hd, :], o_head[hd][:, :], MUL).then_inc(yga_done.sem, 1)
                    else:
                        stt(dq[:, hd, :], dq[:, hd, :], vec[:, V_DNORM + hd:V_DNORM + hd + 1], bk[:, :], MUL, MUL).then_inc(o_normed.sem, 1)

            def branch_tile(L, name, k, n):
                b = tile_wait(L, name, k)
                m = n % 8
                gate = TILES[f"g{name[1]}{m // 2}", m % 2]
                v.wait_ge(emptied["act"].sem, emptied["act"].of(L, gate.emptied))
                g = (sig if n < 12 else sig_late)[:, n % 4, :]
                v.tensor_tensor(g, g, b[:, :], MUL).then_inc(emptied["vec"].sem, 1)
                v.wait_ge(emptied["vec"].sem, emptied["vec"].of(L, TILES[name, k].emptied))
                if n >= 8:
                    v.wait_ge(merged_ready.sem, merged_ready.of(L, n - 7))
                v.tensor_tensor(merged[:, m, :], merged[:, m, :], g, ADD).then_inc(merged_ready.sem, 1)

            def diff_max(L, i):
                hd, qb = divmod(i, TB)
                n = (qb + 1) * P
                sm = smax[:, i % 2, :]
                if i >= 2:
                    v.wait_ge(at_ready.sem, at_ready.of(L, i - 1))
                v.wait_ge(scores_ready.sem, scores_ready.of(L, 2 * i + 2))
                v.sem_inc(scores_seen.sem, 1)
                for par in range(2):
                    st.did(v.tensor_tensor_reduce(prob[i % 2][:, par, 0:n], bank[4 + par][:, 0:n],
                                                  bias_tab[:, 2 * hd + par, SEQ - n:SEQ], 1.0, -3.4e38, ADD, ALU.max,
                                                  sm[:, par:par + 1]))
                st.wait()
                v.tensor_scalar(sm[:, 2:4], sm[:, 0:2], -1.0, None, MUL, ALU.bypass).then_inc(max_ready.sem, 1)

            def diff_mix(L, i):
                hd, qb = divmod(i, TB)
                n = (qb + 1) * P
                sm = smax[:, i % 2, :]
                pr = prob[i % 2]
                v.wait_ge(prob_ready.sem, prob_ready.of(L, i + 1))
                st.did(v.reciprocal(sm[:, 6:8], sm[:, 4:6]))
                st.wait()
                st.did(v.tensor_tensor(sm[:, 7:8], sm[:, 7:8], neg_lam, MUL))
                st.did(v.tensor_scalar(pr[:, 0, 0:n], pr[:, 0, 0:n], sm[:, 6:7], None, MUL, ALU.bypass))
                st.wait()
                stt(pr[:, 0, 0:n], pr[:, 1, 0:n], sm[:, 7:8], pr[:, 0, 0:n], MUL, ADD).then_inc(mix_ready.sem, 1)

            v.memset(rel33[NUM_BUCKETS:NUM_BUCKETS + 1, :], MASKED).then_inc(const_ready, 1)
            for m in range(KT):
                v.wait_ge(x_turned, m + 1)
                v.tensor_copy(h[:, m, :], bank[m if m < 6 else m - 6][:, :]).then_inc((h_by_pool if m in ADDED_BY_POOL else h_by_vector).sem, 1)

            steps = all_vectors()
            v.wait_ge(cond_ready, 1)
            for n in range(3):
                v.wait_ge(first_ada_loaded[3 + n], 16)
                weighted_sum(first_ada_w[3 + n], first_ada_acc[n][:, :], lambda k: v.wait_ge(first_ada_step, n * KT + k), first_ada_step)
            v.wait_ge(first_column, ADA_AHEAD)
            v.tensor_copy(ada[:, 0:16], bank[7][:, 0:16]).then_inc(vec_steps, 1)
            v.wait_ge(vec_steps, steps + 1)
            v.wait_ge(line_copied, 2)
            v.wait_ge(const_ready, 4)
            with v.Fori(0, DEPTH) as L:
                st = Steps(v, vector_steps, L)
                layer_start(L)
                modulate(L, 0)
                ffn(L, 0, 0)
                post(L, 0)
                modulate(L, 1)
                s5_matrices(L)
                s5_turns_and_front(L, 0, None)
                s5_turns_and_front(L, 1, 0)
                for j in range(S5_PAIRS):
                    s5_turns_and_front(L, j + 2 if j + 2 < S5_PAIRS else None, j + 1 if j + 1 < S5_PAIRS else None)
                    for n, name in enumerate(S5_SIDE):
                        if n and n not in S5_BY_POOL and S5_SPLIT_AT[n] == j:
                            split_chunk(L, name)
                    s5_back(L, j)
                    if j >= 4 and j % 4 == 2:
                        s5_y(L, j // 4 - 1)
                s5_y(L, 3)
                for q in range(4):
                    v.wait_ge(gelu_done.sem, gelu_done.of(L, q + 1))
                    split_tile(L, YG, q, yg_lo, yg_hi, su[:, q, :])
                for k in range(4):
                    b = tile_wait(L, "glu0", k)
                    v.wait_ge(emptied["act"].sem, emptied["act"].of(L, TILES["glu1", k].emptied))
                    stt(z_gate[:, k, :], b[:, :], vec[:, V_BGLU + k:V_BGLU + k + 1], z_gate[:, k, :], ADD, MUL)\
                        .then_inc(emptied["vec"].sem, 1)
                v.wait_ge(emptied["vec"].sem, emptied["vec"].of(L, 4))
                for k in range(4):
                    split_tile(L, YS, k, ys_lo, ys_hi, z_gate[:, k, :])
                for k in range(8):
                    b = tile_wait(L, f"bs{k // 4}", k % 4)
                    v.wait_ge(emptied["act"].sem, emptied["act"].of(L, TILES[f"gs{k // 2}", k % 2].emptied))
                    v.tensor_tensor(merged[:, k, :], merged[:, k, :], b[:, :], MUL).then_inc(emptied["vec"].sem, 1)
                for t in range(2):
                    v.wait_ge(alpha_ready.sem, alpha_ready.of(L, t + 1))
                    v.tensor_scalar(lb[:, t, :], bank[4 + t][:, :], vec[:, V_BALPHA + t:V_BALPHA + t + 1], 0.0, ADD, ALU.min)\
                     .then_inc(alpha_read.sem, 1)
                for t in range(2):
                    v.wait_ge(alpha_exps.sem, alpha_exps.of(L, 1))
                    v.wait_ge(alpha_read.sem, alpha_read.of(L, t + 1))
                    st.did(v.tensor_tensor(la[:, t, :], lb[:, t, :], la[:, t, :], SUB))
                    st.wait()
                    v.tensor_tensor_scan(lb[:, t, :], chunk_mask[:, :], la[:, t, :], 0.0, MUL, ADD).then_inc(decay_sum.sem, 1)
                for t in range(2):
                    b3 = lb[:, t, :].rearrange("p (n i) -> p n i", i=GLA_CHUNK)
                    v.wait_ge(gla_exps.sem, gla_exps.of(L, 2 * t + 2))
                    st.did(v.tensor_copy(small[:, 8 * t:8 * t + 8], b3[:, :, GLA_CHUNK - 1]))
                    st.wait()
                    v.tensor_tensor(b3, small[:, 8 * t:8 * t + 8].unsqueeze(2).to_broadcast([P, N_GCH, GLA_CHUNK]), b3, SUB)\
                     .then_inc(decay_last.sem, 1)
                for t in range(2):
                    v.wait_ge(gla_exps.sem, gla_exps.of(L, 2 * t + 2))
                    stt(gq[:, t, :], gq[:, t, :], GLA_DK ** -0.5, eb[:, t, :], MUL, MUL).then_inc(gla_keys.sem, 1)
                    v.tensor_tensor(la[:, t, :], la[:, t, :], gk[:, t, :], MUL).then_inc(gla_keys.sem, 1)
                for t in range(2):
                    v.wait_ge(gla_exps.sem, gla_exps.of(L, 4 + t + 1))
                    v.wait_ge(gla_keys.sem, gla_keys.of(L, 2 * t + 2))
                    v.tensor_tensor(gk[:, t, :], gk[:, t, :], lb[:, t, :], MUL).then_inc(gla_keys.sem, 1)

                def clamp(hd):
                    v.wait_ge(att_ready.sem, att_ready.of(L, hd + 1))
                    a = att[:, hd % 2, :, :]
                    if hd >= 2:
                        v.wait_ge(o_ready.sem, o_ready.of(L, hd - 1))
                    st.did(v.tensor_tensor(a, bank[4][:, :].rearrange("p (b n) -> p b n", b=TB),
                                           clamp_hi[:, :].unsqueeze(1).to_broadcast([P, TB, P]), ALU.min))
                    st.wait()
                    v.tensor_tensor(a, a, clamp_lo[:, :].unsqueeze(1).to_broadcast([P, TB, P]), ALU.max)\
                     .then_inc(att_clamped.sem, 1)

                for t in range(2):
                    v.wait_ge(ds_ready.sem, ds_ready.of(L, t + 1))
                    for n in range(N_GCH - 1):
                        d = bank[6 + n % 2][:, (n // 2) * P:(n // 2 + 1) * P]
                        if n == 0:
                            ins = v.tensor_copy(s_state[:, t, 1, :], d)
                        else:
                            e = n * GLA_CHUNK + GLA_CHUNK - 1
                            ins = stt(s_state[:, t, n + 1, :], s_state[:, t, n, :], eb[:, t, e:e + 1], d, MUL, ADD)
                        if n < N_GCH - 2:
                            st.did(ins)
                            st.wait()
                    ins.then_inc(s_ready.sem, 1)
                    clamp(t)
                for hd in range(GLA_HEADS):
                    if hd + 2 < GLA_HEADS:
                        clamp(hd + 2)
                    head_keep(L, hd, 6 + hd % 2)
                heads_norm(L, 0)
                for k in range(4):
                    split_tile(L, YGA, k, yga_lo, yga_hi, gr[:, k, :])
                v.wait_ge(bias_loaded.sem, bias_loaded.of(L, 16 * P // BIAS_COPIES))
                diff_max(L, 0)
                for i in range(DIFF_HEADS * TB):
                    hd, qb = divmod(i, TB)
                    for name, k in BESIDE_DIFF[i - 1] if i else ():
                        if name[0] == "b":
                            branch_tile(L, name, k, 4 * int(name[-1]) + k)
                    if i + 1 < DIFF_HEADS * TB:
                        diff_max(L, i + 1)
                    if hd and qb == 0:
                        head_keep(L, 4 + hd - 1, 7)
                    diff_mix(L, i)
                head_keep(L, 4 + DIFF_HEADS - 1, 7)
                heads_norm(L, 1)
                for k in range(4):
                    split_tile(L, YD, k, yd_lo, yd_hi, dq[:, k, :])
                for k in range(8):
                    branch_tile(L, f"bd{k // 4}", k % 4, 8 + k)
                for m in range(KT):
                    split_tile(L, MG, m, mg_lo, mg_hi, merged[:, m, :])
                post(L, 1)
                modulate(L, 2)
                ffn(L, 1, C_FFN2)
                post(L, 2)
                assert st.n == VECTOR_STEPS, st.n

            for b, n in ((1, 5), (3, 7)):
                v.wait_ge(out_turned, n)
                v.tensor_copy(x_tok[:, b, SEQ:D_MODEL], bank[2 * b + 1][:, :]).then_inc(out_by_vec, 1)

        @block.gpsimd
        def _(pool):
            pool.memset(ident[:, :], 0.0).then_inc(pool_start, 1)
            pool.memset(ones[:, :], 1.0).then_inc(pool_start, 1)
            pool.memset(chunk_mask[:, :], 1.0).then_inc(pool_start, 1)
            pool.memset(clamp_hi[:, :], BIG).then_inc(pool_start, 1)
            pool.memset(clamp_lo[:, :], -BIG).then_inc(pool_start, 1)
            pool.memset(inv_d[:, 0:1], 1.0 / D_MODEL).then_inc(pool_start, 1)
            pool.memset(inv_d[:, 1:2], 1.0 / P).then_inc(pool_start, 1)
            pool.memset(cst[:, 0:1], EPS).then_inc(pool_start, 1)
            pool.memset(cst[:, 1:2], math.pi / 2).then_inc(pool_start, 1)
            pool.iota(time_row[:, :], [[1, SEQ]], base=0, channel_multiplier=0, allow_small_or_imprecise_dtypes=True)\
                .then_inc(pool_start, 1)
            pool.wait_ge(pool_start, 10)
            pool.affine_select(out=ident[:, :], in_=ident[:, :], compare_op=ALU.not_equal, fill=1.0, base=0,
                               pattern=[[-1, P]], channel_multiplier=1).then_inc(const_ready, 1)
            pool.affine_select(out=chunk_mask[:, :], in_=chunk_mask[:, :], compare_op=ALU.not_equal, fill=0.0, base=0,
                               pattern=[[0, N_GCH], [1, GLA_CHUNK]], channel_multiplier=0).then_inc(const_ready, 1)
            for m in (clamp_hi, clamp_lo):
                pool.affine_select(out=m[:, :], in_=m[:, :], compare_op=ALU.is_ge, fill=0.0, base=0,
                                   pattern=[[1, P]], channel_multiplier=-1).then_inc(pool_start, 1)
            pool.wait_ge(pool_start, 12)
            for m in (clamp_hi, clamp_lo):
                pool.memset(m[0:64, 64:128], 0.0).then_inc(pool_start, 1)
            pool.wait_ge(pool_start, 14)
            pool.sem_inc(const_ready, 1)

            def squares(L, ui, tiles=range(1, KT - 1)):
                for m in tiles:
                    pool.wait_ge(sq_ready.sem, sq_ready.of(L, KT * (2 * ui + 1) + m + 1))
                    if m == 1:
                        pool.tensor_tensor(sq_sum[:, :], sq_buf[:, 0, :], sq_buf[:, 1, :], ALU.add).then_inc(sq_summed.sem, 2)
                    else:
                        pool.wait_ge(sq_summed.sem, sq_summed.of(L, (KT - 1) * ui + m))
                        pool.tensor_tensor(sq_sum[:, :], sq_sum[:, :], sq_buf[:, m % 3, :], ALU.add).then_inc(sq_summed.sem, 1)

            def add(L, ui, n):
                m = ADDED_BY_POOL[n]
                pool.wait_ge(y_scaled.sem, y_scaled.of(L, len(ADDED_BY_POOL) * ui + n + 1))
                pool.tensor_tensor(h[:, m, :], h[:, m, :], y_sub[:, m, :], ALU.add).then_inc(h_by_pool.sem, 1)

            def h_squares(L, ui, tiles=range(1, H_SUMMED)):
                for m in tiles:
                    pool.wait_ge(sq_ready.sem, sq_ready.of(L, KT * 2 * ui + m + 1))
                    if m == 1:
                        pool.tensor_tensor(sq_sum[:, :], sq_buf[:, 0, :], sq_buf[:, 1, :], ALU.add).then_inc(h_sq_summed.sem, 2)
                    else:
                        pool.wait_ge(h_sq_summed.sem, h_sq_summed.of(L, H_SUMMED * ui + m))
                        pool.tensor_tensor(sq_sum[:, :], sq_sum[:, :], sq_buf[:, m % 3, :], ALU.add).then_inc(h_sq_summed.sem, 1)

            def post_and_squares(L, ui):
                add(L, ui, 0)
                h_squares(L, ui + 1, (1, 2))
                add(L, ui, 1)
                h_squares(L, ui + 1, range(3, H_SUMMED))

            def split_low(L, ch, n=CHUNK_ELEMS):
                s = ch % 2
                pool.wait_ge(hi_split[s].sem, slot_value(hi_split[s], L, ch))
                pool.tensor_tensor(w_lo[s][:, 0:n], raw[s][:, 0:n], w_hi[s][:, 0:n].bitcast(F32), ALU.subtract)\
                    .then_inc(lo_split[s].sem, 1)

            def split(L, name):
                split_low(L, CHUNK_OF[name], KT * P if chunk_widths(name) == P else CHUNK_ELEMS)

            with pool.Fori(0, DEPTH) as L:
                h_squares(L, 0)
                split_low(L, 0)
                split_low(L, 1)
                split(L, "su0")
                squares(L, 0)
                post_and_squares(L, 0)
                split(L, "su1")
                s = (C_MIX - 1) % 2
                pool.wait_ge(chunk_done[s].sem, slot_value(chunk_done[s], L, C_MIX - 1))
                pool.sem_inc(room_seen.sem, 1)
                pool.memset(s5_bx[:, :, :, :, :, :].rearrange("p a q i g h -> p (a q i g h)"), 0.0).then_inc(s5_bx_zero.sem, 1)
                pool.memset(s5_mask[:, :, :, :], 0.0).then_inc(s5_mask_ready.sem, 1)
                pool.wait_ge(s5_mask_ready.sem, s5_mask_ready.of(L, 1))
                pool.sem_inc(room_seen.sem, 1)
                for g in range(2):
                    pool.memset(s5_mask[64 * g:64 * g + 64, :, g, :], 1.0).then_inc(s5_mask_ready.sem, 1)
                pool.wait_ge(s5_mask_ready.sem, s5_mask_ready.of(L, 3))
                split(L, "su2")
                split(L, "gq")
                for j in range(S5_PAIRS):
                    r = [rot[j % 3][:, i, :] for i in range(4)]
                    pool.wait_ge(front_done.sem, front_done.of(L, j + 1))
                    pool.tensor_tensor(r[0], r[0], r[1], ALU.add).then_inc(z_in_ready.sem, 1)
                    pool.tensor_tensor(r[2], r[2], r[3], ALU.subtract).then_inc(z_in_ready.sem, 1)
                    for n, name in enumerate(S5_SIDE):
                        if n in S5_BY_POOL and S5_SPLIT_AT[n] == j:
                            split(L, name)
                    if j == S5_PAIRS - 1:
                        split(L, "glu1")
                    pool.wait_ge(back_done.sem, back_done.of(L, j + 1))
                    pool.tensor_tensor(r[0], r[0], r[2], ALU.subtract).then_inc(state_ready.sem, 1)
                    pool.tensor_tensor(r[1], r[1], r[3], ALU.add).then_inc(state_ready.sem, 1)
                for name, _, _ in MIXER[15:-1]:
                    split(L, name)
                squares(L, 1, (1, 2))
                split(L, "wo3")
                squares(L, 1, (3, 4))
                split_low(L, C_FFN2)
                squares(L, 1, (5, 6))
                post_and_squares(L, 1)
                split_low(L, C_FFN2 + 1)
                squares(L, 2)
                add(L, 2, 0)
                add(L, 2, 1)


_NAMES = ["x", "c", "rel_bias", "w_ada", "b_ada", "norm_pre", "norm_post", "ffn1_w_up", "ffn1_w_down", "ffn2_w_up",
          "ffn2_w_down", "w_in", "gla_w_alpha", "gla_b_alpha", "gla_norm", "diff_lambda", "diff_norm", "s5_lam_re",
          "s5_lam_im", "s5_log_step", "s5_b_re", "s5_b_im", "s5_c_re", "s5_c_im", "s5_d", "s5_w_glu", "s5_b_glu",
          "w_branch", "w_out"]


def bucket_onehot():
    hot = np.zeros((NUM_BUCKETS + 1, LINE), np.float32)
    exact = NUM_BUCKETS // 2
    for y in range(LINE):
        d = SEQ - 1 - y
        if d < 0:
            hot[NUM_BUCKETS, y] = 1.0
        elif d < exact:
            hot[d, y] = 1.0
        else:
            scaled = np.log(np.float32(d) / np.float32(exact)) / np.float32(math.log(MAX_DISTANCE / exact))
            hot[min(exact + int(np.float32(scaled * np.float32(NUM_BUCKETS - exact))), NUM_BUCKETS - 1), y] = 1.0
    return hot


def kernel(**inputs):
    import concourse.bacc as bacc
    from concourse.bass_utils import run_bass_kernel_spmd

    nc = bacc.Bacc("TRN2", target_bir_lowering=False, num_devices=1)
    nc.disable_value_cache = True
    arrays = {"in_" + name: np.ascontiguousarray(inputs[name]) for name in _NAMES}
    arrays["in_bucket_onehot"] = bucket_onehot()
    args = [nc.dram_tensor(name, a.shape, mybir.dt.from_np(a.dtype), kind="ExternalInput").ap() for name, a in arrays.items()]
    args.append(nc.dram_tensor("out", (1, SEQ, D_MODEL), F32, kind="ExternalOutput").ap())
    build(nc, *args)
    return run_bass_kernel_spmd(nc, [arrays], core_ids=[0]).results[0]["out"]
```
